# Optimizing a Trainium2 kernel written in Bass

```python
import jax, jax.numpy as jnp
from jax import lax
import numpy as np

D_MODEL = 1024
BATCH = 1
SEQ = 2048
DEPTH = 1

N_META = 16
BLOCK = 128
PAD = BLOCK - N_META
EPS = 1e-6
R_HEADS = 8
R_DK = 128
R_DV = 128
R_QK = R_HEADS * R_DK
R_WIDTH = R_HEADS * R_DV
CHUNK = 64
A_HEADS = 8
A_KV_HEADS = 2
A_HEAD_DIM = 128
A_GROUP = A_HEADS // A_KV_HEADS
A_WIDTH = A_HEADS * A_HEAD_DIM
A_KV = A_KV_HEADS * A_HEAD_DIM
TOPK_MAX = 256
I_HEADS = 8
I_DIM = 64
SPLIT_SIZES = (R_QK, R_QK, R_WIDTH, R_WIDTH,
               A_WIDTH, A_KV, A_KV, A_WIDTH,
               I_HEADS * I_DIM, I_DIM, I_HEADS,
               D_MODEL, D_MODEL)
D_IN = sum(SPLIT_SIZES)

kernel_name = "hybrid_hgrn2_dsa_gated_merge"

def _split_points():
    pts, acc = [], 0
    for s in SPLIT_SIZES[:-1]:
        acc += s
        pts.append(acc)
    return pts

def rmsnorm(x, g):
    xf = x.astype(jnp.float32)
    y = xf * lax.rsqrt(jnp.mean(xf * xf, axis=-1, keepdims=True) + EPS)
    return (y * g.astype(jnp.float32)).astype(x.dtype)

def alibi_slopes(n):
    return 2.0 ** (-8.0 * jnp.arange(1, n + 1, dtype=jnp.float32) / n)

def hgrn2_branch(q, f_logit, inp, lb, valid):
    B, T, _ = q.shape
    lbf = lb.astype(jnp.float32)
    f = lbf + (1.0 - lbf) * jax.nn.sigmoid(f_logit.astype(jnp.float32))
    vm = valid[None, :, None]
    lf = jnp.where(vm, jnp.log(f), 0.0)
    k = jnp.where(vm, 1.0 - f, 0.0)
    qf = jax.nn.silu(q.astype(jnp.float32)) * (R_DK ** -0.5)
    v = inp.astype(jnp.float32)
    nc = T // CHUNK

    def chunks(a, d):
        return a.reshape(B, nc, CHUNK, R_HEADS, d).transpose(1, 0, 3, 2, 4)

    causal = jnp.tril(jnp.ones((CHUNK, CHUNK), bool))

    def step(S, xs):
        qc, kc, vc, lfc = xs
        b = jnp.cumsum(lfc, axis=2)
        o_inter = jnp.einsum('bhtk,bhkv->bhtv', qc * jnp.exp(b), S)
        diff = b[:, :, :, None, :] - b[:, :, None, :, :]
        dec = jnp.exp(jnp.where(causal[:, :, None], diff, -jnp.inf))
        att = jnp.einsum('bhtk,bhsk,bhtsk->bhts', qc, kc, dec)
        o = o_inter + jnp.einsum('bhts,bhsv->bhtv', att, vc)
        b_last = b[:, :, -1:, :]
        S = jnp.exp(b_last[:, :, 0, :])[..., None] * S + jnp.einsum(
            'bhsk,bhsv->bhkv', kc * jnp.exp(b_last - b), vc)
        return S, o

    S0 = jnp.zeros((B, R_HEADS, R_DK, R_DV), jnp.float32)
    _, o = lax.scan(step, S0, (chunks(qf, R_DK), chunks(k, R_DK), chunks(v, R_DV), chunks(lf, R_DK)))
    return o.transpose(1, 0, 3, 2, 4).reshape(B, T, R_HEADS, R_DV).astype(q.dtype)

def dsa_branch(q, k, v, iq, ik, iw, gq, gk, pos, valid, topk):
    B, T, _ = q.shape
    q = rmsnorm(q.reshape(B, T, A_HEADS, A_HEAD_DIM), gq)
    k = rmsnorm(k.reshape(B, T, A_KV_HEADS, A_HEAD_DIM), gk)
    v = v.reshape(B, T, A_KV_HEADS, A_HEAD_DIM)
    iq = iq.reshape(B, T, I_HEADS, I_DIM)
    iw = iw.astype(jnp.float32) * (I_HEADS ** -0.5) * (I_DIM ** -0.5)
    slopes = alibi_slopes(A_HEADS).reshape(A_KV_HEADS, A_GROUP)
    scale = A_HEAD_DIM ** -0.5
    bi = jnp.arange(B)[:, None, None]
    qi = jnp.arange(BLOCK)[None, :, None]

    def one_block(start):
        qb = lax.dynamic_slice_in_dim(q, start, BLOCK, axis=1)
        iqb = lax.dynamic_slice_in_dim(iq, start, BLOCK, axis=1)
        iwb = lax.dynamic_slice_in_dim(iw, start, BLOCK, axis=1)
        qpos = lax.dynamic_slice_in_dim(pos, start, BLOCK)
        admiss = (pos[None, :] <= qpos[:, None]) & valid[None, :]
        logits = jnp.einsum('bqhd,bsd->bqhs', iqb, ik).astype(jnp.float32)
        score = jnp.einsum('bqhs,bqh->bqs', jax.nn.relu(logits), iwb)
        score = jnp.where(admiss[None], score, -jnp.inf)
        _, idx = lax.top_k(score, topk)
        sel_ok = admiss[qi, idx]
        kg = k[bi, idx]
        vg = v[bi, idx]
        qg = qb.reshape(B, BLOCK, A_KV_HEADS, A_GROUP, A_HEAD_DIM)
        s = jnp.einsum('bqhgd,bqkhd->bqhgk', qg, kg).astype(jnp.float32) * scale
        dist = (qpos[None, :, None] - pos[idx]).astype(jnp.float32)
        s = s - slopes[None, None, :, :, None] * dist[:, :, None, None, :]
        s = jnp.where(sel_ok[:, :, None, None, :], s, -1e30)
        p = jax.nn.softmax(s, axis=-1).astype(vg.dtype)
        o = jnp.einsum('bqhgk,bqkhd->bqhgd', p, vg)
        return o.reshape(B, BLOCK, A_WIDTH)

    starts = jnp.arange(T // BLOCK, dtype=jnp.int32) * BLOCK
    out = lax.map(one_block, starts)
    return out.transpose(1, 0, 2, 3).reshape(B, T, A_WIDTH)

def setup_inputs(seed: int = 0) -> dict:
    key = jax.random.key(seed)
    ks = jax.random.split(key, 12)
    f32 = jnp.float32
    return {
        "x": jax.random.normal(ks[0], (BATCH, SEQ, D_MODEL), f32),
        "meta": jax.random.normal(ks[1], (N_META, D_MODEL), f32),
        "norm_g": 1.0 + 0.01 * jax.random.normal(ks[2], (DEPTH, D_MODEL), f32),
        "w_in": jax.random.normal(ks[3], (DEPTH, D_MODEL, D_IN), f32) * D_MODEL ** -0.5,
        "lb_logits": 0.1 * jax.random.normal(ks[4], (DEPTH + 1, R_QK), f32),
        "r_norm_g": 1.0 + 0.01 * jax.random.normal(ks[5], (DEPTH, R_DV), f32),
        "q_norm_g": 1.0 + 0.01 * jax.random.normal(ks[6], (DEPTH, A_HEAD_DIM), f32),
        "k_norm_g": 1.0 + 0.01 * jax.random.normal(ks[7], (DEPTH, A_HEAD_DIM), f32),
        "w_r": jax.random.normal(ks[8], (DEPTH, R_WIDTH, D_MODEL), f32) * R_WIDTH ** -0.5,
        "w_a": jax.random.normal(ks[9], (DEPTH, A_WIDTH, D_MODEL), f32) * A_WIDTH ** -0.5,
        "w_out": jax.random.normal(ks[10], (DEPTH, D_MODEL, D_MODEL), f32) * D_MODEL ** -0.5,
    }

def reference(x, meta, norm_g, w_in, lb_logits, r_norm_g, q_norm_g, k_norm_g, w_r, w_a, w_out):
    B, S, D = x.shape
    topk = min(TOPK_MAX, S // 4)
    T = S + BLOCK
    h = jnp.concatenate([
        jnp.zeros((B, PAD, D), x.dtype),
        jnp.broadcast_to(meta[None].astype(x.dtype), (B, N_META, D)),
        x], axis=1)
    pos = jnp.arange(T, dtype=jnp.int32) - PAD
    valid = pos >= 0
    lb_all = jnp.cumsum(jax.nn.softmax(lb_logits.astype(jnp.float32), axis=0), axis=0)
    pts = _split_points()
    for l in range(DEPTH):
        u = rmsnorm(h, norm_g[l])
        z = u @ w_in[l]
        (r_q, r_f, r_i, r_gate, a_q, a_k, a_v, a_gate,
         i_q, i_k, i_w, m_r, m_a) = jnp.split(z, pts, axis=-1)
        o_r = hgrn2_branch(r_q, r_f, r_i, lb_all[l], valid)
        o_r = rmsnorm(o_r, r_norm_g[l]).reshape(B, T, R_WIDTH)
        y_r = (o_r * jax.nn.silu(r_gate)) @ w_r[l]
        o_a = dsa_branch(a_q, a_k, a_v, i_q, i_k, i_w, q_norm_g[l], k_norm_g[l], pos, valid, topk)
        y_a = (o_a * jax.nn.silu(a_gate)) @ w_a[l]
        merged = jax.nn.sigmoid(m_r) * y_r + jax.nn.sigmoid(m_a) * y_a
        h = h + merged @ w_out[l]
    return h[:, BLOCK:, :]


_drawn_inputs = setup_inputs


def setup_inputs(seed=0):
    import zlib

    import numpy as np

    out = dict(_drawn_inputs(seed))
    spreads = {}
    factors = {'meta': 4.27, 'lb_logits': 8.0, 'r_norm_g': 8.0, 'q_norm_g': 8.0, 'k_norm_g': 8.0}
    for name, (base, spread) in spreads.items():
        noise = np.random.default_rng([zlib.crc32(name.encode()), seed]).standard_normal(out[name].shape)
        drawn = base * np.exp(spread * noise) if base else spread * noise
        out[name] = __import__('jax').numpy.asarray(drawn.astype(out[name].dtype))
    for name, factor in factors.items():
        out[name] = (out[name] * factor).astype(out[name].dtype)
    return out
```

```python
import concourse.bass as bass
from concourse import mybir
from contextlib import ExitStack

F32 = mybir.dt.float32
F16 = mybir.dt.float16
I16 = mybir.dt.int16
U16 = mybir.dt.uint16
I8 = mybir.dt.int8
ALU = mybir.AluOpType
ACT = mybir.ActivationFunctionType
AX = mybir.AxisListType

P = 128
D = 1024
KD = D // P
SEQ = 2048
META = 16
PAD = P - META
T = SEQ + P
NW = T // P
TILE = 512
WPT = TILE // P
NTILE = SEQ // TILE
RH = 8
AH, KVH, AG = 8, 2, 4
IH, ID = 8, 64
TOPK = 256
EPS = 1e-6
WSCALE = 64.0
C_RQ, C_RF, C_RI, C_RG = 0, 1024, 2048, 3072
C_AQ, C_AK, C_AV, C_AG = 4096, 5120, 5376, 5632
C_IQ, C_IK, C_IW = 6656, 7168, 7232
C_MR, C_MA = 7240, 8264


class Semaphores:

    def __init__(self, nc, ctx, prefix):
        self.nc, self.prefix, self.taken = nc, prefix, []
        ctx.callback(self.clear)

    def __call__(self, name):
        self.taken.append(self.nc.alloc_semaphore(self.prefix + name))
        return self.taken[-1]

    def two(self, name):
        return [self(f"{name}{b}") for b in range(2)]

    def clear(self):
        self.nc.clear_and_free_semaphores(self.taken)
        self.nc.all_engine_barrier()


def normed_input(nc, x, meta, norm_g, ut_hi, ut_lo, ident):
    with ExitStack() as ctx:
        def sb(name, shape, dt=F32):
            return ctx.enter_context(nc.sbuf_tensor(name, shape, dt))

        sem = Semaphores(nc, ctx, "n_")

        xw = [sb(f"xw{b}", [P, D]) for b in range(2)]
        xsq = sb("xsq", [P, D])
        xn = [sb(f"xn{b}", [P, D]) for b in range(2)]
        u32 = [sb(f"u32_{b}", [P, KD, P]) for b in range(2)]
        stat = sb("stat", [P, 2, 4])
        eps = sb("eps0", [P, 1])
        g = sb("g0", [P, KD])
        pt = [ctx.enter_context(nc.psum_tensor(f"pt{b}", [P, KD, P], F32)) for b in range(2)]
        meta_ready = sem("meta_ready")
        const_ready = sem("const_ready")
        g_loaded = sem("g_loaded")
        x_loaded = [sem(f"x_loaded{b}") for b in range(2)]
        ssq_ready = sem("ssq_ready")
        sd_ready = sem("sd_ready")
        rstd_ready = sem("rstd_ready")
        xn_ready = sem("xn_ready")
        xt_ready = sem("xt_ready")
        u32_ready = sem("u32_ready")
        hi_ready = sem("hi_ready")
        lo_ready = sem("lo_ready")

        def windows(eng, body):
            body(0, 0, 1, True)
            with eng.Fori(0, (NW - 1) // 2) as i:
                body(i * 2 + 1, 1, i + 1, False)
                body(i * 2 + 2, 0, i + 2, False)

        with nc.Block() as block:
            @block.sync
            def _(sp):
                sp.dma_start(g[:], norm_g.rearrange("o (k p) -> p (o k)", p=P),
                             allow_slow_non_contiguous=True).then_inc(g_loaded, 16)

                def load(n, b, visit, first):
                    if first:
                        sp.wait_ge(meta_ready, 1)
                        sp.dma_start(xw[b][PAD:P, :], meta).then_inc(x_loaded[b], 16)
                        return
                    sp.wait_ge(xn_ready, n - 1)
                    sp.dma_start(xw[b][:], x[bass.ds((n - 1) * P, P), :]).then_inc(x_loaded[b], 16)
                windows(sp, load)

            @block.gpsimd
            def _(pool):
                nc.gpsimd.memset(xw[0][:], 0.0).then_inc(meta_ready, 1)
                nc.gpsimd.memset(eps[:], EPS).then_inc(const_ready, 1)
                nc.gpsimd.memset(ident[:], 0.0).then_inc(const_ready, 1)
                pool.wait_ge(const_ready, 2)
                nc.gpsimd.affine_select(out=ident[:], in_=ident[:], compare_op=ALU.not_equal, fill=1.0,
                                        base=0, pattern=[[-1, P]], channel_multiplier=1).then_inc(const_ready, 1)

                def low(n, b, visit, first):
                    pool.wait_ge(hi_ready, n + 1)
                    t0 = 0 if first else n * P
                    nc.gpsimd.tensor_tensor(out=ut_lo[:, :, bass.ds(t0, P)], in0=u32[b][:],
                                            in1=ut_hi[:, :, bass.ds(t0, P)], op=ALU.subtract).then_inc(lo_ready, 1)
                windows(pool, low)

            @block.scalar
            def _(act):
                act.wait_ge(const_ready, 1)

                def norm(n, b, visit, first):
                    act.wait_ge(x_loaded[b], visit * 16)
                    nc.scalar.activation(xsq[:], xw[b][:], ACT.Square,
                                         accum_out=stat[:, b, 0:1]).then_inc(ssq_ready, 1)
                    act.wait_ge(ssq_ready, n + 1)
                    nc.scalar.activation(stat[:, b, 1:2], stat[:, b, 0:1], ACT.Sqrt,
                                         bias=eps[:], scale=1.0 / D).then_inc(sd_ready, 1)
                    act.wait_ge(u32_ready, n + 1)
                    t0 = 0 if first else n * P
                    nc.scalar.activation(ut_hi[:, :, bass.ds(t0, P)], u32[b][:], ACT.Copy).then_inc(hi_ready, 1)
                windows(act, norm)

            @block.vector
            def _(dve):
                dve.wait_ge(g_loaded, 16)

                def scale(n, b, visit, first):
                    dve.wait_ge(sd_ready, n + 1)
                    nc.vector.reciprocal(stat[:, b, 2:3], stat[:, b, 1:2]).then_inc(rstd_ready, 1)
                    dve.wait_ge(rstd_ready, n + 1)
                    if not first:
                        dve.wait_ge(xt_ready, n - 1)
                    nc.vector.tensor_scalar(xn[b][:], xw[b][:], stat[:, b, 2:3], None,
                                            ALU.mult).then_inc(xn_ready, 1)
                    dve.wait_ge(xt_ready, n + 1)
                    if not first:
                        dve.wait_ge(lo_ready, n - 1)
                    nc.vector.tensor_tensor(out=u32[b][:], in0=pt[b][:],
                                            in1=g[:, :, None].broadcast_to([P, KD, P]),
                                            op=ALU.mult).then_inc(u32_ready, 1)
                windows(dve, scale)

            @block.tensor
            def _(pe):
                pe.wait_ge(const_ready, 3)

                def turn(n, b, visit, first):
                    pe.wait_ge(xn_ready, n + 1)
                    if not first:
                        pe.wait_ge(u32_ready, n - 1)
                    for k in range(KD):
                        mm = nc.tensor.transpose(pt[b][:, k, :], xn[b][:, k * P:(k + 1) * P], ident[:])
                    mm.then_inc(xt_ready, 1)
                windows(pe, turn)


def recurrence(nc, w_cols, lb_logits, r_norm_g, ut_hi, ut_lo, og_parts, ident):
    STEPS = 1 + NTILE
    HPI = 2
    SPI = STEPS * HPI
    TPI = NTILE * HPI
    LEVELS = (128, 64, 32)
    LEAF = 16
    CLAMP = 80.0
    QSCALE = P ** -0.5
    with ExitStack() as ctx:
        def sb(name, shape, dt=F32):
            return ctx.enter_context(nc.sbuf_tensor(name, shape, dt))

        def two(name, shape, dt=F32):
            return [sb(f"{name}{b}", shape, dt) for b in range(2)]

        sem = Semaphores(nc, ctx, "r_")

        w_raw = [sb(f"w_raw{b}", [P, KD, P]) for b in range(2)]
        w_hi = [two(f"w_hi{s}_", [P, KD, P], F16) for s in range(4)]
        w_lo = [two(f"w_lo{s}_", [P, KD, P], F16) for s in range(4)]
        sig = sb("sig", [P, TILE])
        f_ = sb("f_", [P, TILE])
        lf = sb("lf", [P, TILE])
        q_ = two("q_", [P, TILE])
        k_ = sb("k_", [P, TILE])
        b_ = sb("b_", [P, TILE])
        gate = two("gate", [P, TILE])
        v_ = two("v_", [P, WPT, P])
        df = [sb(f"df{i}", [P, TILE]) for i in range(5)]
        ex = [sb(f"ex{i}", [P, TILE]) for i in range(7)]
        lv = [two(f"lv{i}_", [P, TILE]) for i in range(3)]
        lq, lk = two("lq", [P, TILE]), two("lk", [P, TILE])
        qe, ke = two("qe", [P, TILE]), two("ke", [P, TILE])
        eend = two("eend", [P, WPT])
        kt = sb("kt", [P, WPT, P])
        att = sb("att", [P, WPT, P])
        st = [sb(f"st{b}", [P, WPT, P]) for b in range(2)]
        sq = sb("sq", [P, TILE])
        rin = sb("rin", [P, TILE])
        on = sb("on", [P, TILE])
        og = sb("og", [P, TILE])
        oh, ol = two("oh", [P, TILE], F16), two("ol", [P, TILE], F16)
        restart = sb("restart", [P, TILE])
        mask = sb("mask", [P, 4, P], I8)
        mone = sb("mone", [P, P], I8)
        ones = sb("ones", [P, P])
        eps = sb("eps1", [P, 1])
        gq = sb("gq", [P, 1])
        lbl = sb("lbl", [P, 2, RH])
        lbd = sb("lbd", [P, RH])
        lb = sb("lb", [P, RH])
        omlb = sb("omlb", [P, RH])

        def bank(name, dt=F32):
            return ctx.enter_context(nc.psum_tensor("r" + name, [P, TILE], dt))

        pf, pq, pg, pv = bank("pf"), bank("pq"), bank("pg"), bank("pv")
        pa = [bank("pa0"), bank("pa1")]
        pk, po = bank("pk"), bank("po")

        w_loaded = [sem(f"w_loaded{s}") for s in range(4)]
        load_turn = sem("load_turn")
        whi_ready, wlo_ready = sem("whi_ready"), sem("wlo_ready")
        small_loaded, const_ready = sem("small_loaded"), sem("const_ready")
        lb_step, lb_ready = sem("lb_step"), sem("lb_ready")
        pf_ready, pq_ready, pg_ready, pv_ready = (sem(n) for n in ("pf_ready", "pq_ready", "pg_ready", "pv_ready"))
        sig_ready, q_ready, gate_ready, v_ready = (sem(n) for n in ("sig_ready", "q_ready", "gate_ready", "v_ready"))
        f_ready, k_ready, lf_ready, b_ready = (sem(n) for n in ("f_ready", "k_ready", "lf_ready", "b_ready"))
        leaf_raw, df_ready, ex_ready, prod_ready = (sem(n) for n in ("leaf_raw", "df_ready", "ex_ready", "prod_ready"))
        pk_ready, kt_ready, u_ready, st_ready = (sem(n) for n in ("pk_ready", "kt_ready", "u_ready", "st_ready"))
        pa_ready, att_part, att_ready = sem("pa_ready"), sem("att_part"), sem("att_ready")
        o_ready, sq_ready, ms_ready, ln_ready, rin_ready = (sem(n) for n in ("o_ready", "sq_ready", "ms_ready", "ln_ready", "rin_ready"))
        o_stored = [sem(f"o_stored{b}") for b in range(2)]
        on_ready, og_ready, ohi_ready, olo_ready = (sem(n) for n in ("on_ready", "og_ready", "ohi_ready", "olo_ready"))

        class Step:

            def __init__(self, i, s):
                self.n = i * SPI + s
                self.head = i * HPI + s // STEPS
                self.full = s % STEPS > 0
                self.m = i * TPI + (s // STEPS * NTILE + max(0, s % STEPS - 1))
                self.hb = s // STEPS % 2
                self.b = s % 2
                self.tile = s % STEPS - 1
                self.t0 = P + TILE * self.tile if self.full else 0
                self.stores = self.head * NTILE + self.tile // 2 * 2
                self.wins = WPT if self.full else 1
                self.cols = self.wins * P

        def steps(eng, first, second):
            with eng.Fori(0, RH // HPI) as i:
                for s in range(SPI + 1):
                    if s < SPI:
                        first(Step(i, s))
                    if s:
                        second(Step(i, s - 1))

        def level(ap, L, cols):
            return ap[:, 0:cols].rearrange("p (n l) -> p n l", l=L)

        with nc.Block() as block:
            @block.sync
            def _(sp):
                sp.dma_start(lbl[:], lb_logits.rearrange("r (h p) -> p r h", p=P),
                             allow_slow_non_contiguous=True).then_inc(small_loaded, 16)
                sp.dma_start(gq[:], r_norm_g.rearrange("o p -> p o"),
                             allow_slow_non_contiguous=True).then_inc(small_loaded, 16)
                def load(h, half):
                    for s, c in list(enumerate((C_RF, C_RQ, C_RG, C_RI)))[half * 2:half * 2 + 2]:
                        sp.wait_ge(wlo_ready, h * 4 + max(s - 1, 0))
                        sp.sem_inc(load_turn, 1)
                        sp.dma_start(w_raw[s % 2][:], w_cols[:, :, bass.ds(h * P + c, P)]).then_inc(w_loaded[s], 16)

                load(0, 0)
                load(0, 1)

                def store(h, tiles):
                    for j in tiles:
                        sp.wait_ge(olo_ready, h * NTILE + j + 1)
                        for part, o in enumerate((oh, ol)):
                            sp.dma_start(og_parts[part, :, bass.ds(h * SEQ + j * TILE, TILE)],
                                         o[j % 2][:]).then_inc(o_stored[j % 2], 16)
                with sp.Fori(0, RH - 1) as h:
                    load(h + 1, 0)
                    store(h, range(NTILE - 1))
                    load(h + 1, 1)
                    store(h, [NTILE - 1])
                store(RH - 1, range(NTILE))
                for b in range(2):
                    sp.wait_ge(o_stored[b], RH * NTILE * 16)

            @block.gpsimd
            def _(pool):
                nc.gpsimd.memset(restart[:], 1.0).then_inc(const_ready, 1)
                nc.gpsimd.memset(ones[:], 1.0 / P).then_inc(const_ready, 1)
                nc.gpsimd.memset(eps[:], EPS).then_inc(const_ready, 1)
                nc.gpsimd.memset(att[:], 0.0).then_inc(const_ready, 1)
                nc.gpsimd.memset(mone[:], 1).then_inc(const_ready, 1)
                nc.gpsimd.memset(mask[:], 0).then_inc(const_ready, 1)
                pool.wait_ge(const_ready, 6)
                nc.gpsimd.memset(restart[:].rearrange("p (w t) -> p w t", t=P)[:, :, 0], 0.0).then_inc(const_ready, 1)
                count = 7
                for j, L in enumerate(LEVELS):
                    H = L // 2
                    for blk in range(P // L):
                        sub = mask[:, j, blk * L + H:(blk + 1) * L]
                        nc.gpsimd.affine_select(out=sub, in_=mone[:, 0:H], compare_op=ALU.is_ge, fill=0.0,
                                                base=-blk * L, pattern=[[0, H]], channel_multiplier=1
                                                ).then_inc(const_ready, 1)
                        count += 1
                        pool.wait_ge(const_ready, count)
                        nc.gpsimd.affine_select(out=sub, in_=sub, compare_op=ALU.is_gt, fill=0.0,
                                                base=blk * L + H, pattern=[[0, H]], channel_multiplier=-1
                                                ).then_inc(const_ready, 1)
                        count += 1
                for blk in range(P // LEAF):
                    sub = mask[:, 3, blk * LEAF:(blk + 1) * LEAF]
                    nc.gpsimd.affine_select(out=sub, in_=mone[:, 0:LEAF], compare_op=ALU.is_ge, fill=0.0,
                                            base=-blk * LEAF, pattern=[[0, LEAF]], channel_multiplier=1
                                            ).then_inc(const_ready, 1)
                    count += 1
                    pool.wait_ge(const_ready, count)
                    nc.gpsimd.affine_select(out=sub, in_=sub, compare_op=ALU.is_ge, fill=0.0,
                                            base=blk * LEAF, pattern=[[1, LEAF]], channel_multiplier=-1
                                            ).then_inc(const_ready, 1)
                    count += 1
                assert count == CONSTS
                pool.wait_ge(const_ready, CONSTS)
                pool.sem_inc(prod_ready, 2)

                def products(x):
                    b, c = x.b, x.cols
                    pool.wait_ge(k_ready, x.n + 1)
                    pool.wait_ge(ex_ready, x.n + 1)
                    if x.full:
                        pool.wait_ge(q_ready, x.m + 1)
                        pool.wait_ge(o_ready, x.m)
                        for j, L in enumerate(LEVELS):
                            H = L // 2
                            e, o = level(ex[j], L, c), level(lv[j][b], L, c)
                            nc.gpsimd.tensor_tensor(out=o[:, :, 0:H], in0=e[:, :, 0:H],
                                                    in1=level(k_, L, c)[:, :, 0:H], op=ALU.mult)
                            nc.gpsimd.tensor_tensor(out=o[:, :, H:L], in0=e[:, :, H:L],
                                                    in1=level(q_[b], L, c)[:, :, H:L], op=ALU.mult)
                        nc.gpsimd.tensor_tensor(out=lq[b][:], in0=ex[3][:], in1=q_[b][:], op=ALU.mult)
                        nc.gpsimd.tensor_tensor(out=lk[b][:], in0=ex[4][:], in1=k_[:], op=ALU.mult)
                        nc.gpsimd.tensor_tensor(out=qe[b][:], in0=ex[5][:], in1=q_[b][:], op=ALU.mult)
                    nc.gpsimd.tensor_tensor(out=ke[b][:, 0:c], in0=ex[6][:, 0:c], in1=k_[:, 0:c],
                                            op=ALU.mult).then_inc(prod_ready, 1)

                def out_low(x):
                    if x.full:
                        pool.wait_ge(ohi_ready, x.m + 1)
                        pool.wait_ge(o_stored[x.tile % 2], x.stores * 16)
                        nc.gpsimd.tensor_tensor(out=ol[x.tile % 2][:], in0=og[:], in1=oh[x.tile % 2][:],
                                                op=ALU.subtract).then_inc(olo_ready, 1)
                with pool.Fori(0, RH // HPI) as i:
                    for s in range(SPI + 1):
                        if s:
                            out_low(Step(i, s - 1))
                        if s < SPI:
                            products(Step(i, s))

            @block.scalar
            def _(act):
                act.wait_ge(const_ready, CONSTS)
                act.wait_ge(lb_step, 1)
                nc.scalar.activation(lb[:], lbd[:], ACT.Sigmoid).then_inc(lb_ready, 1)
                nc.scalar.activation(omlb[:], lbd[:], ACT.Sigmoid, scale=-1.0).then_inc(lb_ready, 1)
                act.wait_ge(small_loaded, 32)
                nc.scalar.activation(gq[:], gq[:], ACT.Copy, scale=QSCALE).then_inc(lb_ready, 1)

                def weights(x):
                    for s in range(4):
                        act.wait_ge(w_loaded[s], (x.head + 1) * 16)
                        nc.scalar.activation(w_hi[s][x.hb][:], w_raw[s % 2][:], ACT.Copy,
                                             scale=WSCALE).then_inc(whi_ready, 1)

                def turned(x):
                    if not x.full:
                        weights(x)
                    b, c = x.b, x.cols
                    act.wait_ge(pf_ready, x.n + 1)
                    act.wait_ge(f_ready, x.n)
                    nc.scalar.activation(sig[:, 0:c], pf[:, 0:c], ACT.Sigmoid,
                                         scale=1.0 / WSCALE).then_inc(sig_ready, 1)
                    if x.full:
                        act.wait_ge(pq_ready, x.m + 1)
                        nc.scalar.activation(q_[b][:], pq[:], ACT.Silu, scale=1.0 / WSCALE).then_inc(q_ready, 1)
                        act.wait_ge(pg_ready, x.m + 1)
                        nc.scalar.activation(gate[b][:], pg[:], ACT.Silu, scale=1.0 / WSCALE).then_inc(gate_ready, 1)

                def output(x):
                    if not x.full:
                        return
                    act.wait_ge(o_ready, x.m + 1)
                    nc.scalar.activation(sq[:], po[:], ACT.Square, scale=QSCALE).then_inc(sq_ready, 1)
                    act.wait_ge(ms_ready, x.m + 1)
                    nc.scalar.activation(sq[:], pk[:], ACT.Ln, bias=eps[:]).then_inc(ln_ready, 1)
                    act.wait_ge(ln_ready, x.m + 1)
                    nc.scalar.activation(rin[:], sq[:], ACT.Exp, scale=-0.5).then_inc(rin_ready, 1)
                    act.wait_ge(og_ready, x.m + 1)
                    act.wait_ge(o_stored[x.tile % 2], x.stores * 16)
                    nc.scalar.activation(oh[x.tile % 2][:], og[:], ACT.Copy).then_inc(ohi_ready, 1)

                def decays(x):
                    c = x.cols
                    act.wait_ge(f_ready, x.n + 1)
                    nc.scalar.activation(lf[:, 0:c], f_[:, 0:c], ACT.Ln).then_inc(lf_ready, 1)
                    act.wait_ge(df_ready, x.n + 1)
                    act.wait_ge(prod_ready, x.n + 2)
                    if x.full:
                        for j, L in enumerate(LEVELS):
                            H = L // 2
                            d, e = level(df[j], L, c), level(ex[j], L, c)
                            nc.scalar.activation(e[:, :, 0:H], d[:, :, 0:H], ACT.Exp, scale=-1.0)
                            nc.scalar.activation(e[:, :, H:L], d[:, :, H:L], ACT.Exp)
                        nc.scalar.activation(ex[3][:], df[3][:], ACT.Exp)
                        nc.scalar.activation(ex[4][:], df[3][:], ACT.Exp, scale=-1.0)
                        nc.scalar.activation(ex[5][:], b_[:], ACT.Exp)
                        nc.scalar.activation(eend[x.b][:], b_[:].rearrange("p (w t) -> p w t", t=P)[:, :, P - 1],
                                             ACT.Exp)
                    nc.scalar.activation(ex[6][:, 0:c], df[4][:, 0:c], ACT.Exp, scale=-1.0).then_inc(ex_ready, 1)

                with act.Fori(0, RH // HPI) as i:
                    for s in range(SPI + 1):
                        if s < SPI:
                            turned(Step(i, s))
                        if s:
                            output(Step(i, s - 1))
                        if s < SPI:
                            decays(Step(i, s))

            @block.vector
            def _(dve):
                dve.wait_ge(const_ready, CONSTS)
                dve.wait_ge(small_loaded, 32)
                nc.vector.tensor_tensor(out=lbd[:], in0=lbl[:, 0, :], in1=lbl[:, 1, :],
                                        op=ALU.subtract).then_inc(lb_step, 1)
                dve.wait_ge(lb_ready, 3)

                def weights(x):
                    for s in range(4):
                        dve.wait_ge(whi_ready, x.head * 4 + s + 1)
                        nc.vector.scalar_tensor_tensor(out=w_lo[s][x.hb][:], in0=w_raw[s % 2][:], scalar=WSCALE,
                                                       in1=w_hi[s][x.hb][:], op0=ALU.mult,
                                                       op1=ALU.subtract).then_inc(wlo_ready, 1)

                def forget(x):
                    c = x.cols
                    h = x.head
                    dve.wait_ge(sig_ready, x.n + 1)
                    dve.wait_ge(lf_ready, x.n)
                    nc.vector.tensor_scalar(f_[:, 0:c], sig[:, 0:c], omlb[:, bass.ds(h, 1)], lb[:, bass.ds(h, 1)],
                                            ALU.mult, ALU.add).then_inc(f_ready, 1)
                    dve.wait_ge(f_ready, x.n + 1)
                    dve.wait_ge(prod_ready, x.n + 2)
                    nc.vector.tensor_scalar(k_[:, 0:c], f_[:, 0:c], -1.0, 1.0, ALU.mult, ALU.add).then_inc(k_ready, 1)
                    dve.wait_ge(pv_ready, x.n + 1)
                    nc.vector.tensor_scalar(v_[x.b][:, 0:x.wins, :], pv[:, 0:c].rearrange("p (w t) -> p w t", t=P),
                                            1.0 / WSCALE, None, ALU.mult).then_inc(v_ready, 1)
                    dve.wait_ge(lf_ready, x.n + 1)
                    nc.vector.tensor_tensor_scan(out=b_[:, 0:c], data0=restart[:, 0:c], data1=lf[:, 0:c],
                                                 initial=0.0, op0=ALU.mult, op1=ALU.add).then_inc(b_ready, 1)
                    dve.wait_ge(b_ready, x.n + 1)
                    if x.full:
                        a = level(b_, LEAF, c)[:, :, LEAF // 2 - 1:LEAF // 2].broadcast_to([P, c // LEAF, LEAF])
                        nc.vector.tensor_tensor(out=level(df[3], LEAF, c), in0=level(b_, LEAF, c), in1=a,
                                                op=ALU.subtract).then_inc(leaf_raw, 1)
                        for j, L in enumerate(LEVELS):
                            a = level(b_, L, c)[:, :, L // 2 - 1:L // 2].broadcast_to([P, c // L, L])
                            nc.vector.tensor_tensor(out=level(df[j], L, c), in0=level(b_, L, c), in1=a,
                                                    op=ALU.subtract)
                        dve.wait_ge(leaf_raw, x.m + 1)
                        nc.vector.tensor_scalar(df[3][:], df[3][:], CLAMP, -CLAMP, ALU.min, ALU.max)
                    a = level(b_, P, c)[:, :, P - 1:P].broadcast_to([P, c // P, P])
                    nc.vector.tensor_tensor(out=level(df[4], P, c), in0=level(b_, P, c), in1=a,
                                            op=ALU.subtract).then_inc(df_ready, 1)

                def window(x):
                    b = x.b
                    dve.wait_ge(pk_ready, x.n + 1)
                    nc.vector.tensor_copy(kt[:, 0:x.wins, :], pk[:, 0:x.cols].rearrange("p (w t) -> p w t", t=P)
                                          ).then_inc(kt_ready, 1)
                    if not x.full:
                        dve.wait_ge(u_ready, x.n + 1)
                        nc.vector.tensor_copy(st[1 - b][:, 0, :], po[:, 0:P]).then_inc(st_ready, 1)
                        return
                    for j in range(4):
                        dve.wait_ge(pa_ready, x.m * 4 + j + 1)
                        dve.wait_ge(att_ready, x.m * 4 + j)
                        if j == 0:
                            dve.wait_ge(u_ready, x.n + 1)
                        w = j
                        dve.wait_ge(st_ready, x.m * WPT + w + x.head + 1)
                        nxt = st[1 - b][:, 0, :] if w == WPT - 1 else st[b][:, w + 1, :]
                        nc.vector.scalar_tensor_tensor(out=nxt, in0=st[b][:, w, :], scalar=eend[b][:, w:w + 1],
                                                       in1=po[:, w * P:(w + 1) * P], op0=ALU.mult,
                                                       op1=ALU.add).then_inc(st_ready, 1)
                        nc.vector.copy_predicated(att[:], mask[:, j:j + 1, :].broadcast_to([P, WPT, P]),
                                                  pa[j % 2][:].rearrange("p (w t) -> p w t", t=P)
                                                  ).then_inc(att_ready, 1)
                    dve.wait_ge(rin_ready, x.m + 1)
                    nc.vector.scalar_tensor_tensor(out=on[:], in0=po[:], scalar=gq[:], in1=rin[:],
                                                   op0=ALU.mult, op1=ALU.mult).then_inc(on_ready, 1)
                    dve.wait_ge(on_ready, x.m + 1)
                    dve.wait_ge(gate_ready, x.m + 1)
                    dve.wait_ge(olo_ready, x.m)
                    nc.vector.tensor_tensor(out=og[:], in0=on[:], in1=gate[b][:], op=ALU.mult).then_inc(og_ready, 1)

                with dve.Fori(0, RH // HPI) as i:
                    for s in range(SPI + 1):
                        if s < SPI and s % STEPS == 0:
                            weights(Step(i, s))
                        if s:
                            window(Step(i, s - 1))
                        if s < SPI:
                            forget(Step(i, s))

            @block.tensor
            def _(pe):
                pe.wait_ge(const_ready, CONSTS)

                def project(out, s, x):
                    n = 0
                    for k in range(KD):
                        u = slice(x.t0, x.t0 + x.cols)
                        for w, m in ((w_hi, ut_hi), (w_hi, ut_lo), (w_lo, ut_hi)):
                            mm = nc.tensor.matmul(out[:, 0:x.cols], w[s][x.hb][:, k, :], m[:, k, u],
                                                  start=n == 0, stop=n == 3 * KD - 1)
                            n += 1
                    return mm

                def first(x):
                    if not x.full:
                        pe.wait_ge(wlo_ready, (x.head + 1) * 4)
                    pe.wait_ge(sig_ready, x.n)
                    project(pf, 0, x).then_inc(pf_ready, 1)
                    if x.full:
                        pe.wait_ge(q_ready, x.m)
                        project(pq, 1, x).then_inc(pq_ready, 1)
                        pe.wait_ge(gate_ready, x.m)
                        project(pg, 2, x).then_inc(pg_ready, 1)
                    pe.wait_ge(v_ready, x.n)
                    for w in range(x.wins):
                        n = 0
                        for k in range(KD):
                            u = slice(x.t0 + w * P, x.t0 + (w + 1) * P)
                            for m, wt in ((ut_hi, w_hi), (ut_hi, w_lo), (ut_lo, w_hi)):
                                mm = nc.tensor.matmul(pv[:, w * P:(w + 1) * P], m[:, k, u], wt[3][x.hb][:, k, :],
                                                      start=n == 0, stop=n == 3 * KD - 1)
                                n += 1
                    mm.then_inc(pv_ready, 1)

                def second(x):
                    b = x.b
                    pe.wait_ge(prod_ready, x.n + 3)
                    pe.wait_ge(rin_ready, x.m)
                    for w in range(x.wins):
                        c = slice(w * P, (w + 1) * P)
                        mm = nc.tensor.transpose(pk[:, c], ke[b][:, c], ident[:])
                    mm.then_inc(pk_ready, 1)

                    def scores(j):
                        pe.wait_ge(att_ready, x.m * 4 + max(0, j - 1))
                        s_part, t_part = (lv[j][b], lv[j][b]) if j < 3 else (lk[b], lq[b])
                        for w in range(WPT):
                            c = slice(w * P, (w + 1) * P)
                            mm = nc.tensor.matmul(pa[j % 2][:, c], s_part[:, c], t_part[:, c],
                                                  start=True, stop=True)
                        mm.then_inc(pa_ready, 1)
                    if x.full:
                        scores(0)
                        scores(1)
                    pe.wait_ge(kt_ready, x.n + 1)
                    pe.wait_ge(v_ready, x.n + 1)
                    pe.wait_ge(on_ready, x.m)
                    for w in range(x.wins):
                        mm = nc.tensor.matmul(po[:, w * P:(w + 1) * P], kt[:, w, :], v_[b][:, w, :],
                                              start=True, stop=True)
                    mm.then_inc(u_ready, 1)
                    if not x.full:
                        return
                    scores(2)
                    scores(3)
                    pe.wait_ge(att_ready, (x.m + 1) * 4)
                    pe.wait_ge(st_ready, (x.m + 1) * WPT + x.head + 1)
                    for w in range(WPT):
                        c = slice(w * P, (w + 1) * P)
                        nc.tensor.matmul(po[:, c], st[b][:, w, :], qe[b][:, c], start=True, stop=False)
                        mm = nc.tensor.matmul(po[:, c], v_[b][:, w, :], att[:, w, :], start=False, stop=True)
                    mm.then_inc(o_ready, 1)
                    pe.wait_ge(sq_ready, x.m + 1)
                    nc.tensor.matmul(pk[:], ones[:], sq[:], start=True, stop=True).then_inc(ms_ready, 1)
                steps(pe, first, second)


CONSTS = 7 + 2 * sum(P // L for L in (128, 64, 32)) + 2 * (P // 16)


def keys_values(nc, w_cols, k_norm_g, ut_hi, ut_lo, kt_hi, kt_lo, v_all, ik_hi, ik_lo, iw_all):
    TILES = [(0, P)] + [(P + j * TILE, TILE) for j in range(NTILE)]
    IW_SCALE = IH ** -0.5 * ID ** -0.5
    with ExitStack() as ctx:
        def sb(name, shape, dt=F32):
            return ctx.enter_context(nc.sbuf_tensor("kv_" + name, shape, dt))

        sem = Semaphores(nc, ctx, "kv_")

        slices = 5
        w_raw = [sb(f"w_raw{b}", [P, KD, P]) for b in range(slices)]
        w_hi = [sb(f"w_hi{b}", [P, KD, P], F16) for b in range(3)]
        w_lo = [sb(f"w_lo{b}", [P, KD, P], F16) for b in range(3)]
        wv_hi, wv_lo = sb("wv_hi", [P, KD, KVH * P], F16), sb("wv_lo", [P, KD, KVH * P], F16)
        wi_raw = sb("wi_raw", [P, KD, IH])
        wi_hi, wi_lo = sb("wi_hi", [P, KD, IH], F16), sb("wi_lo", [P, KD, IH], F16)
        gk = sb("gk", [P, 1])
        gks = sb("gks", [P, 1])
        eps = sb("eps", [P, 1])
        ones = sb("ones", [P, P])
        sq = sb("sq", [P, TILE])
        lnm = sb("lnm", [P, TILE])
        rin = sb("rin", [P, TILE])
        kn = sb("kn", [P, TILE])
        pz = [ctx.enter_context(nc.psum_tensor(f"kv_pz{b}", [P, TILE], F32)) for b in range(2)]
        pm = ctx.enter_context(nc.psum_tensor("kv_pm", [P, TILE], F32))
        pv = [ctx.enter_context(nc.psum_tensor(f"kv_pv{b}", [P, TILE], F32)) for b in range(2)]

        w_loaded = sem("w_loaded")
        hi_ready, lo_ready = sem("hi_ready"), sem("lo_ready")
        const_ready, gks_ready = sem("const_ready"), sem("gks_ready")
        z_ready, sq_ready, ms_ready, ln_ready, rin_ready = (sem(n) for n in ("z_ready", "sq_ready", "ms_ready", "ln_ready", "rin_ready"))
        kn_ready, khi_ready, klo_ready = (sem(n) for n in ("kn_ready", "khi_ready", "klo_ready"))
        ihi_ready, ilo_ready = sem("ihi_ready"), sem("ilo_ready")
        v_ready, vcopy_ready = sem("v_ready"), sem("vcopy_ready")
        NK = KVH * len(TILES)
        LOADS = slices + 3

        with nc.Block() as block:
            @block.sync
            def _(sp):
                for s in range(KVH):
                    sp.dma_start(w_raw[s][:], w_cols[:, :, C_AK + s * P:C_AK + (s + 1) * P]).then_inc(w_loaded, 16)
                for half in range(2):
                    sp.dma_start(w_raw[2][:, :, half * ID:(half + 1) * ID],
                                 w_cols[:, :, C_IK:C_IK + ID]).then_inc(w_loaded, 16)
                for s in range(KVH):
                    sp.dma_start(w_raw[3 + s][:], w_cols[:, :, C_AV + s * P:C_AV + (s + 1) * P]).then_inc(w_loaded, 16)
                sp.dma_start(wi_raw[:], w_cols[:, :, C_IW:C_IW + IH]).then_inc(w_loaded, 16)
                sp.dma_start(gk[:], k_norm_g.rearrange("o p -> p o"),
                             allow_slow_non_contiguous=True).then_inc(w_loaded, 16)

            def parts():
                for s in range(3):
                    yield w_raw[s][:], w_hi[s][:], w_lo[s][:]
                for s in range(KVH):
                    c = slice(s * P, (s + 1) * P)
                    yield w_raw[3 + s][:], wv_hi[:, :, c], wv_lo[:, :, c]
                yield wi_raw[:], wi_hi[:], wi_lo[:]

            @block.gpsimd
            def _(pool):
                nc.gpsimd.memset(eps[:], EPS).then_inc(const_ready, 1)
                nc.gpsimd.memset(ones[:], 1.0 / P).then_inc(const_ready, 1)
                for n in range(NK):
                    h, (t0, c) = n // len(TILES), TILES[n % len(TILES)]
                    pool.wait_ge(khi_ready, n + 1)
                    nc.gpsimd.tensor_tensor(out=kt_lo[:, h, t0:t0 + c], in0=kn[:, 0:c],
                                            in1=kt_hi[:, h, t0:t0 + c], op=ALU.subtract).then_inc(klo_ready, 1)

            @block.scalar
            def _(act):
                act.wait_ge(const_ready, 2)
                act.wait_ge(w_loaded, LOADS * 16)
                for raw, hi, _ in parts():
                    nc.scalar.activation(hi, raw, ACT.Copy, scale=WSCALE).then_inc(hi_ready, 1)
                nc.scalar.activation(gks[:], gk[:], ACT.Copy, scale=1.0 / WSCALE).then_inc(gks_ready, 1)
                for n in range(NK):
                    h, (t0, c) = n // len(TILES), TILES[n % len(TILES)]
                    act.wait_ge(z_ready, n + 1)
                    nc.scalar.activation(sq[:, 0:c], pz[n % 2][:, 0:c], ACT.Square,
                                         scale=1.0 / WSCALE).then_inc(sq_ready, 1)
                    act.wait_ge(ms_ready, n + 1)
                    nc.scalar.activation(lnm[:, 0:c], pm[:, 0:c], ACT.Ln, bias=eps[:]).then_inc(ln_ready, 1)
                    act.wait_ge(ln_ready, n + 1)
                    nc.scalar.activation(rin[:, 0:c], lnm[:, 0:c], ACT.Exp, scale=-0.5).then_inc(rin_ready, 1)
                    act.wait_ge(kn_ready, n + 1)
                    nc.scalar.activation(kt_hi[:, h, t0:t0 + c], kn[:, 0:c], ACT.Copy).then_inc(khi_ready, 1)
                for j, (t0, c) in enumerate(TILES):
                    act.wait_ge(z_ready, NK + j + 1)
                    nc.scalar.activation(ik_hi[:, t0:t0 + c], pz[(NK + j) % 2][:, 0:c], ACT.Copy,
                                         scale=1.0 / WSCALE).then_inc(ihi_ready, 1)

            @block.vector
            def _(dve):
                for n, (raw, hi, lo) in enumerate(parts()):
                    dve.wait_ge(hi_ready, n + 1)
                    nc.vector.scalar_tensor_tensor(out=lo, in0=raw, scalar=WSCALE, in1=hi, op0=ALU.mult,
                                                   op1=ALU.subtract).then_inc(lo_ready, 1)
                dve.wait_ge(gks_ready, 1)
                for n in range(NK):
                    c = TILES[n % len(TILES)][1]
                    dve.wait_ge(rin_ready, n + 1)
                    dve.wait_ge(klo_ready, n)
                    nc.vector.scalar_tensor_tensor(out=kn[:, 0:c], in0=pz[n % 2][:, 0:c], scalar=gks[:],
                                                   in1=rin[:, 0:c], op0=ALU.mult,
                                                   op1=ALU.mult).then_inc(kn_ready, 1)
                for j, (t0, c) in enumerate(TILES):
                    dve.wait_ge(ihi_ready, j + 1)
                    nc.vector.scalar_tensor_tensor(out=ik_lo[:, t0:t0 + c], in0=pz[(NK + j) % 2][0:ID, 0:c],
                                                   scalar=1.0 / WSCALE, in1=ik_hi[0:ID, t0:t0 + c],
                                                   op0=ALU.mult, op1=ALU.subtract).then_inc(ilo_ready, 1)
                for w in range(NW):
                    dve.wait_ge(v_ready, w + 1)
                    nc.vector.tensor_scalar(v_all[:, w, :], pv[w % 2][:, 0:KVH * P], 1.0 / WSCALE, None, ALU.mult)
                    nc.vector.tensor_scalar(iw_all[:, w, :], pv[w % 2][:, KVH * P:KVH * P + IH],
                                            IW_SCALE / WSCALE, None, ALU.mult).then_inc(vcopy_ready, 1)

            @block.tensor
            def _(pe):
                def project(out, hi, lo, t0, c):
                    n = 0
                    for k in range(KD):
                        for w, m in ((hi, ut_hi), (hi, ut_lo), (lo, ut_hi)):
                            mm = nc.tensor.matmul(out[:, 0:c], w[:, k, :], m[:, k, t0:t0 + c],
                                                  start=n == 0, stop=n == 3 * KD - 1)
                            n += 1
                    return mm

                pe.wait_ge(const_ready, 2)
                pe.wait_ge(lo_ready, 6)
                for n in range(NK + len(TILES)):
                    h, (t0, c) = n // len(TILES), TILES[n % len(TILES)]
                    if 2 <= n < NK + 2:
                        pe.wait_ge(kn_ready, n - 1)
                    if n >= NK + 2:
                        pe.wait_ge(ilo_ready, n - NK - 1)
                    project(pz[n % 2], w_hi[h], w_lo[h], t0, c).then_inc(z_ready, 1)
                    if 1 <= n <= NK:
                        c = TILES[(n - 1) % len(TILES)][1]
                        pe.wait_ge(sq_ready, n)
                        nc.tensor.matmul(pm[:, 0:c], ones[:], sq[:, 0:c], start=True, stop=True).then_inc(ms_ready, 1)
                for w in range(NW):
                    if w >= 2:
                        pe.wait_ge(vcopy_ready, w - 1)
                    for o, hi, lo in ((pv[w % 2][:, 0:KVH * P], wv_hi, wv_lo),
                                      (pv[w % 2][:, KVH * P:KVH * P + IH], wi_hi, wi_lo)):
                        n = 0
                        for k in range(KD):
                            for m, wt in ((ut_hi, hi), (ut_hi, lo), (ut_lo, hi)):
                                mm = nc.tensor.matmul(o, m[:, k, w * P:(w + 1) * P], wt[:, k, :],
                                                      start=n == 0, stop=n == 3 * KD - 1)
                                n += 1
                    mm.then_inc(v_ready, 1)


def queries(nc, w_cols, q_norm_g, ut_hi, ut_lo, aq_parts, iq_parts, ag):
    ITER = 4
    HPI = AH // ITER
    items = [(kind, h, t) for h in range(HPI) for t in range(NTILE) for kind in "qg"]
    items += [("i", 0, t) for t in range(NTILE)]
    NI = len(items)
    QPI = HPI * NTILE
    slot = {("q", 0): 0, ("g", 0): 1, ("q", 1): 2, ("g", 1): 3, ("i", 0): 4}
    with ExitStack() as ctx:
        def sb(name, shape, dt=F32):
            return ctx.enter_context(nc.sbuf_tensor("q_" + name, shape, dt))

        def two(name, shape, dt=F32):
            return [sb(f"{name}{b}", shape, dt) for b in range(2)]

        sem = Semaphores(nc, ctx, "q_")

        w_raw = two("w_raw", [P, KD, P])
        w_hi = [sb(f"w_hi{b}", [P, KD, P], F16) for b in range(5)]
        w_lo = [sb(f"w_lo{b}", [P, KD, P], F16) for b in range(5)]
        gq = sb("gq", [P, 1])
        gqs = sb("gqs", [P, AH])
        eps = sb("eps", [P, 1])
        ones = sb("ones", [P, P])
        sq, lnm, rin, qn = two("sq", [P, TILE]), sb("lnm", [P, TILE]), two("rin", [P, TILE]), two("qn", [P, TILE])
        qh, ql = two("qh", [P, TILE], F16), two("ql", [P, TILE], F16)
        ih, il = two("ih", [P, TILE], F16), two("il", [P, TILE], F16)
        gs = two("gs", [P, TILE])
        pz = [ctx.enter_context(nc.psum_tensor(f"q_pz{b}", [P, TILE], F32)) for b in range(4)]
        pm = [ctx.enter_context(nc.psum_tensor(f"q_pm{b}", [P, TILE], F32)) for b in range(2)]

        g_loaded, w_loaded = sem("g_loaded"), sem.two("w_loaded")
        hi_ready, lo_ready, const_ready, gqs_ready = (sem(n) for n in ("hi_ready", "lo_ready", "const_ready", "gqs_ready"))
        z_ready, sq_ready, ms_ready, ln_ready, rin_ready = (sem(n) for n in ("z_ready", "sq_ready", "ms_ready", "ln_ready", "rin_ready"))
        qn_ready, qhi_ready, qlo_ready = (sem(n) for n in ("qn_ready", "qhi_ready", "qlo_ready"))
        gs_ready, ihi_ready, ilo_ready = (sem(n) for n in ("gs_ready", "ihi_ready", "ilo_ready"))
        store_turn = sem("store_turn")
        q_stored, g_stored, i_stored = (sem.two(n) for n in ("q_stored", "g_stored", "i_stored"))

        class Item:

            def __init__(self, i, s):
                self.kind, self.h, self.t = items[s]
                self.s, self.n = s, i * NI + s
                before = sum(1 for k, _, _ in items[:s] if k == self.kind)
                per = sum(1 for k, _, _ in items if k == self.kind)
                self.m = i * per + before
                self.b = before % 2
                self.uses = i * (per // 2) + before // 2
                self.head = i * HPI + self.h
                self.pair = i
                self.t0 = P + self.t * TILE

        BEFORE = [0, 1, 2, 3]
        INSIDE = {2: [(0, 4)], 9: [(1, 0), (1, 1)], 17: [(1, 2), (1, 3)]}
        SPLITS = 5

        def column(i, sl):
            return {0: C_AQ + i * HPI * P, 1: C_AG + i * HPI * P, 2: C_AQ + i * HPI * P + P,
                    3: C_AG + i * HPI * P + P, 4: C_IQ + i * P}[sl]

        with nc.Block() as block:
            @block.sync
            def _(sp):
                sp.dma_start(gq[:], q_norm_g.rearrange("o p -> p o"),
                             allow_slow_non_contiguous=True).then_inc(g_loaded, 16)
                for n, sl in enumerate(BEFORE):
                    if n >= 2:
                        sp.wait_ge(lo_ready, n - 1)
                    sp.dma_start(w_raw[n % 2][:], w_cols[:, :, column(0, sl):column(0, sl) + P]
                                 ).then_inc(w_loaded[n % 2], 16)
                with sp.Fori(0, ITER // 2) as ii:
                    for half in range(2):
                        i = ii * 2 + half
                        at = 0
                        for s in range(NI):
                            for ahead, sl in INSIDE.get({0: 2, 5: 9, 13: 17}.get(s), ()):
                                b = (half * SPLITS + at) % 2
                                sp.wait_ge(lo_ready, i * SPLITS + at + 3)
                                sp.dma_start(w_raw[b][:], w_cols[:, :, bass.ds(column(i + ahead, sl), P)]
                                             ).then_inc(w_loaded[b], 16)
                                at += 1
                            x = Item(i, s)
                            if x.kind == "q":
                                sp.wait_ge(qlo_ready, x.m + 1)
                                for part, o in enumerate((qh, ql)):
                                    sp.dma_start(aq_parts[part, :, bass.ds(x.head * SEQ + x.t * TILE, TILE)],
                                                 o[x.b][:]).then_inc(q_stored[x.b], 16)
                            elif x.kind == "g":
                                sp.wait_ge(gs_ready, x.m + 1)
                                sp.sem_inc(store_turn, 1)
                                sp.dma_start(ag[:, bass.ds(x.head * SEQ + x.t * TILE, TILE)],
                                             gs[x.b][:]).then_inc(g_stored[x.b], 16)
                            else:
                                sp.wait_ge(ilo_ready, x.m + 1)
                                for part, o in enumerate((ih, il)):
                                    sp.dma_start(iq_parts[part, :, bass.ds(x.pair * SEQ + x.t * TILE, TILE)],
                                                 o[x.b][:]).then_inc(i_stored[x.b], 16)
                for b in range(2):
                    sp.wait_ge(q_stored[b], ITER * QPI * 16)
                    sp.wait_ge(g_stored[b], ITER * QPI // 2 * 16)
                    sp.wait_ge(i_stored[b], ITER * NTILE * 16)

            @block.gpsimd
            def _(pool):
                nc.gpsimd.memset(eps[:], EPS).then_inc(const_ready, 1)
                nc.gpsimd.memset(ones[:], 1.0 / P).then_inc(const_ready, 1)
                with pool.Fori(0, ITER) as i:
                    for s in range(NI):
                        x = Item(i, s)
                        if x.kind == "q":
                            pool.wait_ge(qhi_ready, x.m + 1)
                            pool.wait_ge(q_stored[x.b], x.uses * 32)
                            nc.gpsimd.tensor_tensor(out=ql[x.b][:], in0=qn[x.b][:], in1=qh[x.b][:],
                                                    op=ALU.subtract).then_inc(qlo_ready, 1)

            def split_positions():
                at = 0
                for s in sorted(INSIDE):
                    for _, sl in INSIDE[s]:
                        yield s, at, sl, {4: 0, 0: 8, 1: 8, 2: 16, 3: 16}[sl]
                        at += 1

            @block.scalar
            def _(act):
                act.wait_ge(const_ready, 2)
                act.wait_ge(g_loaded, 16)
                for h in range(AH):
                    nc.scalar.activation(gqs[:, h:h + 1], gq[:], ACT.Copy,
                                         scale=P ** -0.5 * 2.0 ** (h + 1) / WSCALE).then_inc(gqs_ready, 1)

                def split(sl, b, loads, done):
                    act.wait_ge(w_loaded[b], loads)
                    if done is not None:
                        act.wait_ge(z_ready, done)
                    nc.scalar.activation(w_hi[sl][:], w_raw[b][:], ACT.Copy, scale=WSCALE).then_inc(hi_ready, 1)

                def norm_tail(x):
                    act.wait_ge(ms_ready, x.m + 1)
                    act.wait_ge(rin_ready, x.m)
                    nc.scalar.activation(lnm[:], pm[x.b][:], ACT.Ln, bias=eps[:]).then_inc(ln_ready, 1)
                    act.wait_ge(ln_ready, x.m + 1)
                    nc.scalar.activation(rin[x.b][:], lnm[:], ACT.Exp, scale=-0.5).then_inc(rin_ready, 1)
                    act.wait_ge(qn_ready, x.m + 1)
                    act.wait_ge(q_stored[x.b], x.uses * 32)
                    nc.scalar.activation(qh[x.b][:], qn[x.b][:], ACT.Copy).then_inc(qhi_ready, 1)

                for n, sl in enumerate(BEFORE):
                    split(sl, n % 2, (n // 2 + 1) * 16, None)
                with act.Fori(0, ITER // 2) as ii:
                    for half in range(2):
                        i = ii * 2 + half
                        for s in range(NI):
                            for s_, at, sl, done in split_positions():
                                if s_ == s:
                                    k = half * SPLITS + at
                                    split(sl, k % 2, (2 + ii * SPLITS + k // 2 + 1) * 16, i * NI + done)
                            x = Item(i, s)
                            act.wait_ge(z_ready, x.n + 1)
                            if x.kind == "q":
                                nc.scalar.activation(sq[x.b][:], pz[s % 4][:], ACT.Square,
                                                     scale=1.0 / WSCALE).then_inc(sq_ready, 1)
                            elif x.kind == "g":
                                act.wait_ge(g_stored[x.b], x.uses * 16)
                                nc.scalar.activation(gs[x.b][:], pz[s % 4][:], ACT.Silu,
                                                     scale=1.0 / WSCALE).then_inc(gs_ready, 1)
                                norm_tail(Item(i, s - 1))
                            else:
                                act.wait_ge(i_stored[x.b], x.uses * 32)
                                nc.scalar.activation(ih[x.b][:], pz[s % 4][:], ACT.Copy,
                                                     scale=1.0 / WSCALE).then_inc(ihi_ready, 1)

            @block.vector
            def _(dve):
                def split(sl, b, count):
                    dve.wait_ge(hi_ready, count + 1)
                    nc.vector.scalar_tensor_tensor(out=w_lo[sl][:], in0=w_raw[b][:], scalar=WSCALE,
                                                   in1=w_hi[sl][:], op0=ALU.mult,
                                                   op1=ALU.subtract).then_inc(lo_ready, 1)

                for n, sl in enumerate(BEFORE):
                    split(sl, n % 2, n)
                dve.wait_ge(gqs_ready, AH)
                with dve.Fori(0, ITER // 2) as ii:
                    for half in range(2):
                        i = ii * 2 + half
                        for s in range(NI):
                            for s_, at, sl, done in split_positions():
                                if s_ == s:
                                    split(sl, (half * SPLITS + at) % 2, i * SPLITS + at + 4)
                            x = Item(i, s)
                            if x.kind == "g":
                                y = Item(i, s - 1)
                                dve.wait_ge(rin_ready, y.m + 1)
                                nc.vector.scalar_tensor_tensor(
                                    out=qn[y.b][:], in0=pz[(s - 1) % 4][:], scalar=gqs[:, bass.ds(y.head, 1)],
                                    in1=rin[y.b][:], op0=ALU.mult, op1=ALU.mult).then_inc(qn_ready, 1)
                            elif x.kind == "i":
                                dve.wait_ge(ihi_ready, x.m + 1)
                                nc.vector.scalar_tensor_tensor(
                                    out=il[x.b][:], in0=pz[s % 4][:], scalar=1.0 / WSCALE, in1=ih[x.b][:],
                                    op0=ALU.mult, op1=ALU.subtract).then_inc(ilo_ready, 1)

            @block.tensor
            def _(pe):
                pe.wait_ge(const_ready, 2)
                used = {"q": qn_ready, "g": gs_ready, "i": ilo_ready}
                with pe.Fori(0, ITER) as i:
                    for s in range(NI):
                        x = Item(i, s)
                        need = {0: i * SPLITS + 2, 8: i * SPLITS + 4, 16: i * SPLITS + 5}
                        if s in need:
                            pe.wait_ge(lo_ready, need[s])
                        if s == 0:
                            pe.wait_ge(ilo_ready, i * NTILE)
                        if s >= 4:
                            y = Item(i, s - 4)
                            pe.wait_ge(used[y.kind], y.m + 1)
                        n = 0
                        sl = slot[x.kind, x.h]
                        for k in range(KD):
                            for w, m in ((w_hi, ut_hi), (w_hi, ut_lo), (w_lo, ut_hi)):
                                mm = nc.tensor.matmul(pz[s % 4][:], w[sl][:, k, :], m[:, k, x.t0:x.t0 + TILE],
                                                      start=n == 0, stop=n == 3 * KD - 1)
                                n += 1
                        mm.then_inc(z_ready, 1)
                        if x.kind == "g":
                            y = Item(i, s - 1)
                            pe.wait_ge(sq_ready, y.m + 1)
                            nc.tensor.matmul(pm[y.b][:], ones[:], sq[y.b][:], start=True,
                                             stop=True).then_inc(ms_ready, 1)


def attention(nc, aq_parts, iq_parts, ag, kt_hi, kt_lo, v_all, ik_hi, ik_lo, iw_all, oa_parts, ident):
    NB = SEQ // P
    NEG = -1.0e30
    LOWEST = -3.0e38
    SEARCH0 = TOPK // P

    def keys(n):
        return (n + 1) * P

    def tiles(n):
        return [(max(c, PAD), min(c + TILE, keys(n))) for c in range(0, keys(n), TILE)]

    def scored_before(n, first):
        return sum(AH * len(tiles(m)) for m in range(first, n))

    def products_before(n):
        return sum(KVH * (m + 1) for m in range(1, n))

    def turned_before(n):
        return sum(KVH * (m + 2) for m in range(1, n))

    with ExitStack() as ctx:
        def sb(name, shape, dt=F32):
            return ctx.enter_context(nc.sbuf_tensor("a_" + name, shape, dt))

        def two(name, shape, dt=F32):
            return [sb(f"{name}{b}", shape, dt) for b in range(2)]

        sem = Semaphores(nc, ctx, "a_")

        def bank(name):
            return ctx.enter_context(nc.psum_tensor("a_" + name, [P, TILE], F32))

        q_hi, q_lo = two("q_hi", [P, AH, P], F16), two("q_lo", [P, AH, P], F16)
        iq = two("iq", [P, 2, IH // 2, P], F16)
        gate = two("gate", [P, AH, P])
        relu = [sb(f"relu{b}", [P, TILE]) for b in range(4)]
        score = sb("score", [P, T])
        folded = sb("folded", [P, T])
        agree = sb("agree", [P, T])
        low = sb("low", [P, T])
        bias = sb("bias", [P, T])
        junk = sb("junk", [P, T], F16)
        prob = sb("prob", [P, AH, T])
        pt = two("pt", [P, TILE])
        mx = sb("mx", [P, AH, 5])
        mxr = sb("mxr", [P, AH])
        nb = sb("nb", [P, AH])
        nslope = sb("nslope", [P, AH])
        rows = sb("rows", [P, AH])
        rinv = sb("rinv", [P, AH])
        diag = two("diag", [P, AG, P])
        rb = two("rb", [P, TILE])
        gr = two("gr", [P, TILE])
        og = rb
        oh, ol = two("oh", [P, TILE], F16), two("ol", [P, TILE], F16)
        ones = sb("ones", [P, P])
        cnt, neg, sgn, want, want2 = (sb(n, [P, 1]) for n in ("cnt", "neg", "sgn", "want", "want2"))
        keep, cand, cand2, up, need, thr, sthr = (sb(n, [P, 1]) for n in ("keep", "cand", "cand2", "up", "need", "thr", "sthr"))

        qk = [bank("qk0"), bank("qk1")]
        lg = [bank("lg0"), bank("lg1")]
        tp = [bank("tp0"), bank("tp1")]
        po = [bank("po0"), bank("po1")]

        q_loaded = sem.two("q_loaded")
        const_ready = sem("const_ready")
        lg_ready, relu_ready, sc_ready, sfill_ready = (sem(n) for n in ("lg_ready", "relu_ready", "sc_ready", "sfill_ready"))
        dist_ready, bias_ready, bfill_ready = sem("dist_ready"), sem("bias_ready"), sem("bfill_ready")
        qk_ready, biased_ready, nb_ready, prob_ready = (sem(n) for n in ("qk_ready", "biased_ready", "nb_ready", "prob_ready"))
        rinv_ready, diag_ready, tp_ready, pt_ready = (sem(n) for n in ("rinv_ready", "diag_ready", "tp_ready", "pt_ready"))
        gr_ready, og_ready, ohi_ready, olo_ready = (sem(n) for n in ("gr_ready", "og_ready", "ohi_ready", "olo_ready"))
        pv_done, step, stored = sem("pv_done"), sem("step"), sem.two("stored")

        with nc.Block() as block:
            @block.sync
            def _(sp):
                def load(n):
                    b = n % 2
                    if n > 2:
                        sp.wait_ge(pv_done, products_before(n - 1))
                        sp.wait_ge(gr_ready, KVH * (n - 2))
                    t = slice((n - 1) * P, n * P)
                    for src, dst in ((0, q_hi), (1, q_lo)):
                        sp.dma_start(dst[b][:], aq_parts[src].rearrange("p (h t) -> p h t", t=SEQ)[:, :, t]
                                     ).then_inc(q_loaded[b], 16)
                    for part in range(2):
                        for odd in range(2):
                            sp.dma_start(iq[b][part * ID:(part + 1) * ID, odd, :, :],
                                         iq_parts[part, odd * ID:(odd + 1) * ID].rearrange(
                                             "p (h t) -> p h t", t=SEQ)[:, :, t]).then_inc(q_loaded[b], 16)
                    sp.dma_start(gate[b][:], ag.rearrange("p (h t) -> p h t", t=SEQ)[:, :, t]
                                 ).then_inc(q_loaded[b], 16)

                load(1)
                load(2)
                for n in range(1, NB + 1):
                    for g in range(KVH):
                        sp.wait_ge(olo_ready, KVH * (n - 1) + g + 1)
                        for part, o in enumerate((oh, ol)):
                            dst = oa_parts[part].rearrange("p (h t) -> p h t", t=SEQ)
                            sp.dma_start(dst[:, g * AG:(g + 1) * AG, (n - 1) * P:n * P],
                                         o[g][:].rearrange("p (h t) -> p h t", t=P)).then_inc(stored[g], 16)
                    if n + 2 <= NB:
                        load(n + 2)
                for g in range(KVH):
                    sp.wait_ge(stored[g], NB * 32)

            LOADS = 7 * 16

            @block.gpsimd
            def _(pool):
                for h in range(AH):
                    nc.gpsimd.memset(nslope[:, h:h + 1], -2.0 ** -(h + 1)).then_inc(const_ready, 1)
                nc.gpsimd.memset(ones[:], 1.0).then_inc(const_ready, 1)
                nc.gpsimd.memset(prob[:, :, 0:PAD], 0.0).then_inc(const_ready, 1)

                def distances(n):
                    c = keys(n) - PAD
                    nc.gpsimd.iota(bias[:, PAD:keys(n)], pattern=[[1, c]], base=PAD - n * P, channel_multiplier=-1,
                                   allow_small_or_imprecise_dtypes=True).then_inc(dist_ready, 1)

                def causal(buf, n, fill):
                    d = buf[:, n * P:keys(n)]
                    return nc.gpsimd.affine_select(out=d, in_=d, compare_op=ALU.is_ge, fill=fill, base=0,
                                                   pattern=[[-1, P]], channel_multiplier=1)

                distances(1)
                pool.wait_ge(dist_ready, 1)
                causal(bias, 1, NEG).then_inc(bfill_ready, 1)
                for n in range(1, NB + 1):
                    if n < NB:
                        pool.wait_ge(biased_ready, scored_before(n + 1, 1))
                        distances(n + 1)
                        pool.wait_ge(sc_ready, scored_before(n + 2, 2))
                        causal(score, n + 1, LOWEST).then_inc(sfill_ready, 1)
                    pool.wait_ge(rinv_ready, n)
                    if n == 1:
                        pool.wait_ge(const_ready, AH + 2)
                    for g in range(KVH):
                        if n > 1:
                            pool.wait_ge(tp_ready, turned_before(n))
                        h = slice(g * AG, (g + 1) * AG)
                        nc.gpsimd.tensor_tensor(out=diag[g][:], in0=ident[:, None, :].broadcast_to([P, AG, P]),
                                                in1=rinv[:, h, None].broadcast_to([P, AG, P]),
                                                op=ALU.mult).then_inc(diag_ready, 1)
                    for g in range(KVH):
                        pool.wait_ge(pt_ready, turned_before(n + 1) - KVH + g + 1)
                        if n == 1:
                            pool.wait_ge(q_loaded[1], LOADS)
                        else:
                            pool.wait_ge(q_loaded[n % 2], (n + 1) // 2 * LOADS)
                        nc.gpsimd.tensor_tensor(out=gr[g][:], in0=rb[g][:],
                                                in1=gate[n % 2][:, g * AG:(g + 1) * AG, :], op=ALU.mult
                                                ).then_inc(gr_ready, 1)
                    if n < NB:
                        pool.wait_ge(bias_ready, n)
                        causal(bias, n + 1, NEG).then_inc(bfill_ready, 1)
                    for g in range(KVH):
                        pool.wait_ge(ohi_ready, KVH * (n - 1) + g + 1)
                        pool.wait_ge(stored[g], (n - 1) * 32)
                        nc.gpsimd.tensor_tensor(out=ol[g][:], in0=og[g][:], in1=oh[g][:],
                                                op=ALU.subtract).then_inc(olo_ready, 1)

            @block.scalar
            def _(act):
                def relus(n):
                    i = scored_before(n, 2)
                    for h in range(IH):
                        for a, b in tiles(n):
                            act.wait_ge(lg_ready, i + 1)
                            if i >= 4:
                                act.wait_ge(sc_ready, i - 3)
                            nc.scalar.activation(relu[i % 4][:, 0:b - a], lg[i % 2][:, 0:b - a],
                                                 ACT.Relu).then_inc(relu_ready, 1)
                            i += 1

                for n in range(1, NB + 1):
                    for h in range(AH):
                        act.wait_ge(nb_ready, KVH * (n - 1) + h // AG + 1)
                        p = prob[:, h, PAD:keys(n)]
                        nc.scalar.activation(p, p, ACT.Exp, bias=nb[:, h:h + 1], scale=2.0 ** -(h + 1),
                                             accum_out=rows[:, h:h + 1]).then_inc(prob_ready, 1)
                    if n < NB:
                        relus(n + 1)
                    i = turned_before(n)
                    for j in range(KVH * (n + 1)):
                        act.wait_ge(tp_ready, i + 1)
                        if j >= 2:
                            act.wait_ge(pv_done, products_before(n) + j - 1)
                        elif n > 1:
                            act.wait_ge(pv_done, products_before(n))
                        nc.scalar.activation(pt[i % 2][:], tp[i % 2][:], ACT.Copy).then_inc(pt_ready, 1)
                        i += 1
                    for g in range(KVH):
                        act.wait_ge(tp_ready, i + 1)
                        if n > 1:
                            act.wait_ge(olo_ready, KVH * (n - 1))
                        nc.scalar.activation(rb[g][:], tp[i % 2][:], ACT.Copy).then_inc(pt_ready, 1)
                        i += 1
                    for g in range(KVH):
                        act.wait_ge(og_ready, KVH * (n - 1) + g + 1)
                        act.wait_ge(stored[g], (n - 1) * 32)
                        nc.scalar.activation(oh[g][:], og[g][:], ACT.Copy).then_inc(ohi_ready, 1)

            @block.vector
            def _(dve):
                done = [0]

                def then(ins):
                    done[0] += 1
                    ins.then_inc(step, 1)
                    dve.wait_ge(step, done[0])

                V = nc.vector
                dve.wait_ge(const_ready, AH + 2)

                def scores(n):
                    i = scored_before(n, 2)
                    nt = len(tiles(n))
                    for h in range(IH):
                        for a, b in tiles(n):
                            dve.wait_ge(relu_ready, i + 1)
                            iw = iw_all[:, n, h:h + 1]
                            r = relu[i % 4][:, 0:b - a]
                            if h == 0:
                                V.tensor_scalar(score[:, a:b], r, iw, None, ALU.mult).then_inc(sc_ready, 1)
                            else:
                                dve.wait_ge(sc_ready, i - nt + 1)
                                V.scalar_tensor_tensor(out=score[:, a:b], in0=r, scalar=iw, in1=score[:, a:b],
                                                       op0=ALU.mult, op1=ALU.add).then_inc(sc_ready, 1)
                            i += 1

                def count(x, limit, op, out, width):
                    then(V.tensor_scalar(junk[:, 0:width], x, limit, None, op, ALU.add, accum_out=out[:]))

                def select(n):
                    c, e = keys(n) - PAD, keys(n)
                    s = score[:, PAD:e]
                    halves = folded[:, PAD:e].bitcast(I16)
                    upper = halves.rearrange("p (c two) -> p c two", two=2)[:, :, 1]
                    lower = folded[:, PAD:e].bitcast(U16).rearrange("p (c two) -> p c two", two=2)[:, :, 0]
                    dve.wait_ge(sfill_ready, n - 1)
                    count(s, 0.0, ALU.is_ge, cnt, c)
                    then(V.tensor_scalar(neg[:], cnt[:], float(TOPK), None, ALU.is_lt))
                    V.tensor_scalar(want[:], neg[:], float(c + 1 - 2 * TOPK), float(TOPK), ALU.mult, ALU.add)
                    then(V.tensor_scalar(sgn[:], neg[:], -2.0, 1.0, ALU.mult, ALU.add))
                    then(V.tensor_scalar(folded[:, PAD:e], s, sgn[:], None, ALU.mult))
                    then(V.memset(cand[:], 2.0 ** 14))
                    for bit in range(14, -1, -1):
                        count(upper, cand[:], ALU.is_ge, cnt, c)
                        then(V.tensor_scalar(keep[:], cnt[:], want[:], 0.5, ALU.is_ge, ALU.subtract))
                        then(V.scalar_tensor_tensor(out=cand[:], in0=keep[:], scalar=2.0 ** bit, in1=cand[:],
                                                    op0=ALU.mult, op1=ALU.add))
                    count(upper, cand[:], ALU.is_ge, cnt, c)
                    V.tensor_scalar(up[:], cand[:], 0.5, None, ALU.subtract)
                    then(V.tensor_tensor(out=want2[:], in0=want[:], in1=cnt[:], op=ALU.subtract))
                    then(V.tensor_scalar(agree[:, PAD:e], upper, up[:], None, ALU.is_equal))
                    V.memset(cand2[:], 2.0 ** 15 + 1.0)
                    then(V.scalar_tensor_tensor(out=low[:, PAD:e], in0=lower, scalar=1.0, in1=agree[:, PAD:e],
                                                op0=ALU.add, op1=ALU.mult))
                    for bit in range(15, -1, -1):
                        count(low[:, PAD:e], cand2[:], ALU.is_ge, cnt, c)
                        then(V.tensor_scalar(keep[:], cnt[:], want2[:], 0.5, ALU.is_ge, ALU.subtract))
                        then(V.scalar_tensor_tensor(out=cand2[:], in0=keep[:], scalar=2.0 ** bit, in1=cand2[:],
                                                    op0=ALU.mult, op1=ALU.add))
                    V.tensor_scalar(thr[:].bitcast(U16)[:, 0:1], cand2[:], 1.5, None, ALU.subtract)
                    then(V.tensor_scalar(thr[:].bitcast(I16)[:, 1:2], up[:], 1.0, None, ALU.mult))
                    then(V.tensor_tensor(out=sthr[:], in0=thr[:], in1=sgn[:], op=ALU.mult))
                    count(s, sthr[:], ALU.is_gt, cnt, c)
                    V.tensor_scalar(need[:], cnt[:], -1.0, float(TOPK), ALU.mult, ALU.add)
                    tie, rank = agree[:, PAD:e], low[:, PAD:e]
                    then(V.tensor_scalar(tie, s, sthr[:], None, ALU.is_equal))
                    then(V.tensor_tensor_scan(out=rank, data0=tie, data1=tie, initial=0.0, op0=ALU.add, op1=ALU.max))
                    then(V.scalar_tensor_tensor(out=rank, in0=rank, scalar=need[:], in1=tie, op0=ALU.is_gt,
                                                op1=ALU.mult))
                    then(V.scalar_tensor_tensor(out=rank, in0=s, scalar=sthr[:], in1=rank, op0=ALU.is_lt,
                                                op1=ALU.add))
                    dve.wait_ge(dist_ready, n)
                    V.scalar_tensor_tensor(out=bias[:, PAD:e], in0=rank, scalar=NEG, in1=bias[:, PAD:e],
                                           op0=ALU.mult, op1=ALU.add).then_inc(bias_ready, 1)

                for n in range(1, NB + 1):
                    i = scored_before(n, 1)
                    nt = len(tiles(n))
                    dve.wait_ge(bfill_ready, n)
                    if n > 1:
                        dve.wait_ge(pv_done, products_before(n))
                    for h in range(AH):
                        for t, (a, b) in enumerate(tiles(n)):
                            dve.wait_ge(qk_ready, i + 1)
                            i += 1
                            V.tensor_tensor_reduce(out=prob[:, h, a:b], in0=qk[(i - 1) % 2][:, 0:b - a],
                                                   in1=bias[:, a:b], scale=1.0, scalar=LOWEST, op0=ALU.add,
                                                   op1=ALU.max, accum_out=mx[:, h, t:t + 1]
                                                   ).then_inc(biased_ready, 1)
                        if h % AG == AG - 1:
                            g = slice(h + 1 - AG, h + 1)
                            dve.wait_ge(biased_ready, i)
                            then(V.tensor_reduce(mxr[:, g], mx[:, g, 0:nt], AX.X, ALU.max))
                            V.tensor_tensor(out=nb[:, g], in0=mxr[:, g], in1=nslope[:, g],
                                            op=ALU.mult).then_inc(nb_ready, 1)
                    if n < NB:
                        scores(n + 1)
                    dve.wait_ge(prob_ready, AH * n)
                    dve.wait_ge(diag_ready, KVH * (n - 1))
                    V.reciprocal(rinv[:], rows[:]).then_inc(rinv_ready, 1)
                    if n < NB and n + 1 >= SEARCH0:
                        select(n + 1)
                    for g in range(KVH):
                        dve.wait_ge(gr_ready, KVH * (n - 1) + g + 1)
                        dve.wait_ge(pv_done, products_before(n) + (g + 1) * (n + 1))
                        dve.wait_ge(olo_ready, KVH * (n - 1))
                        V.tensor_tensor(out=og[g][:], in0=po[g][:], in1=gr[g][:], op=ALU.mult).then_inc(og_ready, 1)

            @block.tensor
            def _(pe):
                def logits(n):
                    i = scored_before(n, 2)
                    pe.wait_ge(q_loaded[n % 2], (n + 1) // 2 * LOADS)
                    for h in range(IH):
                        w = iq[n % 2][:, h % 2, h // 2, :]
                        for a, b in tiles(n):
                            if i >= 2:
                                pe.wait_ge(relu_ready, i - 1)
                            nc.tensor.matmul(lg[i % 2][:, 0:b - a], w, ik_hi[:, a:b], start=True, stop=False)
                            nc.tensor.matmul(lg[i % 2][:, 0:b - a], w[0:ID], ik_lo[:, a:b],
                                             start=False, stop=True).then_inc(lg_ready, 1)
                            i += 1

                def dots(n):
                    i = scored_before(n, 1)
                    pe.wait_ge(q_loaded[n % 2], (n + 1) // 2 * LOADS)
                    for h in range(AH):
                        for a, b in tiles(n):
                            if i >= 2:
                                pe.wait_ge(biased_ready, i - 1)
                            o = qk[i % 2][:, 0:b - a]
                            g = h // AG
                            nc.tensor.matmul(o, q_hi[n % 2][:, h, :], kt_hi[:, g, a:b], start=True, stop=False)
                            nc.tensor.matmul(o, q_hi[n % 2][:, h, :], kt_lo[:, g, a:b], start=False, stop=False)
                            nc.tensor.matmul(o, q_lo[n % 2][:, h, :], kt_hi[:, g, a:b],
                                             start=False, stop=True).then_inc(qk_ready, 1)
                            i += 1

                def values(n):
                    i = turned_before(n)

                    def turn(j, i):
                        g, k = divmod(j, n + 1)
                        pe.wait_ge(prob_ready, AH * (n - 1) + AG * (g + 1))
                        if i >= 2:
                            pe.wait_ge(pt_ready, i - 1)
                        for h in range(AG):
                            mm = nc.tensor.transpose(tp[i % 2][:, h * P:(h + 1) * P],
                                                     prob[:, g * AG + h, k * P:(k + 1) * P], ident[:])
                        mm.then_inc(tp_ready, 1)

                    total = KVH * (n + 1)
                    turn(0, i)
                    for j in range(total):
                        if j + 1 < total:
                            turn(j + 1, i + j + 1)
                        g, k = divmod(j, n + 1)
                        pe.wait_ge(pt_ready, i + j + 1)
                        if n > 1 and k == 0:
                            pe.wait_ge(og_ready, KVH * (n - 2) + g + 1)
                        mm = nc.tensor.matmul(po[g][:], v_all[:, k, g * P:(g + 1) * P], pt[(i + j) % 2][:],
                                              start=k == 0, stop=k == n)
                        mm.then_inc(pv_done, 1)
                    i += total
                    for g in range(KVH):
                        pe.wait_ge(diag_ready, KVH * (n - 1) + g + 1)
                        pe.wait_ge(pt_ready, i - 1)
                        nc.tensor.matmul(tp[i % 2][:], ones[:], diag[g][:].rearrange("p h q -> p (h q)"),
                                         start=True, stop=True).then_inc(tp_ready, 1)
                        i += 1

                pe.wait_ge(const_ready, AH + 2)
                for n in range(1, NB + 1):
                    dots(n)
                    if n < NB:
                        logits(n + 1)
                    values(n)


def load_parts(nc, parts, hi, lo, loaded):
    with nc.Block() as block:
        @block.sync
        def _(sp):
            for part, dst in enumerate((hi, lo)):
                for h in range(KD):
                    c = slice(h * SEQ, (h + 1) * SEQ)
                    sp.dma_start(dst[:, c], parts[part, :, c]).then_inc(loaded, 16)
            sp.wait_ge(loaded, 2 * KD * 16)


def merge_recurrent(nc, w_cols, w_r, ut_hi, ut_lo, ogr, merged_r, gate_a):
    KINDS = "gay"
    NI = len(KINDS) * NTILE
    with ExitStack() as ctx:
        def sb(name, shape, dt=F32):
            return ctx.enter_context(nc.sbuf_tensor("mr_" + name, shape, dt))

        sem = Semaphores(nc, ctx, "mr_")

        og_hi, og_lo = sb("og_hi", [P, RH * SEQ], F16), sb("og_lo", [P, RH * SEQ], F16)
        w_raw = [sb(f"w_raw{s}", [P, KD, P]) for s in range(3)]
        w_hi = [sb(f"w_hi{s}", [P, KD, P], F16) for s in range(3)]
        w_lo = [sb(f"w_lo{s}", [P, KD, P], F16) for s in range(3)]
        sg = [sb(f"sg{b}", [P, TILE]) for b in range(NTILE)]
        sa = [sb(f"sa{b}", [P, TILE]) for b in range(2)]
        mr = [sb(f"mr{b}", [P, TILE]) for b in range(2)]
        pz = [ctx.enter_context(nc.psum_tensor(f"mr_pz{b}", [P, TILE], F32)) for b in range(4)]
        w_loaded = [sem(f"w_loaded{s}") for s in range(3)]
        hi_ready, lo_ready, z_ready = sem("hi_ready"), sem("lo_ready"), sem("z_ready")
        load_turn = sem("load_turn")
        sg_ready, sa_ready, mr_ready = sem("sg_ready"), sem("sa_ready"), sem("mr_ready")
        a_stored, y_stored = sem.two("a_stored"), sem.two("y_stored")

        load_parts(nc, ogr, og_hi, og_lo, sem("og_loaded"))
        w_rc = w_r.rearrange("(k p) n -> p k n", p=P)
        SOURCE = [(w_cols, C_MR), (w_cols, C_MA), (w_rc, 0)]
        FREED = [NTILE, 2 * NTILE, 3 * NTILE]
        SPLIT_AT = {1: (2, 0), NTILE + 1: (0, 1), 2 * NTILE + 1: (1, 1)}

        def all_steps(eng, body):
            with eng.Fori(0, KD - 1) as i:
                body(i, False)
            body(KD - 1, True)

        with nc.Block() as block:
            @block.sync
            def _(sp):
                def load(s, i):
                    src, c = SOURCE[s]
                    sp.dma_start(w_raw[s][:], src[:, :, bass.ds(i * P + c, P)]).then_inc(w_loaded[s], 16)

                for s in range(3):
                    load(s, 0)

                def body(i, last):
                    if not last:
                        for s in range(2):
                            sp.wait_ge(lo_ready, i * 3 + s + 1)
                            load(s, i + 1)
                    for s in range(NI):
                        kind, t = KINDS[s // NTILE], s % NTILE
                        c = bass.ds(i * SEQ + t * TILE, TILE)
                        if kind == "a":
                            sp.wait_ge(sa_ready, i * NTILE + t + 1)
                            sp.dma_start(gate_a[:, c], sa[t % 2][:]).then_inc(a_stored[t % 2], 16)
                        if kind == "y":
                            if t == 0 and not last:
                                sp.wait_ge(lo_ready, i * 3 + 3)
                                sp.sem_inc(load_turn, 1)
                                load(2, i + 1)
                            sp.wait_ge(mr_ready, i * NTILE + t + 1)
                            sp.dma_start(merged_r[:, c], mr[t % 2][:]).then_inc(y_stored[t % 2], 16)
                all_steps(sp, body)
                for b in range(2):
                    sp.wait_ge(a_stored[b], KD * NTILE // 2 * 16)
                    sp.wait_ge(y_stored[b], KD * NTILE // 2 * 16)

            @block.scalar
            def _(act):
                def split(s, i, freed):
                    act.wait_ge(w_loaded[s], (i + 1) * 16)
                    act.wait_ge(z_ready, freed)
                    nc.scalar.activation(w_hi[s][:], w_raw[s][:], ACT.Copy, scale=WSCALE).then_inc(hi_ready, 1)

                split(0, 0, 0)
                split(1, 0, 0)

                def body(i, last):
                    for s in range(NI):
                        if s in SPLIT_AT:
                            sl, ahead = SPLIT_AT[s]
                            if not (last and ahead):
                                split(sl, i + ahead, i * NI + (FREED[sl] if ahead else 0))
                        kind, t = KINDS[s // NTILE], s % NTILE
                        if kind == "y":
                            continue
                        act.wait_ge(z_ready, i * NI + s + 1)
                        if kind == "g":
                            act.wait_ge(mr_ready, i * NTILE)
                            nc.scalar.activation(sg[t][:], pz[s % 4][:], ACT.Sigmoid,
                                                 scale=1.0 / WSCALE).then_inc(sg_ready, 1)
                        else:
                            act.wait_ge(a_stored[t % 2], (i * 2 + t // 2) * 16)
                            nc.scalar.activation(sa[t % 2][:], pz[s % 4][:], ACT.Sigmoid,
                                                 scale=1.0 / WSCALE).then_inc(sa_ready, 1)
                all_steps(act, body)

            @block.vector
            def _(dve):
                def split(s, count):
                    dve.wait_ge(hi_ready, count)
                    nc.vector.scalar_tensor_tensor(out=w_lo[s][:], in0=w_raw[s][:], scalar=WSCALE, in1=w_hi[s][:],
                                                   op0=ALU.mult, op1=ALU.subtract).then_inc(lo_ready, 1)

                split(0, 1)
                split(1, 2)

                def body(i, last):
                    for s in range(NI):
                        if s in SPLIT_AT:
                            sl, ahead = SPLIT_AT[s]
                            if not (last and ahead):
                                split(sl, i * 3 + {2: 3, 0: 4, 1: 5}[sl])
                        if KINDS[s // NTILE] == "y":
                            t = s % NTILE
                            dve.wait_ge(z_ready, i * NI + s + 1)
                            dve.wait_ge(sg_ready, i * NTILE + t + 1)
                            dve.wait_ge(y_stored[t % 2], (i * 2 + t // 2) * 16)
                            nc.vector.scalar_tensor_tensor(out=mr[t % 2][:], in0=pz[s % 4][:], scalar=1.0 / WSCALE,
                                                           in1=sg[t][:], op0=ALU.mult,
                                                           op1=ALU.mult).then_inc(mr_ready, 1)
                all_steps(dve, body)

            @block.tensor
            def _(pe):
                def body(i, last):
                    for s in range(NI):
                        kind, t = KINDS[s // NTILE], s % NTILE
                        if t == 0:
                            pe.wait_ge(lo_ready, i * 3 + s // NTILE + 1)
                        pe.wait_ge({"g": mr_ready, "a": sg_ready, "y": sa_ready}[kind],
                                   i * NTILE if kind == "g" else i * NTILE + t + 1)
                        n = 0
                        for k in range(KD):
                            if kind == "y":
                                c = slice(k * SEQ + t * TILE, k * SEQ + (t + 1) * TILE)
                                hi, lo = og_hi[:, c], og_lo[:, c]
                            else:
                                c = slice(P + t * TILE, P + (t + 1) * TILE)
                                hi, lo = ut_hi[:, k, c], ut_lo[:, k, c]
                            sl = s // NTILE
                            for w, m in ((w_hi, hi), (w_hi, lo), (w_lo, hi)):
                                mm = nc.tensor.matmul(pz[s % 4][:], w[sl][:, k, :], m,
                                                      start=n == 0, stop=n == 3 * KD - 1)
                                n += 1
                        mm.then_inc(z_ready, 1)
                all_steps(pe, body)


def merge_and_project(nc, x, w_a, w_out, oa_parts, merged_r, gate_a, out):
    with ExitStack() as ctx:
        def sb(name, shape, dt=F32):
            return ctx.enter_context(nc.sbuf_tensor("mo_" + name, shape, dt))

        sem = Semaphores(nc, ctx, "mo_")

        og_hi, og_lo = sb("og_hi", [P, AH * SEQ], F16), sb("og_lo", [P, AH * SEQ], F16)
        m_hi, m_lo = sb("m_hi", [P, KD, SEQ], F16), sb("m_lo", [P, KD, SEQ], F16)
        w_raw = [sb(f"w_raw{b}", [P, KD, P]) for b in range(2)]
        w_hi = [sb(f"w_hi{b}", [P, KD, P], F16) for b in range(2)]
        w_lo = [sb(f"w_lo{b}", [P, KD, P], F16) for b in range(2)]
        wo_hi, wo_lo = sb("wo_hi", [P, KD, D], F16), sb("wo_lo", [P, KD, D], F16)
        rp = [sb(f"rp{b}", [P, TILE]) for b in range(2)]
        ga = [sb(f"ga{b}", [P, TILE]) for b in range(2)]
        ya = [sb(f"ya{b}", [P, TILE]) for b in range(2)]
        mg = [sb(f"mg{b}", [P, TILE]) for b in range(2)]
        xw = [sb(f"xw{b}", [P, D]) for b in range(2)]
        pz = [ctx.enter_context(nc.psum_tensor(f"mo_pz{b}", [P, TILE], F32)) for b in range(4)]
        w_loaded, t_loaded, x_loaded = (sem.two(n) for n in ("w_loaded", "t_loaded", "x_loaded"))
        hi_ready, lo_ready, z_ready = sem("hi_ready"), sem("lo_ready"), sem("z_ready")
        ya_ready, mg_ready, mhi_ready, mlo_ready = (sem(n) for n in ("ya_ready", "mg_ready", "mhi_ready", "mlo_ready"))
        o_ready, y_ready, stored = sem("o_ready"), sem("y_ready"), sem.two("stored")

        load_parts(nc, oa_parts, og_hi, og_lo, sem("og_loaded"))
        w_ac = w_a.rearrange("(k p) n -> p k n", p=P)
        w_oc = w_out.rearrange("(k p) n -> p k n", p=P)

        with nc.Block() as block:
            @block.sync
            def _(sp):
                with sp.Fori(0, KD // 2) as ii:
                    for b in range(2):
                        i = ii * 2 + b
                        sp.wait_ge(lo_ready, i * 2)
                        sp.dma_start(w_raw[0][:], w_ac[:, :, bass.ds(i * P, P)]).then_inc(w_loaded[0], 16)
                        sp.dma_start(w_raw[1][:], w_oc[:, :, bass.ds(i * P, P)]).then_inc(w_loaded[1], 16)
                        for t in range(NTILE):
                            c = bass.ds(i * SEQ + t * TILE, TILE)
                            sp.wait_ge(mg_ready, i * NTILE + max(0, t - 1))
                            sp.dma_start(rp[t % 2][:], merged_r[:, c]).then_inc(t_loaded[t % 2], 16)
                            sp.dma_start(ga[t % 2][:], gate_a[:, c]).then_inc(t_loaded[t % 2], 16)

            @block.gpsimd
            def _(pool):
                with pool.Fori(0, KD) as i:
                    for t in range(NTILE + 1):
                        if t < NTILE:
                            pool.wait_ge(ya_ready, i * NTILE + t + 1)
                            pool.wait_ge(mlo_ready, i * NTILE + max(0, t - 1))
                            nc.gpsimd.tensor_tensor(out=mg[t % 2][:], in0=ya[t % 2][:], in1=rp[t % 2][:],
                                                    op=ALU.add).then_inc(mg_ready, 1)
                        if t:
                            pool.wait_ge(mhi_ready, i * NTILE + t)
                            c = slice((t - 1) * TILE, t * TILE)
                            nc.gpsimd.tensor_tensor(out=m_lo[:, bass.ds(i, 1), c], in0=mg[(t - 1) % 2][:, None, :],
                                                    in1=m_hi[:, bass.ds(i, 1), c], op=ALU.subtract
                                                    ).then_inc(mlo_ready, 1)

            @block.scalar
            def _(act):
                with act.Fori(0, KD // 2) as ii:
                    for b in range(2):
                        i = ii * 2 + b
                        act.wait_ge(w_loaded[0], (i + 1) * 16)
                        act.wait_ge(z_ready, ii * 2 * NTILE)
                        nc.scalar.activation(w_hi[b][:], w_raw[0][:], ACT.Copy, scale=WSCALE).then_inc(hi_ready, 1)
                        act.wait_ge(w_loaded[1], (i + 1) * 16)
                        nc.scalar.activation(wo_hi[:, :, bass.ds(i * P, P)], w_raw[1][:], ACT.Copy,
                                             scale=WSCALE).then_inc(hi_ready, 1)
                        for t in range(NTILE):
                            act.wait_ge(mg_ready, i * NTILE + t + 1)
                            nc.scalar.activation(m_hi[:, bass.ds(i, 1), t * TILE:(t + 1) * TILE],
                                                 mg[t % 2][:, None, :], ACT.Copy).then_inc(mhi_ready, 1)

            @block.vector
            def _(dve):
                with dve.Fori(0, KD // 2) as ii:
                    for b in range(2):
                        i = ii * 2 + b
                        dve.wait_ge(hi_ready, i * 2 + 1)
                        nc.vector.scalar_tensor_tensor(out=w_lo[b][:], in0=w_raw[0][:], scalar=WSCALE,
                                                       in1=w_hi[b][:], op0=ALU.mult,
                                                       op1=ALU.subtract).then_inc(lo_ready, 1)
                        dve.wait_ge(hi_ready, i * 2 + 2)
                        c = bass.ds(i * P, P)
                        nc.vector.scalar_tensor_tensor(out=wo_lo[:, :, c], in0=w_raw[1][:], scalar=WSCALE,
                                                       in1=wo_hi[:, :, c], op0=ALU.mult,
                                                       op1=ALU.subtract).then_inc(lo_ready, 1)
                        for t in range(NTILE):
                            dve.wait_ge(z_ready, i * NTILE + t + 1)
                            dve.wait_ge(t_loaded[t % 2], (i * 2 + t // 2 + 1) * 32)
                            nc.vector.scalar_tensor_tensor(out=ya[t % 2][:], in0=pz[t][:], scalar=1.0 / WSCALE,
                                                           in1=ga[t % 2][:], op0=ALU.mult,
                                                           op1=ALU.mult).then_inc(ya_ready, 1)

            @block.tensor
            def _(pe):
                with pe.Fori(0, KD // 2) as ii:
                    for b in range(2):
                        i = ii * 2 + b
                        pe.wait_ge(lo_ready, i * 2 + 1)
                        for t in range(NTILE):
                            pe.wait_ge(ya_ready, i * NTILE)
                            n = 0
                            for k in range(KD):
                                c = slice(k * SEQ + t * TILE, k * SEQ + (t + 1) * TILE)
                                for w, m in ((w_hi, og_hi), (w_hi, og_lo), (w_lo, og_hi)):
                                    mm = nc.tensor.matmul(pz[t][:], w[b][:, k, :], m[:, c],
                                                          start=n == 0, stop=n == 3 * KD - 1)
                                    n += 1
                            mm.then_inc(z_ready, 1)

        with nc.Block() as block:
            @block.sync
            def _(sp):
                with sp.Fori(0, SEQ // P // 2) as ii:
                    for b in range(2):
                        w = ii * 2 + b
                        sp.wait_ge(stored[b], ii * 16)
                        sp.dma_start(xw[b][:], x[bass.ds(w * P, P), :]).then_inc(x_loaded[b], 16)

            @block.scalar
            def _(act):
                with act.Fori(0, SEQ // P // 2) as ii:
                    for b in range(2):
                        w = ii * 2 + b
                        act.wait_ge(y_ready, w * 2 + 2)
                        act.dma_start(out[bass.ds(w * P, P), :], xw[b][:]).then_inc(stored[b], 16)
                for b in range(2):
                    act.wait_ge(stored[b], SEQ // P // 2 * 16)

            @block.vector
            def _(dve):
                with dve.Fori(0, SEQ // P // 2) as ii:
                    for b in range(2):
                        w = ii * 2 + b
                        dve.wait_ge(x_loaded[b], (ii + 1) * 16)
                        for j in range(2):
                            dve.wait_ge(o_ready, w * 2 + j + 1)
                            c = slice(j * TILE, (j + 1) * TILE)
                            nc.vector.scalar_tensor_tensor(out=xw[b][:, c], in0=pz[2 * b + j][:],
                                                           scalar=1.0 / WSCALE, in1=xw[b][:, c], op0=ALU.mult,
                                                           op1=ALU.add).then_inc(y_ready, 1)

            @block.tensor
            def _(pe):
                with pe.Fori(0, SEQ // P // 2) as ii:
                    for b in range(2):
                        w = ii * 2 + b
                        for j in range(2):
                            pe.wait_ge(y_ready, ii * 4)
                            n = 0
                            for k in range(KD):
                                c = bass.ds(w * P, P)
                                for m, wo in ((m_hi, wo_hi), (m_hi, wo_lo), (m_lo, wo_hi)):
                                    mm = nc.tensor.matmul(pz[2 * b + j][:], m[:, k, c],
                                                          wo[:, k, j * TILE:(j + 1) * TILE],
                                                          start=n == 0, stop=n == 3 * KD - 1)
                                    n += 1
                            mm.then_inc(o_ready, 1)


def hybrid_layer(nc, x, meta, norm_g, w_in, lb_logits, r_norm_g, q_norm_g, k_norm_g, w_r, w_a, w_out, out):
    w_cols = w_in[0].rearrange("(k p) n -> p k n", p=P)
    x, w_r, w_a, w_out, out = x[0], w_r[0], w_a[0], w_out[0], out[0]

    def scratch(name, shape, dt):
        return nc.dram_tensor(name, shape, dt).ap()

    or_parts = scratch("or_parts", [2, P, RH * SEQ], F16)
    merged_r = scratch("merged_r", [P, KD * SEQ], F32)
    gate_a = scratch("gate_a", [P, KD * SEQ], F32)
    aq_parts = scratch("aq_parts", [2, P, AH * SEQ], F16)
    iq_parts = scratch("iq_parts", [2, P, IH // 2 * SEQ], F16)
    ag = scratch("ag", [P, AH * SEQ], F32)
    oa_parts = scratch("oa_parts", [2, P, AH * SEQ], F16)

    with ExitStack() as ctx:
        def sb(name, shape, dt):
            return ctx.enter_context(nc.sbuf_tensor(name, shape, dt))

        ident = sb("ident", [P, P], F32)
        with ExitStack() as keys_live:
            with nc.sbuf_tensor("ut_hi", [P, KD, T], F16) as ut_hi, nc.sbuf_tensor("ut_lo", [P, KD, T], F16) as ut_lo:
                normed_input(nc, x, meta, norm_g, ut_hi, ut_lo, ident)
                recurrence(nc, w_cols, lb_logits, r_norm_g, ut_hi, ut_lo, or_parts, ident)
                merge_recurrent(nc, w_cols, w_r, ut_hi, ut_lo, or_parts, merged_r, gate_a)

                def keyed(name, shape, dt):
                    return keys_live.enter_context(nc.sbuf_tensor(name, shape, dt, side="right"))
                kt_hi, kt_lo = keyed("kt_hi", [P, KVH, T], F16), keyed("kt_lo", [P, KVH, T], F16)
                v_all = keyed("v_all", [P, NW, KVH * P], F32)
                ik_hi, ik_lo = keyed("ik_hi", [P, T], F16), keyed("ik_lo", [ID, T], F16)
                iw_all = keyed("iw_all", [P, NW, IH], F32)
                keys_values(nc, w_cols, k_norm_g, ut_hi, ut_lo, kt_hi, kt_lo, v_all, ik_hi, ik_lo, iw_all)
                queries(nc, w_cols, q_norm_g, ut_hi, ut_lo, aq_parts, iq_parts, ag)
            attention(nc, aq_parts, iq_parts, ag, kt_hi, kt_lo, v_all, ik_hi, ik_lo, iw_all, oa_parts, ident)
        merge_and_project(nc, x, w_a, w_out, oa_parts, merged_r, gate_a, out)


_INS = ["x", "meta", "norm_g", "w_in", "lb_logits", "r_norm_g", "q_norm_g", "k_norm_g", "w_r", "w_a", "w_out"]


def kernel(**inputs):
    import numpy as np
    from concourse import bacc
    from concourse.bass_utils import run_bass_kernel_spmd

    nc = bacc.Bacc("TRN2", target_bir_lowering=False, num_devices=1)
    arrays, args = {}, []
    for name in _INS:
        a = np.ascontiguousarray(inputs[name])
        arrays[f"in_{name}"] = a
        args.append(nc.dram_tensor(f"in_{name}", a.shape, mybir.dt.from_np(a.dtype), kind="ExternalInput").ap())
    out = nc.dram_tensor("out0", (1, SEQ, D), F32, kind="ExternalOutput").ap()
    hybrid_layer(nc, *args, out)
    return run_bass_kernel_spmd(nc, [arrays], core_ids=[0]).results[0]["out0"]
```

```python
import concourse.bass as bass
from concourse import mybir
from contextlib import ExitStack

F32 = mybir.dt.float32
F16 = mybir.dt.float16
I16 = mybir.dt.int16
U16 = mybir.dt.uint16
I8 = mybir.dt.int8
ALU = mybir.AluOpType
ACT = mybir.ActivationFunctionType
AX = mybir.AxisListType

P = 128
D = 1024
KD = D // P
SEQ = 2048
META = 16
PAD = P - META
T = SEQ + P
NW = T // P
TILE = 512
WPT = TILE // P
NTILE = SEQ // TILE
RH = 8
AH, KVH, AG = 8, 2, 4
IH, ID = 8, 64
TOPK = 256
EPS = 1e-6
WSCALE = 64.0
C_RQ, C_RF, C_RI, C_RG = 0, 1024, 2048, 3072
C_AQ, C_AK, C_AV, C_AG = 4096, 5120, 5376, 5632
C_IQ, C_IK, C_IW = 6656, 7168, 7232
C_MR, C_MA = 7240, 8264


class Semaphores:

    def __init__(self, nc, ctx, prefix):
        self.nc, self.prefix, self.taken = nc, prefix, []
        ctx.callback(self.clear)

    def __call__(self, name):
        self.taken.append(self.nc.alloc_semaphore(self.prefix + name))
        return self.taken[-1]

    def two(self, name):
        return [self(f"{name}{b}") for b in range(2)]

    def clear(self):
        self.nc.clear_and_free_semaphores(self.taken)
        self.nc.all_engine_barrier()


def normed_input(nc, x, meta, norm_g, ut_hi, ut_lo, ident):
    with ExitStack() as ctx:
        def sb(name, shape, dt=F32):
            return ctx.enter_context(nc.sbuf_tensor(name, shape, dt))

        sem = Semaphores(nc, ctx, "n_")

        xw = [sb(f"xw{b}", [P, D]) for b in range(2)]
        xsq = sb("xsq", [P, D])
        xn = [sb(f"xn{b}", [P, D]) for b in range(2)]
        u32 = [sb(f"u32_{b}", [P, KD, P]) for b in range(2)]
        stat = sb("stat", [P, 2, 4])
        eps = sb("eps0", [P, 1])
        g = sb("g0", [P, KD])
        pt = [ctx.enter_context(nc.psum_tensor(f"pt{b}", [P, KD, P], F32)) for b in range(2)]
        meta_ready = sem("meta_ready")
        const_ready = sem("const_ready")
        g_loaded = sem("g_loaded")
        x_loaded = [sem(f"x_loaded{b}") for b in range(2)]
        ssq_ready = sem("ssq_ready")
        sd_ready = sem("sd_ready")
        rstd_ready = sem("rstd_ready")
        xn_ready = sem("xn_ready")
        xt_ready = sem("xt_ready")
        u32_ready = sem("u32_ready")
        hi_ready = sem("hi_ready")
        lo_ready = sem("lo_ready")

        def windows(eng, body):
            body(0, 0, 1, True)
            with eng.Fori(0, (NW - 1) // 2) as i:
                body(i * 2 + 1, 1, i + 1, False)
                body(i * 2 + 2, 0, i + 2, False)

        with nc.Block() as block:
            @block.sync
            def _(sp):
                sp.dma_start(g[:], norm_g.rearrange("o (k p) -> p (o k)", p=P),
                             allow_slow_non_contiguous=True).then_inc(g_loaded, 16)

                def load(n, b, visit, first):
                    if first:
                        sp.wait_ge(meta_ready, 1)
                        sp.dma_start(xw[b][PAD:P, :], meta).then_inc(x_loaded[b], 16)
                        return
                    sp.wait_ge(xn_ready, n - 1)
                    sp.dma_start(xw[b][:], x[bass.ds((n - 1) * P, P), :]).then_inc(x_loaded[b], 16)
                windows(sp, load)

            @block.gpsimd
            def _(pool):
                nc.gpsimd.memset(xw[0][:], 0.0).then_inc(meta_ready, 1)
                nc.gpsimd.memset(eps[:], EPS).then_inc(const_ready, 1)
                nc.gpsimd.memset(ident[:], 0.0).then_inc(const_ready, 1)
                pool.wait_ge(const_ready, 2)
                nc.gpsimd.affine_select(out=ident[:], in_=ident[:], compare_op=ALU.not_equal, fill=1.0,
                                        base=0, pattern=[[-1, P]], channel_multiplier=1).then_inc(const_ready, 1)

                def low(n, b, visit, first):
                    pool.wait_ge(hi_ready, n + 1)
                    t0 = 0 if first else n * P
                    nc.gpsimd.tensor_tensor(out=ut_lo[:, :, bass.ds(t0, P)], in0=u32[b][:],
                                            in1=ut_hi[:, :, bass.ds(t0, P)], op=ALU.subtract).then_inc(lo_ready, 1)
                windows(pool, low)

            @block.scalar
            def _(act):
                act.wait_ge(const_ready, 1)

                def norm(n, b, visit, first):
                    act.wait_ge(x_loaded[b], visit * 16)
                    nc.scalar.activation(xsq[:], xw[b][:], ACT.Square,
                                         accum_out=stat[:, b, 0:1]).then_inc(ssq_ready, 1)
                    act.wait_ge(ssq_ready, n + 1)
                    nc.scalar.activation(stat[:, b, 1:2], stat[:, b, 0:1], ACT.Sqrt,
                                         bias=eps[:], scale=1.0 / D).then_inc(sd_ready, 1)
                    act.wait_ge(u32_ready, n + 1)
                    t0 = 0 if first else n * P
                    nc.scalar.activation(ut_hi[:, :, bass.ds(t0, P)], u32[b][:], ACT.Copy).then_inc(hi_ready, 1)
                windows(act, norm)

            @block.vector
            def _(dve):
                dve.wait_ge(g_loaded, 16)

                def scale(n, b, visit, first):
                    dve.wait_ge(sd_ready, n + 1)
                    nc.vector.reciprocal(stat[:, b, 2:3], stat[:, b, 1:2]).then_inc(rstd_ready, 1)
                    dve.wait_ge(rstd_ready, n + 1)
                    if not first:
                        dve.wait_ge(xt_ready, n - 1)
                    nc.vector.tensor_scalar(xn[b][:], xw[b][:], stat[:, b, 2:3], None,
                                            ALU.mult).then_inc(xn_ready, 1)
                    dve.wait_ge(xt_ready, n + 1)
                    if not first:
                        dve.wait_ge(lo_ready, n - 1)
                    nc.vector.tensor_tensor(out=u32[b][:], in0=pt[b][:],
                                            in1=g[:, :, None].broadcast_to([P, KD, P]),
                                            op=ALU.mult).then_inc(u32_ready, 1)
                windows(dve, scale)

            @block.tensor
            def _(pe):
                pe.wait_ge(const_ready, 3)

                def turn(n, b, visit, first):
                    pe.wait_ge(xn_ready, n + 1)
                    if not first:
                        pe.wait_ge(u32_ready, n - 1)
                    for k in range(KD):
                        mm = nc.tensor.transpose(pt[b][:, k, :], xn[b][:, k * P:(k + 1) * P], ident[:])
                    mm.then_inc(xt_ready, 1)
                windows(pe, turn)


def recurrence(nc, w_cols, lb_logits, r_norm_g, ut_hi, ut_lo, og_parts, ident):
    STEPS = 1 + NTILE
    HPI = 2
    SPI = STEPS * HPI
    TPI = NTILE * HPI
    LEVELS = (128, 64, 32)
    LEAF = 16
    CLAMP = 80.0
    HALF = 0.5 / WSCALE
    QSCALE = P ** -0.5 * HALF
    with ExitStack() as ctx:
        def sb(name, shape, dt=F32):
            return ctx.enter_context(nc.sbuf_tensor(name, shape, dt))

        def two(name, shape, dt=F32):
            return [sb(f"{name}{b}", shape, dt) for b in range(2)]

        sem = Semaphores(nc, ctx, "r_")

        w_raw = [sb(f"w_raw{b}", [P, KD, P]) for b in range(2)]
        w_hi = [two(f"w_hi{s}_", [P, KD, P], F16) for s in range(4)]
        w_lo = [two(f"w_lo{s}_", [P, KD, P], F16) for s in range(4)]
        sig = sb("sig", [P, TILE])
        f_ = sb("f_", [P, TILE])
        lf = sb("lf", [P, TILE])
        q_ = two("q_", [P, TILE])
        k_ = sb("k_", [P, TILE])
        b_ = sb("b_", [P, TILE])
        gate = two("gate", [P, TILE])
        v_ = two("v_", [P, WPT, P])
        df = [sb(f"df{i}", [P, TILE]) for i in range(5)]
        ex = [sb(f"ex{i}", [P, TILE]) for i in range(7)]
        lv = [two(f"lv{i}_", [P, TILE]) for i in range(3)]
        lq, lk = two("lq", [P, TILE]), two("lk", [P, TILE])
        qe, ke = two("qe", [P, TILE]), two("ke", [P, TILE])
        eend = two("eend", [P, WPT])
        kt = sb("kt", [P, WPT, P])
        att = sb("att", [P, WPT, P])
        st = [sb(f"st{b}", [P, WPT, P]) for b in range(2)]
        sq = sb("sq", [P, TILE])
        rin = sb("rin", [P, TILE])
        on = sb("on", [P, TILE])
        og = sb("og", [P, TILE])
        oh, ol = two("oh", [P, TILE], F16), two("ol", [P, TILE], F16)
        restart = sb("restart", [P, TILE])
        mask = sb("mask", [P, 4, P], I8)
        mone = sb("mone", [P, P], I8)
        ones = sb("ones", [P, P])
        eps = sb("eps1", [P, 1])
        gq = sb("gq", [P, 1])
        lbl = sb("lbl", [P, 2, RH])
        lbd = sb("lbd", [P, RH])
        lb = sb("lb", [P, RH])
        omlb = sb("omlb", [P, RH])

        def bank(name, dt=F32):
            return ctx.enter_context(nc.psum_tensor("r" + name, [P, TILE], dt))

        pf, pq, pg, pv = bank("pf"), bank("pq"), bank("pg"), bank("pv")
        pa = [bank("pa0"), bank("pa1")]
        pk, po = bank("pk"), bank("po")

        w_loaded = [sem(f"w_loaded{s}") for s in range(4)]
        load_turn, copy_turn = sem("load_turn"), sem("copy_turn")
        whi_ready, wlo_ready = sem("whi_ready"), sem("wlo_ready")
        small_loaded, const_ready = sem("small_loaded"), sem("const_ready")
        lb_step, lb_ready = sem("lb_step"), sem("lb_ready")
        pf_ready, pq_ready, pg_ready, pv_ready = (sem(n) for n in ("pf_ready", "pq_ready", "pg_ready", "pv_ready"))
        sig_ready, q_ready, gate_ready, v_ready = (sem(n) for n in ("sig_ready", "q_ready", "gate_ready", "v_ready"))
        th_q_ready, th_g_ready = sem("th_q_ready"), sem("th_g_ready")
        f_ready, k_ready, lf_ready, b_ready = (sem(n) for n in ("f_ready", "k_ready", "lf_ready", "b_ready"))
        leaf_raw, df_ready, ex_ready, prod_ready = (sem(n) for n in ("leaf_raw", "df_ready", "ex_ready", "prod_ready"))
        pk_ready, kt_ready, u_ready, st_ready = (sem(n) for n in ("pk_ready", "kt_ready", "u_ready", "st_ready"))
        pa_ready, att_ready = sem("pa_ready"), sem("att_ready")
        o_ready, sq_ready, ms_ready = sem("o_ready"), sem("sq_ready"), sem("ms_ready")
        ln_ready, rin_ready = sem("ln_ready"), sem("rin_ready")
        o_stored = [sem(f"o_stored{b}") for b in range(2)]
        on_ready, og_ready, ohi_ready, olo_ready = (sem(n) for n in ("on_ready", "og_ready", "ohi_ready", "olo_ready"))

        class Step:

            def __init__(self, i, s):
                self.n = i * SPI + s
                self.head = i * HPI + s // STEPS
                self.full = s % STEPS > 0
                self.m = i * TPI + (s // STEPS * NTILE + max(0, s % STEPS - 1))
                self.hb = s // STEPS % 2
                self.b = s % 2
                self.tile = s % STEPS - 1
                self.t0 = P + TILE * self.tile if self.full else 0
                self.stores = self.head * NTILE + self.tile // 2 * 2
                self.wins = WPT if self.full else 1
                self.cols = self.wins * P

        def run(eng, body):
            last = RH // HPI - 1
            body(Step(0, 0), None)
            with eng.Fori(0, last) as i:
                for s in range(1, SPI + 1):
                    body(Step(i, s), Step(i, s - 1))
            for s in range(1, SPI):
                body(Step(last, s), Step(last, s - 1))
            body(None, Step(last, SPI - 1))

        def splits(x):
            return x.full and not (isinstance(x.head, int) and x.head == RH - 1)

        def level(ap, L, cols):
            return ap[:, 0:cols].rearrange("p (n l) -> p n l", l=L)

        with nc.Block() as block:
            @block.sync
            def _(sp):
                sp.dma_start(lbl[:], lb_logits.rearrange("r (h p) -> p r h", p=P),
                             allow_slow_non_contiguous=True).then_inc(small_loaded, 16)
                sp.dma_start(gq[:], r_norm_g.rearrange("o p -> p o"),
                             allow_slow_non_contiguous=True).then_inc(small_loaded, 16)
                def load(h, s):
                    c = (C_RF, C_RQ, C_RG, C_RI)[s]
                    sp.wait_ge(wlo_ready, h * 4 + s - 1)
                    sp.sem_inc(load_turn, 1)
                    sp.dma_start(w_raw[s % 2][:], w_cols[:, :, bass.ds(h * P + c, P)]).then_inc(w_loaded[s], 16)

                for s, c in enumerate((C_RF, C_RQ)):
                    sp.dma_start(w_raw[s][:], w_cols[:, :, c:c + P]).then_inc(w_loaded[s], 16)
                load(0, 2)
                load(0, 3)

                def store(h):
                    for j in range(NTILE):
                        sp.wait_ge(olo_ready, h * NTILE + j + 1)
                        for part, o in enumerate((oh, ol)):
                            sp.dma_start(og_parts[part, :, bass.ds(h * SEQ + j * TILE, TILE)],
                                         o[j % 2][:]).then_inc(o_stored[j % 2], 16)
                with sp.Fori(0, RH - 1) as h:
                    for s in range(4):
                        load(h + 1, s)
                    store(h)
                store(RH - 1)
                for b in range(2):
                    sp.wait_ge(o_stored[b], RH * NTILE * 16)

            @block.gpsimd
            def _(pool):
                nc.gpsimd.memset(restart[:], 1.0).then_inc(const_ready, 1)
                nc.gpsimd.memset(ones[:], 1.0 / P).then_inc(const_ready, 1)
                nc.gpsimd.memset(eps[:], EPS).then_inc(const_ready, 1)
                nc.gpsimd.memset(att[:], 0.0).then_inc(const_ready, 1)
                nc.gpsimd.memset(mone[:], 1).then_inc(const_ready, 1)
                nc.gpsimd.memset(mask[:], 0).then_inc(const_ready, 1)
                pool.wait_ge(const_ready, 6)
                nc.gpsimd.memset(restart[:].rearrange("p (w t) -> p w t", t=P)[:, :, 0], 0.0).then_inc(const_ready, 1)
                count = 7
                for j, L in enumerate(LEVELS):
                    H = L // 2
                    for blk in range(P // L):
                        sub = mask[:, j, blk * L + H:(blk + 1) * L]
                        nc.gpsimd.affine_select(out=sub, in_=mone[:, 0:H], compare_op=ALU.is_ge, fill=0.0,
                                                base=-blk * L, pattern=[[0, H]], channel_multiplier=1
                                                ).then_inc(const_ready, 1)
                        count += 1
                        pool.wait_ge(const_ready, count)
                        nc.gpsimd.affine_select(out=sub, in_=sub, compare_op=ALU.is_gt, fill=0.0,
                                                base=blk * L + H, pattern=[[0, H]], channel_multiplier=-1
                                                ).then_inc(const_ready, 1)
                        count += 1
                for blk in range(P // LEAF):
                    sub = mask[:, 3, blk * LEAF:(blk + 1) * LEAF]
                    nc.gpsimd.affine_select(out=sub, in_=mone[:, 0:LEAF], compare_op=ALU.is_ge, fill=0.0,
                                            base=-blk * LEAF, pattern=[[0, LEAF]], channel_multiplier=1
                                            ).then_inc(const_ready, 1)
                    count += 1
                    pool.wait_ge(const_ready, count)
                    nc.gpsimd.affine_select(out=sub, in_=sub, compare_op=ALU.is_ge, fill=0.0,
                                            base=blk * LEAF, pattern=[[1, LEAF]], channel_multiplier=-1
                                            ).then_inc(const_ready, 1)
                    count += 1
                assert count == CONSTS
                pool.wait_ge(const_ready, CONSTS)
                pool.sem_inc(prod_ready, 2)

                def products(x):
                    b, c = x.b, x.cols
                    pool.wait_ge(k_ready, x.n + 1)
                    pool.wait_ge(ex_ready, x.n + 1)
                    if x.full:
                        pool.wait_ge(q_ready, x.m + 1)
                        pool.wait_ge(o_ready, x.m - (x.tile > 0))
                        for j, L in enumerate(LEVELS):
                            H = L // 2
                            e, o = level(ex[j], L, c), level(lv[j][b], L, c)
                            nc.gpsimd.tensor_tensor(out=o[:, :, 0:H], in0=e[:, :, 0:H],
                                                    in1=level(k_, L, c)[:, :, 0:H], op=ALU.mult)
                            nc.gpsimd.tensor_tensor(out=o[:, :, H:L], in0=e[:, :, H:L],
                                                    in1=level(q_[b], L, c)[:, :, H:L], op=ALU.mult)
                        nc.gpsimd.tensor_tensor(out=lq[b][:], in0=ex[3][:], in1=q_[b][:], op=ALU.mult)
                        nc.gpsimd.tensor_tensor(out=lk[b][:], in0=ex[4][:], in1=k_[:], op=ALU.mult)
                        nc.gpsimd.tensor_tensor(out=qe[b][:], in0=ex[5][:], in1=q_[b][:], op=ALU.mult)
                    nc.gpsimd.tensor_tensor(out=ke[b][:, 0:c], in0=ex[6][:, 0:c], in1=k_[:, 0:c],
                                            op=ALU.mult).then_inc(prod_ready, 1)

                def out_low(x):
                    if x.full:
                        pool.wait_ge(ohi_ready, x.m + 1)
                        pool.wait_ge(o_stored[x.tile % 2], x.stores * 16)
                        nc.gpsimd.tensor_tensor(out=ol[x.tile % 2][:], in0=og[:], in1=oh[x.tile % 2][:],
                                                op=ALU.subtract).then_inc(olo_ready, 1)
                def body(x, y):
                    if x:
                        products(x)
                    if y:
                        out_low(y)
                run(pool, body)

            @block.scalar
            def _(act):
                act.wait_ge(const_ready, CONSTS)
                act.wait_ge(lb_step, 1)
                nc.scalar.activation(lb[:], lbd[:], ACT.Sigmoid).then_inc(lb_ready, 1)
                nc.scalar.activation(omlb[:], lbd[:], ACT.Sigmoid, scale=-1.0).then_inc(lb_ready, 1)
                act.wait_ge(small_loaded, 32)
                nc.scalar.activation(gq[:], gq[:], ACT.Copy, scale=QSCALE * HALF).then_inc(lb_ready, 1)

                def weights(h, s, hb):
                    act.wait_ge(w_loaded[s], (h + 1) * 16)
                    nc.scalar.activation(w_hi[s][hb][:], w_raw[s % 2][:], ACT.Copy,
                                         scale=WSCALE).then_inc(whi_ready, 1)

                def sigmoid(x):
                    c = x.cols
                    act.wait_ge(pf_ready, x.n + 1)
                    act.wait_ge(f_ready, x.n)
                    nc.scalar.activation(sig[:, 0:c], pf[:, 0:c], ACT.Sigmoid,
                                         scale=1.0 / WSCALE).then_inc(sig_ready, 1)

                def tanhs(x):
                    act.wait_ge(pq_ready, x.m + 1)
                    nc.scalar.activation(q_[x.b][:], pq[:], ACT.Tanh, scale=HALF).then_inc(th_q_ready, 1)
                    if splits(x):
                        weights(x.head + 1, x.tile, 1 - x.hb)
                    act.wait_ge(pg_ready, x.m + 1)
                    nc.scalar.activation(gate[x.b][:], pg[:], ACT.Tanh, scale=HALF).then_inc(th_g_ready, 1)

                def output(x):
                    act.wait_ge(o_ready, x.m + 1)
                    nc.scalar.activation(sq[:], po[:], ACT.Square, scale=QSCALE).then_inc(sq_ready, 1)
                    act.wait_ge(ms_ready, x.m + 1)
                    nc.scalar.activation(sq[:], pk[:], ACT.Ln, bias=eps[:]).then_inc(ln_ready, 1)
                    act.wait_ge(ln_ready, x.m + 1)
                    nc.scalar.activation(rin[:], sq[:], ACT.Exp, scale=-0.5).then_inc(rin_ready, 1)
                    act.wait_ge(og_ready, x.m + 1)
                    act.wait_ge(o_stored[x.tile % 2], x.stores * 16)
                    nc.scalar.activation(oh[x.tile % 2][:], og[:], ACT.Copy).then_inc(ohi_ready, 1)

                def decays(x):
                    c = x.cols
                    act.wait_ge(f_ready, x.n + 1)
                    nc.scalar.activation(lf[:, 0:c], f_[:, 0:c], ACT.Ln).then_inc(lf_ready, 1)
                    act.wait_ge(df_ready, x.n + 1)
                    act.wait_ge(prod_ready, x.n + 2)
                    if x.full:
                        for j, L in enumerate(LEVELS):
                            H = L // 2
                            d, e = level(df[j], L, c), level(ex[j], L, c)
                            nc.scalar.activation(e[:, :, 0:H], d[:, :, 0:H], ACT.Exp, scale=-1.0)
                            nc.scalar.activation(e[:, :, H:L], d[:, :, H:L], ACT.Exp)
                        nc.scalar.activation(ex[3][:], df[3][:], ACT.Exp)
                        nc.scalar.activation(ex[4][:], df[3][:], ACT.Exp, scale=-1.0)
                        nc.scalar.activation(ex[5][:], b_[:], ACT.Exp)
                        nc.scalar.activation(eend[x.b][:], b_[:].rearrange("p (w t) -> p w t", t=P)[:, :, P - 1],
                                             ACT.Exp)
                    nc.scalar.activation(ex[6][:, 0:c], df[4][:, 0:c], ACT.Exp, scale=-1.0).then_inc(ex_ready, 1)

                def body(x, y):
                    if x:
                        sigmoid(x)
                        decays(x)
                    if x and x.full:
                        tanhs(x)
                    if y and y.full:
                        output(y)

                for s in range(4):
                    weights(0, s, 0)
                run(act, body)

            @block.vector
            def _(dve):
                dve.wait_ge(const_ready, CONSTS)
                dve.wait_ge(small_loaded, 32)
                nc.vector.tensor_tensor(out=lbd[:], in0=lbl[:, 0, :], in1=lbl[:, 1, :],
                                        op=ALU.subtract).then_inc(lb_step, 1)
                dve.wait_ge(lb_ready, 3)

                def weights(h, s, hb):
                    dve.wait_ge(whi_ready, h * 4 + s + 1)
                    nc.vector.scalar_tensor_tensor(out=w_lo[s][hb][:], in0=w_raw[s % 2][:], scalar=WSCALE,
                                                   in1=w_hi[s][hb][:], op0=ALU.mult,
                                                   op1=ALU.subtract).then_inc(wlo_ready, 1)

                def forget(x):
                    c = x.cols
                    h = x.head
                    dve.wait_ge(sig_ready, x.n + 1)
                    dve.wait_ge(lf_ready, x.n)
                    nc.vector.tensor_scalar(f_[:, 0:c], sig[:, 0:c], omlb[:, bass.ds(h, 1)], lb[:, bass.ds(h, 1)],
                                            ALU.mult, ALU.add).then_inc(f_ready, 1)
                    dve.wait_ge(f_ready, x.n + 1)
                    dve.wait_ge(prod_ready, x.n + 2)
                    nc.vector.tensor_scalar(k_[:, 0:c], f_[:, 0:c], -1.0, 1.0, ALU.mult, ALU.add).then_inc(k_ready, 1)

                def differences(x):
                    c = x.cols
                    dve.wait_ge(lf_ready, x.n + 1)
                    nc.vector.tensor_tensor_scan(out=b_[:, 0:c], data0=restart[:, 0:c], data1=lf[:, 0:c],
                                                 initial=0.0, op0=ALU.mult, op1=ALU.add).then_inc(b_ready, 1)
                    dve.wait_ge(b_ready, x.n + 1)
                    if x.full:
                        a = level(b_, LEAF, c)[:, :, LEAF // 2 - 1:LEAF // 2].broadcast_to([P, c // LEAF, LEAF])
                        nc.vector.tensor_tensor(out=level(df[3], LEAF, c), in0=level(b_, LEAF, c), in1=a,
                                                op=ALU.subtract).then_inc(leaf_raw, 1)
                        for j, L in enumerate(LEVELS):
                            a = level(b_, L, c)[:, :, L // 2 - 1:L // 2].broadcast_to([P, c // L, L])
                            nc.vector.tensor_tensor(out=level(df[j], L, c), in0=level(b_, L, c), in1=a,
                                                    op=ALU.subtract)
                        dve.wait_ge(leaf_raw, x.m + 1)
                        nc.vector.tensor_scalar(df[3][:], df[3][:], CLAMP, -CLAMP, ALU.min, ALU.max)
                    a = level(b_, P, c)[:, :, P - 1:P].broadcast_to([P, c // P, P])
                    nc.vector.tensor_tensor(out=level(df[4], P, c), in0=level(b_, P, c), in1=a,
                                            op=ALU.subtract).then_inc(df_ready, 1)

                def gates(x):
                    dve.wait_ge(th_q_ready, x.m + 1)
                    nc.vector.scalar_tensor_tensor(out=q_[x.b][:], in0=q_[x.b][:], scalar=1.0, in1=pq[:],
                                                   op0=ALU.add, op1=ALU.mult).then_inc(q_ready, 1)
                    dve.wait_ge(th_g_ready, x.m + 1)
                    nc.vector.scalar_tensor_tensor(out=gate[x.b][:], in0=gate[x.b][:], scalar=1.0, in1=pg[:],
                                                   op0=ALU.add, op1=ALU.mult).then_inc(gate_ready, 1)

                def values(x):
                    c = x.cols
                    dve.wait_ge(pv_ready, x.n + 1)
                    nc.vector.tensor_scalar(v_[x.b][:, 0:x.wins, :], pv[:, 0:c].rearrange("p (w t) -> p w t", t=P),
                                            1.0 / WSCALE, None, ALU.mult).then_inc(v_ready, 1)

                def masked(x, j):
                    nc.vector.copy_predicated(att[:], mask[:, j:j + 1, :].broadcast_to([P, WPT, P]),
                                              pa[j % 2][:].rearrange("p (w t) -> p w t", t=P)
                                              ).then_inc(att_ready, 1)

                def keys(x):
                    dve.wait_ge(pk_ready, x.n + 1)
                    if x.full:
                        dve.wait_ge(pa_ready, x.m * 4 + 1)
                    nc.vector.tensor_copy(kt[:, 0:x.wins, :], pk[:, 0:x.cols].rearrange("p (w t) -> p w t", t=P)
                                          ).then_inc(kt_ready, 1)
                    if x.full:
                        masked(x, 0)

                def window(x):
                    b = x.b
                    if not x.full:
                        dve.wait_ge(u_ready, x.n + 1)
                        nc.vector.tensor_copy(st[1 - b][:, 0, :], po[:, 0:P]).then_inc(st_ready, 1)
                        return
                    dve.wait_ge(pa_ready, x.m * 4 + 2)
                    dve.wait_ge(att_ready, x.m * 4 + 1)
                    dve.sem_inc(copy_turn, 1)
                    masked(x, 1)
                    dve.wait_ge(u_ready, x.n + 1)
                    for w in range(WPT):
                        if w >= 2:
                            dve.wait_ge(pa_ready, x.m * 4 + w + 1)
                            dve.wait_ge(att_ready, x.m * 4 + w)
                        dve.wait_ge(st_ready, x.m * WPT + w + x.head + 1)
                        nxt = st[1 - b][:, 0, :] if w == WPT - 1 else st[b][:, w + 1, :]
                        nc.vector.scalar_tensor_tensor(out=nxt, in0=st[b][:, w, :], scalar=eend[b][:, w:w + 1],
                                                       in1=po[:, w * P:(w + 1) * P], op0=ALU.mult,
                                                       op1=ALU.add).then_inc(st_ready, 1)
                        if w >= 2:
                            masked(x, w)

                def output(x):
                    dve.wait_ge(rin_ready, x.m + 1)
                    nc.vector.scalar_tensor_tensor(out=on[:], in0=po[:], scalar=gq[:], in1=rin[:],
                                                   op0=ALU.mult, op1=ALU.mult).then_inc(on_ready, 1)
                    dve.wait_ge(on_ready, x.m + 1)
                    dve.wait_ge(gate_ready, x.m + 1)
                    dve.wait_ge(olo_ready, x.m)
                    nc.vector.tensor_tensor(out=og[:], in0=on[:], in1=gate[x.b][:], op=ALU.mult).then_inc(og_ready, 1)

                def body(x, y):
                    if x:
                        forget(x)
                    if y:
                        keys(y)
                    if x:
                        differences(x)
                    if y:
                        window(y)
                    if x and splits(x):
                        weights(x.head + 1, x.tile, 1 - x.hb)
                    if x and x.full:
                        gates(x)
                    if x:
                        values(x)
                    if y and y.full:
                        output(y)

                for s in range(4):
                    weights(0, s, 0)
                run(dve, body)

            @block.tensor
            def _(pe):
                pe.wait_ge(const_ready, CONSTS)

                def project(out, s, x):
                    n = 0
                    for k in range(KD):
                        u = slice(x.t0, x.t0 + x.cols)
                        for w, m in ((w_hi, ut_hi), (w_hi, ut_lo), (w_lo, ut_hi)):
                            mm = nc.tensor.matmul(out[:, 0:x.cols], w[s][x.hb][:, k, :], m[:, k, u],
                                                  start=n == 0, stop=n == 3 * KD - 1)
                            n += 1
                    return mm

                def values(x):
                    pe.wait_ge(v_ready, x.n)
                    for w in range(x.wins):
                        n = 0
                        for k in range(KD):
                            u = slice(x.t0 + w * P, x.t0 + (w + 1) * P)
                            for m, wt in ((ut_hi, w_hi), (ut_hi, w_lo), (ut_lo, w_hi)):
                                mm = nc.tensor.matmul(pv[:, w * P:(w + 1) * P], m[:, k, u], wt[3][x.hb][:, k, :],
                                                      start=n == 0, stop=n == 3 * KD - 1)
                                n += 1
                    mm.then_inc(pv_ready, 1)

                def turned_keys(x):
                    pe.wait_ge(prod_ready, x.n + 3)
                    pe.wait_ge(ln_ready, x.m)
                    for w in range(x.wins):
                        c = slice(w * P, (w + 1) * P)
                        mm = nc.tensor.transpose(pk[:, c], ke[x.b][:, c], ident[:])
                    mm.then_inc(pk_ready, 1)

                def scores(x, j):
                    pe.wait_ge(att_ready, x.m * 4 + max(0, j - 1))
                    s_part, t_part = (lv[j][x.b], lv[j][x.b]) if j < 3 else (lk[x.b], lq[x.b])
                    for w in range(WPT):
                        c = slice(w * P, (w + 1) * P)
                        mm = nc.tensor.matmul(pa[j % 2][:, c], s_part[:, c], t_part[:, c],
                                              start=True, stop=True)
                    mm.then_inc(pa_ready, 1)

                def key_values(x):
                    pe.wait_ge(kt_ready, x.n + 1)
                    pe.wait_ge(v_ready, x.n + 1)
                    pe.wait_ge(on_ready, x.m)
                    for w in range(x.wins):
                        mm = nc.tensor.matmul(po[:, w * P:(w + 1) * P], kt[:, w, :], v_[x.b][:, w, :],
                                              start=True, stop=True)
                    mm.then_inc(u_ready, 1)

                def outputs(x):
                    b = x.b
                    pe.wait_ge(att_ready, (x.m + 1) * 4)
                    pe.wait_ge(st_ready, (x.m + 1) * WPT + x.head + 1)
                    for w in range(WPT):
                        c = slice(w * P, (w + 1) * P)
                        nc.tensor.matmul(po[:, c], st[b][:, w, :], qe[b][:, c], start=True, stop=False)
                        mm = nc.tensor.matmul(po[:, c], v_[b][:, w, :], att[:, w, :], start=False, stop=True)
                    mm.then_inc(o_ready, 1)

                def mean_squares(x):
                    pe.wait_ge(sq_ready, x.m + 1)
                    nc.tensor.matmul(pk[:], ones[:], sq[:], start=True, stop=True).then_inc(ms_ready, 1)

                def body(x, y):
                    tile = y and y.full
                    if x:
                        if not x.full:
                            pe.wait_ge(wlo_ready, (x.head + 1) * 4)
                        pe.wait_ge(sig_ready, x.n)
                        project(pf, 0, x).then_inc(pf_ready, 1)
                    if y:
                        turned_keys(y)
                    if tile:
                        scores(y, 0)
                        scores(y, 1)
                    if x and x.full:
                        pe.wait_ge(q_ready, x.m)
                        project(pq, 1, x).then_inc(pq_ready, 1)
                    if y:
                        key_values(y)
                    if tile:
                        scores(y, 2)
                        scores(y, 3)
                    if x and x.full:
                        pe.wait_ge(gate_ready, x.m)
                        project(pg, 2, x).then_inc(pg_ready, 1)
                    if tile:
                        outputs(y)
                    if x:
                        values(x)
                    if tile:
                        mean_squares(y)
                run(pe, body)


CONSTS = 7 + 2 * sum(P // L for L in (128, 64, 32)) + 2 * (P // 16)


def keys_values(nc, w_cols, k_norm_g, ut_hi, ut_lo, kt_hi, kt_lo, v_all, ik_hi, ik_lo, iw_all):
    TILES = [(0, P)] + [(P + j * TILE, TILE) for j in range(NTILE)]
    IW_SCALE = IH ** -0.5 * ID ** -0.5
    with ExitStack() as ctx:
        def sb(name, shape, dt=F32):
            return ctx.enter_context(nc.sbuf_tensor("kv_" + name, shape, dt))

        sem = Semaphores(nc, ctx, "kv_")

        slices = 5
        w_raw = [sb(f"w_raw{b}", [P, KD, P]) for b in range(slices)]
        w_hi = [sb(f"w_hi{b}", [P, KD, P], F16) for b in range(3)]
        w_lo = [sb(f"w_lo{b}", [P, KD, P], F16) for b in range(3)]
        wv_hi, wv_lo = sb("wv_hi", [P, KD, KVH * P], F16), sb("wv_lo", [P, KD, KVH * P], F16)
        wi_raw = sb("wi_raw", [P, KD, IH])
        wi_hi, wi_lo = sb("wi_hi", [P, KD, IH], F16), sb("wi_lo", [P, KD, IH], F16)
        gk = sb("gk", [P, 1])
        gks = sb("gks", [P, 1])
        eps = sb("eps", [P, 1])
        ones = sb("ones", [P, P])
        sq = sb("sq", [P, TILE])
        lnm = sb("lnm", [P, TILE])
        rin = sb("rin", [P, TILE])
        kn = sb("kn", [P, TILE])
        pz = [ctx.enter_context(nc.psum_tensor(f"kv_pz{b}", [P, TILE], F32)) for b in range(2)]
        pm = ctx.enter_context(nc.psum_tensor("kv_pm", [P, TILE], F32))
        pv = [ctx.enter_context(nc.psum_tensor(f"kv_pv{b}", [P, TILE], F32)) for b in range(2)]

        w_loaded = sem("w_loaded")
        hi_ready, lo_ready = sem("hi_ready"), sem("lo_ready")
        const_ready, gks_ready = sem("const_ready"), sem("gks_ready")
        z_ready, sq_ready, ms_ready, ln_ready, rin_ready = (sem(n) for n in ("z_ready", "sq_ready", "ms_ready", "ln_ready", "rin_ready"))
        kn_ready, khi_ready, klo_ready = (sem(n) for n in ("kn_ready", "khi_ready", "klo_ready"))
        ihi_ready, ilo_ready = sem("ihi_ready"), sem("ilo_ready")
        v_ready, vcopy_ready = sem("v_ready"), sem("vcopy_ready")
        NK = KVH * len(TILES)
        LOADS = slices + 3

        with nc.Block() as block:
            @block.sync
            def _(sp):
                for s in range(KVH):
                    sp.dma_start(w_raw[s][:], w_cols[:, :, C_AK + s * P:C_AK + (s + 1) * P]).then_inc(w_loaded, 16)
                for half in range(2):
                    sp.dma_start(w_raw[2][:, :, half * ID:(half + 1) * ID],
                                 w_cols[:, :, C_IK:C_IK + ID]).then_inc(w_loaded, 16)
                for s in range(KVH):
                    sp.dma_start(w_raw[3 + s][:], w_cols[:, :, C_AV + s * P:C_AV + (s + 1) * P]).then_inc(w_loaded, 16)
                sp.dma_start(wi_raw[:], w_cols[:, :, C_IW:C_IW + IH]).then_inc(w_loaded, 16)
                sp.dma_start(gk[:], k_norm_g.rearrange("o p -> p o"),
                             allow_slow_non_contiguous=True).then_inc(w_loaded, 16)

            def parts():
                for s in range(3):
                    yield w_raw[s][:], w_hi[s][:], w_lo[s][:]
                for s in range(KVH):
                    c = slice(s * P, (s + 1) * P)
                    yield w_raw[3 + s][:], wv_hi[:, :, c], wv_lo[:, :, c]
                yield wi_raw[:], wi_hi[:], wi_lo[:]

            @block.gpsimd
            def _(pool):
                nc.gpsimd.memset(eps[:], EPS).then_inc(const_ready, 1)
                nc.gpsimd.memset(ones[:], 1.0 / P).then_inc(const_ready, 1)
                for n in range(NK):
                    h, (t0, c) = n // len(TILES), TILES[n % len(TILES)]
                    pool.wait_ge(khi_ready, n + 1)
                    nc.gpsimd.tensor_tensor(out=kt_lo[:, h, t0:t0 + c], in0=kn[:, 0:c],
                                            in1=kt_hi[:, h, t0:t0 + c], op=ALU.subtract).then_inc(klo_ready, 1)

            @block.scalar
            def _(act):
                act.wait_ge(const_ready, 2)
                act.wait_ge(w_loaded, LOADS * 16)
                for raw, hi, _ in parts():
                    nc.scalar.activation(hi, raw, ACT.Copy, scale=WSCALE).then_inc(hi_ready, 1)
                nc.scalar.activation(gks[:], gk[:], ACT.Copy, scale=1.0 / WSCALE).then_inc(gks_ready, 1)
                for n in range(NK):
                    h, (t0, c) = n // len(TILES), TILES[n % len(TILES)]
                    act.wait_ge(z_ready, n + 1)
                    nc.scalar.activation(sq[:, 0:c], pz[n % 2][:, 0:c], ACT.Square,
                                         scale=1.0 / WSCALE).then_inc(sq_ready, 1)
                    act.wait_ge(ms_ready, n + 1)
                    nc.scalar.activation(lnm[:, 0:c], pm[:, 0:c], ACT.Ln, bias=eps[:]).then_inc(ln_ready, 1)
                    act.wait_ge(ln_ready, n + 1)
                    nc.scalar.activation(rin[:, 0:c], lnm[:, 0:c], ACT.Exp, scale=-0.5).then_inc(rin_ready, 1)
                    act.wait_ge(kn_ready, n + 1)
                    nc.scalar.activation(kt_hi[:, h, t0:t0 + c], kn[:, 0:c], ACT.Copy).then_inc(khi_ready, 1)
                for j, (t0, c) in enumerate(TILES):
                    act.wait_ge(z_ready, NK + j + 1)
                    nc.scalar.activation(ik_hi[:, t0:t0 + c], pz[(NK + j) % 2][:, 0:c], ACT.Copy,
                                         scale=1.0 / WSCALE).then_inc(ihi_ready, 1)

            @block.vector
            def _(dve):
                for n, (raw, hi, lo) in enumerate(parts()):
                    dve.wait_ge(hi_ready, n + 1)
                    nc.vector.scalar_tensor_tensor(out=lo, in0=raw, scalar=WSCALE, in1=hi, op0=ALU.mult,
                                                   op1=ALU.subtract).then_inc(lo_ready, 1)
                dve.wait_ge(gks_ready, 1)
                for n in range(NK):
                    c = TILES[n % len(TILES)][1]
                    dve.wait_ge(rin_ready, n + 1)
                    dve.wait_ge(klo_ready, n)
                    nc.vector.scalar_tensor_tensor(out=kn[:, 0:c], in0=pz[n % 2][:, 0:c], scalar=gks[:],
                                                   in1=rin[:, 0:c], op0=ALU.mult,
                                                   op1=ALU.mult).then_inc(kn_ready, 1)
                for j, (t0, c) in enumerate(TILES):
                    dve.wait_ge(ihi_ready, j + 1)
                    nc.vector.scalar_tensor_tensor(out=ik_lo[:, t0:t0 + c], in0=pz[(NK + j) % 2][0:ID, 0:c],
                                                   scalar=1.0 / WSCALE, in1=ik_hi[0:ID, t0:t0 + c],
                                                   op0=ALU.mult, op1=ALU.subtract).then_inc(ilo_ready, 1)
                for w in range(NW):
                    dve.wait_ge(v_ready, w + 1)
                    nc.vector.tensor_scalar(v_all[:, w, :], pv[w % 2][:, 0:KVH * P], 1.0 / WSCALE, None, ALU.mult)
                    nc.vector.tensor_scalar(iw_all[:, w, :], pv[w % 2][:, KVH * P:KVH * P + IH],
                                            IW_SCALE / WSCALE, None, ALU.mult).then_inc(vcopy_ready, 1)

            @block.tensor
            def _(pe):
                def project(out, hi, lo, t0, c):
                    n = 0
                    for k in range(KD):
                        for w, m in ((hi, ut_hi), (hi, ut_lo), (lo, ut_hi)):
                            mm = nc.tensor.matmul(out[:, 0:c], w[:, k, :], m[:, k, t0:t0 + c],
                                                  start=n == 0, stop=n == 3 * KD - 1)
                            n += 1
                    return mm

                pe.wait_ge(const_ready, 2)
                pe.wait_ge(lo_ready, 6)
                for n in range(NK + len(TILES)):
                    h, (t0, c) = n // len(TILES), TILES[n % len(TILES)]
                    if 2 <= n < NK + 2:
                        pe.wait_ge(kn_ready, n - 1)
                    if n >= NK + 2:
                        pe.wait_ge(ilo_ready, n - NK - 1)
                    project(pz[n % 2], w_hi[h], w_lo[h], t0, c).then_inc(z_ready, 1)
                    if 1 <= n <= NK:
                        c = TILES[(n - 1) % len(TILES)][1]
                        pe.wait_ge(sq_ready, n)
                        nc.tensor.matmul(pm[:, 0:c], ones[:], sq[:, 0:c], start=True, stop=True).then_inc(ms_ready, 1)
                for w in range(NW):
                    if w >= 2:
                        pe.wait_ge(vcopy_ready, w - 1)
                    for o, hi, lo in ((pv[w % 2][:, 0:KVH * P], wv_hi, wv_lo),
                                      (pv[w % 2][:, KVH * P:KVH * P + IH], wi_hi, wi_lo)):
                        n = 0
                        for k in range(KD):
                            for m, wt in ((ut_hi, hi), (ut_hi, lo), (ut_lo, hi)):
                                mm = nc.tensor.matmul(o, m[:, k, w * P:(w + 1) * P], wt[:, k, :],
                                                      start=n == 0, stop=n == 3 * KD - 1)
                                n += 1
                    mm.then_inc(v_ready, 1)


def queries(nc, w_cols, q_norm_g, ut_hi, ut_lo, aq_parts, iq_parts, ag):
    ITER = 4
    HPI = AH // ITER
    items = [(kind, h, t) for h in range(HPI) for t in range(NTILE) for kind in "qg"]
    items += [("i", 0, t) for t in range(NTILE)]
    NI = len(items)
    QPI = HPI * NTILE
    slot = {("q", 0): 0, ("g", 0): 1, ("q", 1): 2, ("g", 1): 3, ("i", 0): 4}
    with ExitStack() as ctx:
        def sb(name, shape, dt=F32):
            return ctx.enter_context(nc.sbuf_tensor("q_" + name, shape, dt))

        def two(name, shape, dt=F32):
            return [sb(f"{name}{b}", shape, dt) for b in range(2)]

        sem = Semaphores(nc, ctx, "q_")

        w_raw = two("w_raw", [P, KD, P])
        w_hi = [sb(f"w_hi{b}", [P, KD, P], F16) for b in range(5)]
        w_lo = [sb(f"w_lo{b}", [P, KD, P], F16) for b in range(5)]
        gq = sb("gq", [P, 1])
        gqs = sb("gqs", [P, AH])
        eps = sb("eps", [P, 1])
        ones = sb("ones", [P, P])
        sq, lnm, rin, qn = two("sq", [P, TILE]), sb("lnm", [P, TILE]), two("rin", [P, TILE]), two("qn", [P, TILE])
        qh, ql = two("qh", [P, TILE], F16), two("ql", [P, TILE], F16)
        ih, il = two("ih", [P, TILE], F16), two("il", [P, TILE], F16)
        gs = two("gs", [P, TILE])
        pz = [ctx.enter_context(nc.psum_tensor(f"q_pz{b}", [P, TILE], F32)) for b in range(4)]
        pm = [ctx.enter_context(nc.psum_tensor(f"q_pm{b}", [P, TILE], F32)) for b in range(2)]

        g_loaded, w_loaded = sem("g_loaded"), sem.two("w_loaded")
        hi_ready, lo_ready, const_ready, gqs_ready = (sem(n) for n in ("hi_ready", "lo_ready", "const_ready", "gqs_ready"))
        z_ready, sq_ready, ms_ready, ln_ready, rin_ready = (sem(n) for n in ("z_ready", "sq_ready", "ms_ready", "ln_ready", "rin_ready"))
        qn_ready, qhi_ready, qlo_ready = (sem(n) for n in ("qn_ready", "qhi_ready", "qlo_ready"))
        gs_ready, ihi_ready, ilo_ready = (sem(n) for n in ("gs_ready", "ihi_ready", "ilo_ready"))
        store_turn = sem("store_turn")
        q_stored, g_stored, i_stored = (sem.two(n) for n in ("q_stored", "g_stored", "i_stored"))

        class Item:

            def __init__(self, i, s):
                self.kind, self.h, self.t = items[s]
                self.s, self.n = s, i * NI + s
                before = sum(1 for k, _, _ in items[:s] if k == self.kind)
                per = sum(1 for k, _, _ in items if k == self.kind)
                self.m = i * per + before
                self.b = before % 2
                self.uses = i * (per // 2) + before // 2
                self.head = i * HPI + self.h
                self.pair = i
                self.t0 = P + self.t * TILE

        BEFORE = [0, 1, 2, 3]
        INSIDE = {2: [(0, 4)], 9: [(1, 0), (1, 1)], 17: [(1, 2), (1, 3)]}
        SPLITS = 5

        def column(i, sl):
            return {0: C_AQ + i * HPI * P, 1: C_AG + i * HPI * P, 2: C_AQ + i * HPI * P + P,
                    3: C_AG + i * HPI * P + P, 4: C_IQ + i * P}[sl]

        with nc.Block() as block:
            @block.sync
            def _(sp):
                sp.dma_start(gq[:], q_norm_g.rearrange("o p -> p o"),
                             allow_slow_non_contiguous=True).then_inc(g_loaded, 16)
                for n, sl in enumerate(BEFORE):
                    if n >= 2:
                        sp.wait_ge(lo_ready, n - 1)
                    sp.dma_start(w_raw[n % 2][:], w_cols[:, :, column(0, sl):column(0, sl) + P]
                                 ).then_inc(w_loaded[n % 2], 16)
                with sp.Fori(0, ITER // 2) as ii:
                    for half in range(2):
                        i = ii * 2 + half
                        at = 0
                        for s in range(NI):
                            for ahead, sl in INSIDE.get({0: 2, 5: 9, 13: 17}.get(s), ()):
                                b = (half * SPLITS + at) % 2
                                sp.wait_ge(lo_ready, i * SPLITS + at + 3)
                                sp.dma_start(w_raw[b][:], w_cols[:, :, bass.ds(column(i + ahead, sl), P)]
                                             ).then_inc(w_loaded[b], 16)
                                at += 1
                            x = Item(i, s)
                            if x.kind == "q":
                                sp.wait_ge(qlo_ready, x.m + 1)
                                for part, o in enumerate((qh, ql)):
                                    sp.dma_start(aq_parts[part, :, bass.ds(x.head * SEQ + x.t * TILE, TILE)],
                                                 o[x.b][:]).then_inc(q_stored[x.b], 16)
                            elif x.kind == "g":
                                sp.wait_ge(gs_ready, x.m + 1)
                                sp.sem_inc(store_turn, 1)
                                sp.dma_start(ag[:, bass.ds(x.head * SEQ + x.t * TILE, TILE)],
                                             gs[x.b][:]).then_inc(g_stored[x.b], 16)
                            else:
                                sp.wait_ge(ilo_ready, x.m + 1)
                                for part, o in enumerate((ih, il)):
                                    sp.dma_start(iq_parts[part, :, bass.ds(x.pair * SEQ + x.t * TILE, TILE)],
                                                 o[x.b][:]).then_inc(i_stored[x.b], 16)
                for b in range(2):
                    sp.wait_ge(q_stored[b], ITER * QPI * 16)
                    sp.wait_ge(g_stored[b], ITER * QPI // 2 * 16)
                    sp.wait_ge(i_stored[b], ITER * NTILE * 16)

            @block.gpsimd
            def _(pool):
                nc.gpsimd.memset(eps[:], EPS).then_inc(const_ready, 1)
                nc.gpsimd.memset(ones[:], 1.0 / P).then_inc(const_ready, 1)
                with pool.Fori(0, ITER) as i:
                    for s in range(NI):
                        x = Item(i, s)
                        if x.kind == "q":
                            pool.wait_ge(qhi_ready, x.m + 1)
                            pool.wait_ge(q_stored[x.b], x.uses * 32)
                            nc.gpsimd.tensor_tensor(out=ql[x.b][:], in0=qn[x.b][:], in1=qh[x.b][:],
                                                    op=ALU.subtract).then_inc(qlo_ready, 1)

            def split_positions():
                at = 0
                for s in sorted(INSIDE):
                    for _, sl in INSIDE[s]:
                        yield s, at, sl, {4: 0, 0: 8, 1: 8, 2: 16, 3: 16}[sl]
                        at += 1

            @block.scalar
            def _(act):
                act.wait_ge(const_ready, 2)
                act.wait_ge(g_loaded, 16)
                for h in range(AH):
                    nc.scalar.activation(gqs[:, h:h + 1], gq[:], ACT.Copy,
                                         scale=P ** -0.5 * 2.0 ** (h + 1) / WSCALE).then_inc(gqs_ready, 1)

                def split(sl, b, loads, done):
                    act.wait_ge(w_loaded[b], loads)
                    if done is not None:
                        act.wait_ge(z_ready, done)
                    nc.scalar.activation(w_hi[sl][:], w_raw[b][:], ACT.Copy, scale=WSCALE).then_inc(hi_ready, 1)

                def norm_tail(x):
                    act.wait_ge(ms_ready, x.m + 1)
                    act.wait_ge(rin_ready, x.m)
                    nc.scalar.activation(lnm[:], pm[x.b][:], ACT.Ln, bias=eps[:]).then_inc(ln_ready, 1)
                    act.wait_ge(ln_ready, x.m + 1)
                    nc.scalar.activation(rin[x.b][:], lnm[:], ACT.Exp, scale=-0.5).then_inc(rin_ready, 1)
                    act.wait_ge(qn_ready, x.m + 1)
                    act.wait_ge(q_stored[x.b], x.uses * 32)
                    nc.scalar.activation(qh[x.b][:], qn[x.b][:], ACT.Copy).then_inc(qhi_ready, 1)

                for n, sl in enumerate(BEFORE):
                    split(sl, n % 2, (n // 2 + 1) * 16, None)
                with act.Fori(0, ITER // 2) as ii:
                    for half in range(2):
                        i = ii * 2 + half
                        for s in range(NI):
                            for s_, at, sl, done in split_positions():
                                if s_ == s:
                                    k = half * SPLITS + at
                                    split(sl, k % 2, (2 + ii * SPLITS + k // 2 + 1) * 16, i * NI + done)
                            x = Item(i, s)
                            act.wait_ge(z_ready, x.n + 1)
                            if x.kind == "q":
                                nc.scalar.activation(sq[x.b][:], pz[s % 4][:], ACT.Square,
                                                     scale=1.0 / WSCALE).then_inc(sq_ready, 1)
                            elif x.kind == "g":
                                act.wait_ge(g_stored[x.b], x.uses * 16)
                                nc.scalar.activation(gs[x.b][:], pz[s % 4][:], ACT.Silu,
                                                     scale=1.0 / WSCALE).then_inc(gs_ready, 1)
                                norm_tail(Item(i, s - 1))
                            else:
                                act.wait_ge(i_stored[x.b], x.uses * 32)
                                nc.scalar.activation(ih[x.b][:], pz[s % 4][:], ACT.Copy,
                                                     scale=1.0 / WSCALE).then_inc(ihi_ready, 1)

            @block.vector
            def _(dve):
                def split(sl, b, count):
                    dve.wait_ge(hi_ready, count + 1)
                    nc.vector.scalar_tensor_tensor(out=w_lo[sl][:], in0=w_raw[b][:], scalar=WSCALE,
                                                   in1=w_hi[sl][:], op0=ALU.mult,
                                                   op1=ALU.subtract).then_inc(lo_ready, 1)

                for n, sl in enumerate(BEFORE):
                    split(sl, n % 2, n)
                dve.wait_ge(gqs_ready, AH)
                with dve.Fori(0, ITER // 2) as ii:
                    for half in range(2):
                        i = ii * 2 + half
                        for s in range(NI):
                            for s_, at, sl, done in split_positions():
                                if s_ == s:
                                    split(sl, (half * SPLITS + at) % 2, i * SPLITS + at + 4)
                            x = Item(i, s)
                            if x.kind == "g":
                                y = Item(i, s - 1)
                                dve.wait_ge(rin_ready, y.m + 1)
                                nc.vector.scalar_tensor_tensor(
                                    out=qn[y.b][:], in0=pz[(s - 1) % 4][:], scalar=gqs[:, bass.ds(y.head, 1)],
                                    in1=rin[y.b][:], op0=ALU.mult, op1=ALU.mult).then_inc(qn_ready, 1)
                            elif x.kind == "i":
                                dve.wait_ge(ihi_ready, x.m + 1)
                                nc.vector.scalar_tensor_tensor(
                                    out=il[x.b][:], in0=pz[s % 4][:], scalar=1.0 / WSCALE, in1=ih[x.b][:],
                                    op0=ALU.mult, op1=ALU.subtract).then_inc(ilo_ready, 1)

            @block.tensor
            def _(pe):
                pe.wait_ge(const_ready, 2)
                used = {"q": qn_ready, "g": gs_ready, "i": ilo_ready}
                with pe.Fori(0, ITER) as i:
                    for s in range(NI):
                        x = Item(i, s)
                        need = {0: i * SPLITS + 2, 8: i * SPLITS + 4, 16: i * SPLITS + 5}
                        if s in need:
                            pe.wait_ge(lo_ready, need[s])
                        if s == 0:
                            pe.wait_ge(ilo_ready, i * NTILE)
                        if s >= 4:
                            y = Item(i, s - 4)
                            pe.wait_ge(used[y.kind], y.m + 1)
                        n = 0
                        sl = slot[x.kind, x.h]
                        for k in range(KD):
                            for w, m in ((w_hi, ut_hi), (w_hi, ut_lo), (w_lo, ut_hi)):
                                mm = nc.tensor.matmul(pz[s % 4][:], w[sl][:, k, :], m[:, k, x.t0:x.t0 + TILE],
                                                      start=n == 0, stop=n == 3 * KD - 1)
                                n += 1
                        mm.then_inc(z_ready, 1)
                        if x.kind == "g":
                            y = Item(i, s - 1)
                            pe.wait_ge(sq_ready, y.m + 1)
                            nc.tensor.matmul(pm[y.b][:], ones[:], sq[y.b][:], start=True,
                                             stop=True).then_inc(ms_ready, 1)


def attention(nc, aq_parts, iq_parts, ag, kt_hi, kt_lo, v_all, ik_hi, ik_lo, iw_all, oa_parts, ident):
    NB = SEQ // P
    NEG = -1.0e30
    LOWEST = -3.0e38

    def keys(n):
        return (n + 1) * P

    def tiles(n):
        return [(max(c, PAD), min(c + TILE, keys(n))) for c in range(0, keys(n), TILE)]

    attended = [(1,)] + [tuple(m for m in (n, n + 1) if m <= NB) for n in range(2, NB + 1, 2)]
    STEPS = [(a, s) for a, s in zip(attended, attended[1:] + [()])]

    def dotted_before(n):
        return sum(AH * len(tiles(m)) for m in range(1, n))

    def row_of_set(n):
        mates = next(a for a in attended if n in a)
        before = sum(IH * len(tiles(m)) for m in range(2, mates[0]))
        return before + sum(len(tiles(m)) for m in mates if m < n), sum(len(tiles(m)) for m in mates)

    def scored_through(searched):
        return sum(IH * len(tiles(m)) for m in range(2, searched[-1] + 1))

    def split(n):
        return PAD + (keys(n) - PAD) * 5 // 8

    UPPER_BITS, LOWER_BITS = range(14, -1, -1), range(15, -1, -1)
    CANDS = len(UPPER_BITS) + len(LOWER_BITS) + 2
    PARTS = len(UPPER_BITS) + len(LOWER_BITS)

    def set_of(n):
        return n // 2 - 1

    def products_before(n):
        return sum(KVH * (m + 1) for m in range(1, n))

    def turned_before(n):
        return sum(KVH * (m + 2) for m in range(1, n))

    with ExitStack() as ctx:
        def sb(name, shape, dt=F32):
            return ctx.enter_context(nc.sbuf_tensor("a_" + name, shape, dt))

        def two(name, shape, dt=F32):
            return [sb(f"{name}{b}", shape, dt) for b in range(2)]

        sem = Semaphores(nc, ctx, "a_")

        def bank(name):
            return ctx.enter_context(nc.psum_tensor("a_" + name, [P, TILE], F32))

        q_hi, q_lo = two("q_hi", [P, AH, P], F16), two("q_lo", [P, AH, P], F16)
        iq = two("iq", [P, 2, IH // 2, P], F16)
        gate = two("gate", [P, AH, P])
        relu = [sb(f"relu{b}", [P, TILE]) for b in range(4)]
        score = two("score", [P, T])
        agree = two("agree", [P, T], I8)
        low = two("low", [P, T])
        junk = two("junk", [P, T], I8)
        bias = sb("bias", [P, T])
        prob = sb("prob", [P, AH, T])
        pt = two("pt", [P, TILE])
        mx = sb("mx", [P, AH, 5])
        mxr = sb("mxr", [P, AH])
        nb = sb("nb", [P, AH])
        nslope = sb("nslope", [P, AH])
        rows = sb("rows", [P, AH])
        rinv = sb("rinv", [P, AH])
        diag = sb("diag", [P, AG, P])
        rb = two("rb", [P, TILE])
        og = rb
        oh, ol = two("oh", [P, TILE], F16), two("ol", [P, TILE], F16)
        ones = sb("ones", [P, P])
        cnt, part, total, neg, sgn = (two(n, [P, 1]) for n in ("cnt", "part", "total", "neg", "sgn"))
        want, wanted, keep, cand, up = (two(n, [P, 1]) for n in ("want", "wanted", "keep", "cand", "up"))
        need, thr, sthr = (two(n, [P, 1]) for n in ("need", "thr", "sthr"))

        qk = [bank("qk0"), bank("qk1")]
        lg = [bank("lg0"), bank("lg1")]
        tp = [bank("tp0"), bank("tp1")]
        po = [bank("po0"), bank("po1")]

        q_loaded, iq_loaded = sem.two("q_loaded"), sem.two("iq_loaded")
        const_ready = sem("const_ready")
        lg_ready, relu_ready, sc_ready, sfill_ready = (sem(n) for n in ("lg_ready", "relu_ready", "sc_ready", "sfill_ready"))
        dist_ready, bias_ready, bfill_ready = sem("dist_ready"), sem("bias_ready"), sem("bfill_ready")
        qk_ready, biased_ready, nb_ready, prob_ready = (sem(n) for n in ("qk_ready", "biased_ready", "nb_ready", "prob_ready"))
        rinv_ready, diag_ready, tp_ready, pt_ready = (sem(n) for n in ("rinv_ready", "diag_ready", "tp_ready", "pt_ready"))
        gr_ready, og_ready, ohi_ready, olo_ready = (sem(n) for n in ("gr_ready", "og_ready", "ohi_ready", "olo_ready"))
        pv_done, step, stored = sem("pv_done"), sem("step"), sem.two("stored")
        found, cand_ready, part_ready = sem.two("found"), sem.two("cand_ready"), sem.two("part_ready")

        with nc.Block() as block:
            @block.sync
            def _(sp):
                def load(n):
                    b = n % 2
                    if n > 2:
                        sp.wait_ge(pv_done, products_before(n - 1))
                        sp.wait_ge(og_ready, KVH * (n - 2))
                    t = slice((n - 1) * P, n * P)
                    for src, dst in ((0, q_hi), (1, q_lo)):
                        sp.dma_start(dst[b][:], aq_parts[src].rearrange("p (h t) -> p h t", t=SEQ)[:, :, t]
                                     ).then_inc(q_loaded[b], 16)
                    sp.dma_start(gate[b][:], ag.rearrange("p (h t) -> p h t", t=SEQ)[:, :, t]
                                 ).then_inc(q_loaded[b], 16)

                def load_indexer(n):
                    b = n % 2
                    t = slice((n - 1) * P, n * P)
                    for half in range(2):
                        for odd in range(2):
                            sp.dma_start(iq[b][half * ID:(half + 1) * ID, odd, :, :],
                                         iq_parts[half, odd * ID:(odd + 1) * ID].rearrange(
                                             "p (h t) -> p h t", t=SEQ)[:, :, t]).then_inc(iq_loaded[b], 16)

                load_indexer(2)
                load(1)
                load_indexer(3)
                load(2)
                for (blocks, searched), (_, after) in zip(STEPS, STEPS[1:] + [((), ())]):
                    for n in after:
                        sp.wait_ge(lg_ready, scored_through(searched))
                        load_indexer(n)
                    for n in blocks:
                        for g in range(KVH):
                            sp.wait_ge(olo_ready, KVH * (n - 1) + g + 1)
                            for part_, o in enumerate((oh, ol)):
                                dst = oa_parts[part_].rearrange("p (h t) -> p h t", t=SEQ)
                                sp.dma_start(dst[:, g * AG:(g + 1) * AG, (n - 1) * P:n * P],
                                             o[g][:].rearrange("p (h t) -> p h t", t=P)).then_inc(stored[g], 16)
                        if n + 2 <= NB:
                            load(n + 2)
                for g in range(KVH):
                    sp.wait_ge(stored[g], NB * 32)

            LOADS, INDEXER_LOADS = 3 * 16, 4 * 16

            @block.gpsimd
            def _(pool):
                for h in range(AH):
                    nc.gpsimd.memset(nslope[:, h:h + 1], -2.0 ** -(h + 1)).then_inc(const_ready, 1)
                nc.gpsimd.memset(ones[:], 1.0).then_inc(const_ready, 1)
                nc.gpsimd.memset(prob[:, :, 0:PAD], 0.0).then_inc(const_ready, 1)

                def distances(n):
                    c = keys(n) - PAD
                    nc.gpsimd.iota(bias[:, PAD:keys(n)], pattern=[[1, c]], base=PAD - n * P, channel_multiplier=-1,
                                   allow_small_or_imprecise_dtypes=True).then_inc(dist_ready, 1)

                def causal(buf, n, fill):
                    d = buf[:, n * P:keys(n)]
                    return nc.gpsimd.affine_select(out=d, in_=d, compare_op=ALU.is_ge, fill=fill, base=0,
                                                   pattern=[[-1, P]], channel_multiplier=1)

                distances(1)
                pool.wait_ge(dist_ready, 1)
                causal(bias, 1, NEG).then_inc(bfill_ready, 1)

                def gated(n):
                    pool.wait_ge(rinv_ready, n)
                    if n == 1:
                        pool.wait_ge(const_ready, AH + 2)
                    for g in range(KVH):
                        if n > 1 or g:
                            pool.wait_ge(tp_ready, turned_before(n + 1) - KVH + g if g else turned_before(n))
                        h = slice(g * AG, (g + 1) * AG)
                        nc.gpsimd.tensor_tensor(out=diag[:], in0=ident[:, None, :].broadcast_to([P, AG, P]),
                                                in1=rinv[:, h, None].broadcast_to([P, AG, P]),
                                                op=ALU.mult).then_inc(diag_ready, 1)
                    for g in range(KVH):
                        pool.wait_ge(pt_ready, turned_before(n + 1) - KVH + g + 1)
                        pool.wait_ge(q_loaded[n % 2], (n + 1) // 2 * LOADS)
                        gr = gate[n % 2][:, g * AG:(g + 1) * AG, :]
                        nc.gpsimd.tensor_tensor(out=gr, in0=rb[g][:].rearrange("p (h t) -> p h t", t=P), in1=gr,
                                                op=ALU.mult).then_inc(gr_ready, 1)
                    for g in range(KVH):
                        pool.wait_ge(ohi_ready, KVH * (n - 1) + g + 1)
                        pool.wait_ge(stored[g], (n - 1) * 32)
                        nc.gpsimd.tensor_tensor(out=ol[g][:], in0=og[g][:], in1=oh[g][:],
                                                op=ALU.subtract).then_inc(olo_ready, 1)

                for blocks, searched in STEPS:
                    for n in blocks[1:]:
                        pool.wait_ge(biased_ready, dotted_before(n))
                        distances(n)
                    for n in searched:
                        pool.wait_ge(sc_ready, scored_through(searched))
                        causal(score[n % 2], n, LOWEST).then_inc(sfill_ready, 1)
                    for n in blocks[1:]:
                        pool.wait_ge(bias_ready, n - 1)
                        causal(bias, n, NEG).then_inc(bfill_ready, 1)
                    gated(blocks[0])
                    for n in searched[:1]:
                        pool.wait_ge(biased_ready, dotted_before(n))
                        distances(n)
                    for n in blocks[1:]:
                        gated(n)
                    for n in searched[:1]:
                        pool.wait_ge(bias_ready, n - 1)
                        causal(bias, n, NEG).then_inc(bfill_ready, 1)

            @block.scalar
            def _(act):
                def relus(n, h):
                    first, row = row_of_set(n)
                    for t, (a, b) in enumerate(tiles(n)):
                        i = first + h * row + t
                        act.wait_ge(lg_ready, i + 1)
                        if i >= 4:
                            act.wait_ge(sc_ready, i - 3)
                        nc.scalar.activation(relu[i % 4][:, 0:b - a], lg[i % 2][:, 0:b - a],
                                             ACT.Relu).then_inc(relu_ready, 1)

                def exponentials(n, h):
                    act.wait_ge(nb_ready, KVH * (n - 1) + h // AG + 1)
                    p = prob[:, h, PAD:keys(n)]
                    nc.scalar.activation(p, p, ACT.Exp, bias=nb[:, h:h + 1], scale=2.0 ** -(h + 1),
                                         accum_out=rows[:, h:h + 1]).then_inc(prob_ready, 1)

                def turned(n, items):
                    for j in items:
                        i = turned_before(n) + j
                        act.wait_ge(tp_ready, i + 1)
                        if j < KVH * (n + 1):
                            if j >= 2:
                                act.wait_ge(pv_done, products_before(n) + j - 1)
                            elif n > 1:
                                act.wait_ge(pv_done, products_before(n))
                            nc.scalar.activation(pt[i % 2][:], tp[i % 2][:], ACT.Copy).then_inc(pt_ready, 1)
                        else:
                            if n > 1:
                                act.wait_ge(olo_ready, KVH * (n - 1))
                            nc.scalar.activation(rb[j - KVH * (n + 1)][:], tp[i % 2][:],
                                                 ACT.Copy).then_inc(pt_ready, 1)

                def passes(searched, n, bits, cands, parts):
                    items = KVH * (n + 2) if n else 0
                    for q in range(len(bits)):
                        for m in searched:
                            ch = m % 2
                            act.wait_ge(cand_ready[ch], set_of(m) * CANDS + cands + q + 1)
                            view = low[ch] if bits is LOWER_BITS else score[ch]
                            part_keys = view[:, split(m):keys(m)]
                            if bits is UPPER_BITS:
                                part_keys = part_keys.bitcast(I16).rearrange("p (c two) -> p c two", two=2)[:, :, 1]
                            nc.scalar.activation(junk[ch][:, split(m):keys(m)], part_keys, ACT.Sign,
                                                 bias=cand[ch][:], scale=-1.0,
                                                 accum_out=part[ch][:]).then_inc(part_ready[ch], 1)
                        turned(n, range(items * q // len(bits), items * (q + 1) // len(bits)))

                def upper_outputs(n):
                    for g in range(KVH):
                        act.wait_ge(og_ready, KVH * (n - 1) + g + 1)
                        act.wait_ge(stored[g], (n - 1) * 32)
                        nc.scalar.activation(oh[g][:], og[g][:], ACT.Copy).then_inc(ohi_ready, 1)

                for blocks, searched in STEPS:
                    n = blocks[0]
                    for h in range(IH):
                        for m in searched:
                            relus(m, h)
                        if h > AG:
                            exponentials(n, h - AG - 1)
                    for h in range(AG - 1, AH):
                        exponentials(n, h)
                    passes(searched, n, UPPER_BITS, 0, 0)
                    upper_outputs(n)
                    for n in blocks[1:]:
                        for h in range(AH):
                            exponentials(n, h)
                    n = blocks[1] if blocks[1:] else None
                    passes(searched, n, LOWER_BITS, len(UPPER_BITS) + 1, len(UPPER_BITS))
                    if n:
                        upper_outputs(n)

            @block.vector
            def _(dve):
                done = [0]

                def then(ins):
                    done[0] += 1
                    ins.then_inc(step, 1)
                    dve.wait_ge(step, done[0])

                V = nc.vector
                dve.wait_ge(const_ready, AH + 2)

                def scores(n, h):
                    first, row = row_of_set(n)
                    s = score[n % 2]
                    for t, (a, b) in enumerate(tiles(n)):
                        i = first + h * row + t
                        dve.wait_ge(relu_ready, i + 1)
                        iw = iw_all[:, n, h:h + 1]
                        r = relu[i % 4][:, 0:b - a]
                        if h == 0:
                            V.tensor_scalar(s[:, a:b], r, iw, None, ALU.mult).then_inc(sc_ready, 1)
                        else:
                            dve.wait_ge(sc_ready, i - row + 1)
                            V.scalar_tensor_tensor(out=s[:, a:b], in0=r, scalar=iw, in1=s[:, a:b],
                                                   op0=ALU.mult, op1=ALU.add).then_inc(sc_ready, 1)

                def reciprocals(n):
                    dve.wait_ge(prob_ready, AH * n)
                    dve.wait_ge(diag_ready, KVH * (n - 1))
                    V.reciprocal(rinv[:], rows[:]).then_inc(rinv_ready, 1)

                results = [0, 0]

                def last(ch):
                    dve.wait_ge(found[ch], results[ch])

                def result(ch, ins):
                    results[ch] += 1
                    ins.then_inc(found[ch], 1)

                def count(ch, x, limit, op):
                    result(ch, V.tensor_scalar(junk[ch][:, PAD:PAD + x.shape[1]], x, limit, None, op, ALU.add,
                                               accum_out=cnt[ch][:]))

                def halves(n):
                    s = score[n % 2][:, PAD:keys(n)]
                    return (s.bitcast(I16).rearrange("p (c two) -> p c two", two=2)[:, :, 1],
                            s.bitcast(U16).rearrange("p (c two) -> p c two", two=2)[:, :, 0])

                def signs(searched):
                    both = [(n % 2, n, keys(n) - PAD) for n in searched]
                    for ch, n, c in both:
                        dve.wait_ge(sfill_ready, n - 1)
                        count(ch, score[ch][:, PAD:keys(n)], 0.0, ALU.is_ge)
                    for ch, n, c in both:
                        last(ch)
                        result(ch, V.tensor_scalar(neg[ch][:], cnt[ch][:], float(TOPK), None, ALU.is_lt))
                    for ch, n, c in both:
                        last(ch)
                        V.tensor_scalar(want[ch][:], neg[ch][:], float(c + 1 - 2 * TOPK), float(TOPK),
                                        ALU.mult, ALU.add)
                        result(ch, V.tensor_scalar(sgn[ch][:], neg[ch][:], -2.0, 1.0, ALU.mult, ALU.add))
                    for ch, n, c in both:
                        last(ch)
                        V.tensor_scalar(wanted[ch][:], want[ch][:], 0.5 * (keys(n) - split(n)), None, ALU.subtract)
                        s = score[ch][:, PAD:keys(n)]
                        result(ch, V.tensor_scalar(s, s, sgn[ch][:], 0.0, ALU.mult, ALU.add))
                    for ch, n, c in both:
                        last(ch)
                        V.memset(cand[ch][:], 2.0 ** 14 - 0.5).then_inc(cand_ready[ch], 1)

                def bits_of(searched, bits, cands, parts, n):
                    for q, bit in enumerate(bits):
                        for m in searched:
                            ch = m % 2
                            dve.wait_ge(cand_ready[ch], set_of(m) * CANDS + cands + q + 1)
                            x = halves(m)[0] if bits is UPPER_BITS else low[ch][:, PAD:keys(m)]
                            count(ch, x[:, 0:split(m) - PAD], cand[ch][:], ALU.is_ge)
                        for m in searched:
                            ch = m % 2
                            last(ch)
                            dve.wait_ge(part_ready[ch], set_of(m) * PARTS + parts + q + 1)
                            result(ch, V.scalar_tensor_tensor(out=total[ch][:], in0=part[ch][:], scalar=-0.5,
                                                              in1=cnt[ch][:], op0=ALU.mult, op1=ALU.add))
                        for m in searched:
                            ch = m % 2
                            last(ch)
                            result(ch, V.tensor_scalar(keep[ch][:], total[ch][:], wanted[ch][:], 0.5,
                                                       ALU.is_ge, ALU.subtract))
                        for m in searched:
                            ch = m % 2
                            last(ch)
                            V.scalar_tensor_tensor(out=cand[ch][:], in0=keep[ch][:], scalar=2.0 ** bit,
                                                   in1=cand[ch][:], op0=ALU.mult,
                                                   op1=ALU.add).then_inc(cand_ready[ch], 1)
                        if q == RECIPROCALS_AT and n:
                            reciprocals(n)

                def agreeing(searched):
                    for n in searched:
                        ch = n % 2
                        dve.wait_ge(cand_ready[ch], set_of(n) * CANDS + len(UPPER_BITS) + 1)
                        V.tensor_scalar(up[ch][:], cand[ch][:], 1.0, None, ALU.mult)
                        count(ch, halves(n)[0], cand[ch][:], ALU.is_gt)
                    for n in searched:
                        ch = n % 2
                        last(ch)
                        V.scalar_tensor_tensor(out=wanted[ch][:], in0=wanted[ch][:], scalar=1.0, in1=cnt[ch][:],
                                               op0=ALU.mult, op1=ALU.subtract)
                        result(ch, V.tensor_scalar(agree[ch][:, PAD:keys(n)], halves(n)[0], up[ch][:], None,
                                                   ALU.is_equal))
                    for n in searched:
                        ch = n % 2
                        last(ch)
                        result(ch, V.scalar_tensor_tensor(out=low[ch][:, PAD:keys(n)], in0=halves(n)[1], scalar=1.0,
                                                          in1=agree[ch][:, PAD:keys(n)], op0=ALU.add, op1=ALU.mult))
                    for n in searched:
                        ch = n % 2
                        last(ch)
                        V.memset(cand[ch][:], 2.0 ** 15 + 0.5).then_inc(cand_ready[ch], 1)

                def unselected(searched):
                    for n in searched:
                        ch = n % 2
                        dve.wait_ge(cand_ready[ch], (set_of(n) + 1) * CANDS)
                        V.tensor_scalar(thr[ch][:].bitcast(U16)[:, 0:1], cand[ch][:], 1.0, None, ALU.subtract)
                        V.tensor_scalar(thr[ch][:].bitcast(I16)[:, 1:2], up[ch][:], 1.0, None, ALU.mult)
                        s = score[ch][:, PAD:keys(n)]
                        result(ch, V.tensor_scalar(s, s, sgn[ch][:], None, ALU.mult))
                    for n in searched:
                        ch = n % 2
                        last(ch)
                        result(ch, V.tensor_tensor(out=sthr[ch][:], in0=thr[ch][:], in1=sgn[ch][:], op=ALU.mult))
                    for n in searched:
                        ch, e = n % 2, keys(n)
                        last(ch)
                        V.tensor_scalar(agree[ch][:, PAD:e], score[ch][:, PAD:e], sthr[ch][:], None, ALU.is_equal)
                        count(ch, score[ch][:, PAD:e], sthr[ch][:], ALU.is_gt)
                    for n in searched:
                        ch, e = n % 2, keys(n)
                        last(ch)
                        V.tensor_scalar(need[ch][:], cnt[ch][:], -1.0, float(TOPK), ALU.mult, ALU.add)
                        tie = agree[ch][:, PAD:e]
                        result(ch, V.tensor_tensor_scan(out=low[ch][:, PAD:e], data0=tie, data1=tie, initial=0.0,
                                                        op0=ALU.add, op1=ALU.max))
                    for n in searched:
                        ch, e = n % 2, keys(n)
                        last(ch)
                        result(ch, V.scalar_tensor_tensor(out=low[ch][:, PAD:e], in0=low[ch][:, PAD:e],
                                                          scalar=need[ch][:], in1=agree[ch][:, PAD:e],
                                                          op0=ALU.is_gt, op1=ALU.mult))
                    for n in searched:
                        ch, e = n % 2, keys(n)
                        last(ch)
                        result(ch, V.scalar_tensor_tensor(out=low[ch][:, PAD:e], in0=score[ch][:, PAD:e],
                                                          scalar=sthr[ch][:], in1=low[ch][:, PAD:e],
                                                          op0=ALU.is_lt, op1=ALU.add))

                def biases(n):
                    ch, e = n % 2, keys(n)
                    last(ch)
                    dve.wait_ge(dist_ready, n)
                    V.scalar_tensor_tensor(out=bias[:, PAD:e], in0=low[ch][:, PAD:e], scalar=NEG, in1=bias[:, PAD:e],
                                           op0=ALU.mult, op1=ALU.add).then_inc(bias_ready, 1)

                def biased(n, h):
                    if h == 0:
                        dve.wait_ge(bfill_ready, n)
                        if n > 1:
                            dve.wait_ge(pv_done, products_before(n))
                    nt = len(tiles(n))
                    for t, (a, b) in enumerate(tiles(n)):
                        i = dotted_before(n) + h * nt + t
                        dve.wait_ge(qk_ready, i + 1)
                        V.tensor_tensor_reduce(out=prob[:, h, a:b], in0=qk[i % 2][:, 0:b - a],
                                               in1=bias[:, a:b], scale=1.0, scalar=LOWEST, op0=ALU.add,
                                               op1=ALU.max, accum_out=mx[:, h, t:t + 1]
                                               ).then_inc(biased_ready, 1)
                    if h % AG == AG - 1:
                        g = slice(h + 1 - AG, h + 1)
                        dve.wait_ge(biased_ready, dotted_before(n) + (h + 1) * nt)
                        then(V.tensor_reduce(mxr[:, g], mx[:, g, 0:nt], AX.X, ALU.max))
                        V.tensor_tensor(out=nb[:, g], in0=mxr[:, g], in1=nslope[:, g],
                                        op=ALU.mult).then_inc(nb_ready, 1)

                def outputs(n):
                    for g in range(KVH):
                        dve.wait_ge(gr_ready, KVH * (n - 1) + g + 1)
                        dve.wait_ge(pv_done, products_before(n) + (g + 1) * (n + 1))
                        if n > 1:
                            dve.wait_ge(olo_ready, KVH * (n - 1))
                        V.tensor_tensor(out=og[g][:].rearrange("p (h t) -> p h t", t=P),
                                        in0=po[g][:].rearrange("p (h t) -> p h t", t=P),
                                        in1=gate[n % 2][:, g * AG:(g + 1) * AG, :],
                                        op=ALU.mult).then_inc(og_ready, 1)

                RECIPROCALS_AT = 5
                for blocks, searched in STEPS:
                    n = blocks[0]
                    for h in range(AH):
                        biased(n, h)
                        for m in searched:
                            scores(m, h)
                    for m in blocks[1:]:
                        biases(m)
                    if searched:
                        signs(searched)
                        bits_of(searched, UPPER_BITS, 0, 0, n)
                    else:
                        reciprocals(n)
                    outputs(n)
                    n = blocks[1] if blocks[1:] else None
                    if n:
                        for h in range(AH):
                            biased(n, h)
                    if searched:
                        agreeing(searched)
                        bits_of(searched, LOWER_BITS, len(UPPER_BITS) + 1, len(UPPER_BITS), n)
                    elif n:
                        reciprocals(n)
                    if n:
                        outputs(n)
                    if searched:
                        unselected(searched)
                        biases(searched[0])

            @block.tensor
            def _(pe):
                def logits(n, h):
                    first, row = row_of_set(n)
                    if h == 0:
                        pe.wait_ge(iq_loaded[n % 2], n // 2 * INDEXER_LOADS)
                    w = iq[n % 2][:, h % 2, h // 2, :]
                    for t, (a, b) in enumerate(tiles(n)):
                        i = first + h * row + t
                        if i >= 2:
                            pe.wait_ge(relu_ready, i - 1)
                        nc.tensor.matmul(lg[i % 2][:, 0:b - a], w, ik_hi[:, a:b], start=True, stop=False)
                        nc.tensor.matmul(lg[i % 2][:, 0:b - a], w[0:ID], ik_lo[:, a:b],
                                         start=False, stop=True).then_inc(lg_ready, 1)

                def dots(n, h):
                    if h == 0:
                        pe.wait_ge(q_loaded[n % 2], (n + 1) // 2 * LOADS)
                    for t, (a, b) in enumerate(tiles(n)):
                        i = dotted_before(n) + h * len(tiles(n)) + t
                        if i >= 2:
                            pe.wait_ge(biased_ready, i - 1)
                        o = qk[i % 2][:, 0:b - a]
                        g = h // AG
                        nc.tensor.matmul(o, q_hi[n % 2][:, h, :], kt_hi[:, g, a:b], start=True, stop=False)
                        nc.tensor.matmul(o, q_hi[n % 2][:, h, :], kt_lo[:, g, a:b], start=False, stop=False)
                        nc.tensor.matmul(o, q_lo[n % 2][:, h, :], kt_hi[:, g, a:b],
                                         start=False, stop=True).then_inc(qk_ready, 1)

                def values(n):
                    i = turned_before(n)

                    def turn(j, i):
                        g, k = divmod(j, n + 1)
                        pe.wait_ge(prob_ready, AH * (n - 1) + AG * (g + 1))
                        if i >= 2:
                            pe.wait_ge(pt_ready, i - 1)
                        for h in range(AG):
                            mm = nc.tensor.transpose(tp[i % 2][:, h * P:(h + 1) * P],
                                                     prob[:, g * AG + h, k * P:(k + 1) * P], ident[:])
                        mm.then_inc(tp_ready, 1)

                    total = KVH * (n + 1)
                    turn(0, i)
                    for j in range(total):
                        if j + 1 < total:
                            turn(j + 1, i + j + 1)
                        g, k = divmod(j, n + 1)
                        pe.wait_ge(pt_ready, i + j + 1)
                        if n > 1 and k == 0:
                            pe.wait_ge(og_ready, KVH * (n - 2) + g + 1)
                        mm = nc.tensor.matmul(po[g][:], v_all[:, k, g * P:(g + 1) * P], pt[(i + j) % 2][:],
                                              start=k == 0, stop=k == n)
                        mm.then_inc(pv_done, 1)
                    i += total
                    for g in range(KVH):
                        pe.wait_ge(diag_ready, KVH * (n - 1) + g + 1)
                        pe.wait_ge(pt_ready, i - 1)
                        nc.tensor.matmul(tp[i % 2][:], ones[:], diag[:].rearrange("p h q -> p (h q)"),
                                         start=True, stop=True).then_inc(tp_ready, 1)
                        i += 1

                pe.wait_ge(const_ready, AH + 2)
                for blocks, searched in STEPS:
                    for h in range(AH):
                        dots(blocks[0], h)
                        for m in searched:
                            logits(m, h)
                    values(blocks[0])
                    for n in blocks[1:]:
                        for h in range(AH):
                            dots(n, h)
                        values(n)


def load_parts(nc, parts, hi, lo, loaded):
    with nc.Block() as block:
        @block.sync
        def _(sp):
            for part, dst in enumerate((hi, lo)):
                for h in range(KD):
                    c = slice(h * SEQ, (h + 1) * SEQ)
                    sp.dma_start(dst[:, c], parts[part, :, c]).then_inc(loaded, 16)
            sp.wait_ge(loaded, 2 * KD * 16)


def merge_recurrent(nc, w_cols, w_r, ut_hi, ut_lo, ogr, merged_r, gate_a):
    KINDS = "gay"
    NI = len(KINDS) * NTILE
    with ExitStack() as ctx:
        def sb(name, shape, dt=F32):
            return ctx.enter_context(nc.sbuf_tensor("mr_" + name, shape, dt))

        sem = Semaphores(nc, ctx, "mr_")

        og_hi, og_lo = sb("og_hi", [P, RH * SEQ], F16), sb("og_lo", [P, RH * SEQ], F16)
        w_raw = [sb(f"w_raw{s}", [P, KD, P]) for s in range(3)]
        w_hi = [sb(f"w_hi{s}", [P, KD, P], F16) for s in range(3)]
        w_lo = [sb(f"w_lo{s}", [P, KD, P], F16) for s in range(3)]
        sg = [sb(f"sg{b}", [P, TILE]) for b in range(NTILE)]
        sa = [sb(f"sa{b}", [P, TILE]) for b in range(2)]
        mr = [sb(f"mr{b}", [P, TILE]) for b in range(2)]
        pz = [ctx.enter_context(nc.psum_tensor(f"mr_pz{b}", [P, TILE], F32)) for b in range(4)]
        w_loaded = [sem(f"w_loaded{s}") for s in range(3)]
        hi_ready, lo_ready, z_ready = sem("hi_ready"), sem("lo_ready"), sem("z_ready")
        load_turn = sem("load_turn")
        sg_ready, sa_ready, mr_ready = sem("sg_ready"), sem("sa_ready"), sem("mr_ready")
        a_stored, y_stored = sem.two("a_stored"), sem.two("y_stored")

        load_parts(nc, ogr, og_hi, og_lo, sem("og_loaded"))
        w_rc = w_r.rearrange("(k p) n -> p k n", p=P)
        SOURCE = [(w_cols, C_MR), (w_cols, C_MA), (w_rc, 0)]
        FREED = [NTILE, 2 * NTILE, 3 * NTILE]
        SPLIT_AT = {1: (2, 0), NTILE + 1: (0, 1), 2 * NTILE + 1: (1, 1)}

        def all_steps(eng, body):
            with eng.Fori(0, KD - 1) as i:
                body(i, False)
            body(KD - 1, True)

        with nc.Block() as block:
            @block.sync
            def _(sp):
                def load(s, i):
                    src, c = SOURCE[s]
                    sp.dma_start(w_raw[s][:], src[:, :, bass.ds(i * P + c, P)]).then_inc(w_loaded[s], 16)

                for s in range(3):
                    load(s, 0)

                def body(i, last):
                    if not last:
                        for s in range(2):
                            sp.wait_ge(lo_ready, i * 3 + s + 1)
                            load(s, i + 1)
                    for s in range(NI):
                        kind, t = KINDS[s // NTILE], s % NTILE
                        c = bass.ds(i * SEQ + t * TILE, TILE)
                        if kind == "a":
                            sp.wait_ge(sa_ready, i * NTILE + t + 1)
                            sp.dma_start(gate_a[:, c], sa[t % 2][:]).then_inc(a_stored[t % 2], 16)
                        if kind == "y":
                            if t == 0 and not last:
                                sp.wait_ge(lo_ready, i * 3 + 3)
                                sp.sem_inc(load_turn, 1)
                                load(2, i + 1)
                            sp.wait_ge(mr_ready, i * NTILE + t + 1)
                            sp.dma_start(merged_r[:, c], mr[t % 2][:]).then_inc(y_stored[t % 2], 16)
                all_steps(sp, body)
                for b in range(2):
                    sp.wait_ge(a_stored[b], KD * NTILE // 2 * 16)
                    sp.wait_ge(y_stored[b], KD * NTILE // 2 * 16)

            @block.scalar
            def _(act):
                def split(s, i, freed):
                    act.wait_ge(w_loaded[s], (i + 1) * 16)
                    act.wait_ge(z_ready, freed)
                    nc.scalar.activation(w_hi[s][:], w_raw[s][:], ACT.Copy, scale=WSCALE).then_inc(hi_ready, 1)

                split(0, 0, 0)
                split(1, 0, 0)

                def body(i, last):
                    for s in range(NI):
                        if s in SPLIT_AT:
                            sl, ahead = SPLIT_AT[s]
                            if not (last and ahead):
                                split(sl, i + ahead, i * NI + (FREED[sl] if ahead else 0))
                        kind, t = KINDS[s // NTILE], s % NTILE
                        if kind == "y":
                            continue
                        act.wait_ge(z_ready, i * NI + s + 1)
                        if kind == "g":
                            act.wait_ge(mr_ready, i * NTILE)
                            nc.scalar.activation(sg[t][:], pz[s % 4][:], ACT.Sigmoid,
                                                 scale=1.0 / WSCALE).then_inc(sg_ready, 1)
                        else:
                            act.wait_ge(a_stored[t % 2], (i * 2 + t // 2) * 16)
                            nc.scalar.activation(sa[t % 2][:], pz[s % 4][:], ACT.Sigmoid,
                                                 scale=1.0 / WSCALE).then_inc(sa_ready, 1)
                all_steps(act, body)

            @block.vector
            def _(dve):
                def split(s, count):
                    dve.wait_ge(hi_ready, count)
                    nc.vector.scalar_tensor_tensor(out=w_lo[s][:], in0=w_raw[s][:], scalar=WSCALE, in1=w_hi[s][:],
                                                   op0=ALU.mult, op1=ALU.subtract).then_inc(lo_ready, 1)

                split(0, 1)
                split(1, 2)

                def body(i, last):
                    for s in range(NI):
                        if s in SPLIT_AT:
                            sl, ahead = SPLIT_AT[s]
                            if not (last and ahead):
                                split(sl, i * 3 + {2: 3, 0: 4, 1: 5}[sl])
                        if KINDS[s // NTILE] == "y":
                            t = s % NTILE
                            dve.wait_ge(z_ready, i * NI + s + 1)
                            dve.wait_ge(sg_ready, i * NTILE + t + 1)
                            dve.wait_ge(y_stored[t % 2], (i * 2 + t // 2) * 16)
                            nc.vector.scalar_tensor_tensor(out=mr[t % 2][:], in0=pz[s % 4][:], scalar=1.0 / WSCALE,
                                                           in1=sg[t][:], op0=ALU.mult,
                                                           op1=ALU.mult).then_inc(mr_ready, 1)
                all_steps(dve, body)

            @block.tensor
            def _(pe):
                def body(i, last):
                    for s in range(NI):
                        kind, t = KINDS[s // NTILE], s % NTILE
                        if t == 0:
                            pe.wait_ge(lo_ready, i * 3 + s // NTILE + 1)
                        pe.wait_ge({"g": mr_ready, "a": sg_ready, "y": sa_ready}[kind],
                                   i * NTILE if kind == "g" else i * NTILE + t + 1)
                        n = 0
                        for k in range(KD):
                            if kind == "y":
                                c = slice(k * SEQ + t * TILE, k * SEQ + (t + 1) * TILE)
                                hi, lo = og_hi[:, c], og_lo[:, c]
                            else:
                                c = slice(P + t * TILE, P + (t + 1) * TILE)
                                hi, lo = ut_hi[:, k, c], ut_lo[:, k, c]
                            sl = s // NTILE
                            for w, m in ((w_hi, hi), (w_hi, lo), (w_lo, hi)):
                                mm = nc.tensor.matmul(pz[s % 4][:], w[sl][:, k, :], m,
                                                      start=n == 0, stop=n == 3 * KD - 1)
                                n += 1
                        mm.then_inc(z_ready, 1)
                all_steps(pe, body)


def merge_and_project(nc, x, w_a, w_out, oa_parts, merged_r, gate_a, out):
    with ExitStack() as ctx:
        def sb(name, shape, dt=F32):
            return ctx.enter_context(nc.sbuf_tensor("mo_" + name, shape, dt))

        sem = Semaphores(nc, ctx, "mo_")

        og_hi, og_lo = sb("og_hi", [P, AH * SEQ], F16), sb("og_lo", [P, AH * SEQ], F16)
        m_hi, m_lo = sb("m_hi", [P, KD, SEQ], F16), sb("m_lo", [P, KD, SEQ], F16)
        w_raw = [sb(f"w_raw{b}", [P, KD, P]) for b in range(2)]
        w_hi = [sb(f"w_hi{b}", [P, KD, P], F16) for b in range(2)]
        w_lo = [sb(f"w_lo{b}", [P, KD, P], F16) for b in range(2)]
        wo_hi, wo_lo = sb("wo_hi", [P, KD, D], F16), sb("wo_lo", [P, KD, D], F16)
        rp = [sb(f"rp{b}", [P, TILE]) for b in range(2)]
        ga = [sb(f"ga{b}", [P, TILE]) for b in range(2)]
        ya = [sb(f"ya{b}", [P, TILE]) for b in range(2)]
        mg = [sb(f"mg{b}", [P, TILE]) for b in range(2)]
        xw = [sb(f"xw{b}", [P, D]) for b in range(2)]
        pz = [ctx.enter_context(nc.psum_tensor(f"mo_pz{b}", [P, TILE], F32)) for b in range(4)]
        w_loaded, t_loaded, x_loaded = (sem.two(n) for n in ("w_loaded", "t_loaded", "x_loaded"))
        hi_ready, lo_ready, z_ready = sem("hi_ready"), sem("lo_ready"), sem("z_ready")
        ya_ready, mg_ready, mhi_ready, mlo_ready = (sem(n) for n in ("ya_ready", "mg_ready", "mhi_ready", "mlo_ready"))
        o_ready, y_ready, stored = sem("o_ready"), sem("y_ready"), sem.two("stored")

        load_parts(nc, oa_parts, og_hi, og_lo, sem("og_loaded"))
        w_ac = w_a.rearrange("(k p) n -> p k n", p=P)
        w_oc = w_out.rearrange("(k p) n -> p k n", p=P)

        with nc.Block() as block:
            @block.sync
            def _(sp):
                with sp.Fori(0, KD // 2) as ii:
                    for b in range(2):
                        i = ii * 2 + b
                        sp.wait_ge(lo_ready, i * 2)
                        sp.dma_start(w_raw[0][:], w_ac[:, :, bass.ds(i * P, P)]).then_inc(w_loaded[0], 16)
                        sp.dma_start(w_raw[1][:], w_oc[:, :, bass.ds(i * P, P)]).then_inc(w_loaded[1], 16)
                        for t in range(NTILE):
                            c = bass.ds(i * SEQ + t * TILE, TILE)
                            sp.wait_ge(mg_ready, i * NTILE + max(0, t - 1))
                            sp.dma_start(rp[t % 2][:], merged_r[:, c]).then_inc(t_loaded[t % 2], 16)
                            sp.dma_start(ga[t % 2][:], gate_a[:, c]).then_inc(t_loaded[t % 2], 16)

            @block.gpsimd
            def _(pool):
                with pool.Fori(0, KD) as i:
                    for t in range(NTILE + 1):
                        if t < NTILE:
                            pool.wait_ge(ya_ready, i * NTILE + t + 1)
                            pool.wait_ge(mlo_ready, i * NTILE + max(0, t - 1))
                            nc.gpsimd.tensor_tensor(out=mg[t % 2][:], in0=ya[t % 2][:], in1=rp[t % 2][:],
                                                    op=ALU.add).then_inc(mg_ready, 1)
                        if t:
                            pool.wait_ge(mhi_ready, i * NTILE + t)
                            c = slice((t - 1) * TILE, t * TILE)
                            nc.gpsimd.tensor_tensor(out=m_lo[:, bass.ds(i, 1), c], in0=mg[(t - 1) % 2][:, None, :],
                                                    in1=m_hi[:, bass.ds(i, 1), c], op=ALU.subtract
                                                    ).then_inc(mlo_ready, 1)

            @block.scalar
            def _(act):
                with act.Fori(0, KD // 2) as ii:
                    for b in range(2):
                        i = ii * 2 + b
                        act.wait_ge(w_loaded[0], (i + 1) * 16)
                        act.wait_ge(z_ready, ii * 2 * NTILE)
                        nc.scalar.activation(w_hi[b][:], w_raw[0][:], ACT.Copy, scale=WSCALE).then_inc(hi_ready, 1)
                        act.wait_ge(w_loaded[1], (i + 1) * 16)
                        nc.scalar.activation(wo_hi[:, :, bass.ds(i * P, P)], w_raw[1][:], ACT.Copy,
                                             scale=WSCALE).then_inc(hi_ready, 1)
                        for t in range(NTILE):
                            act.wait_ge(mg_ready, i * NTILE + t + 1)
                            nc.scalar.activation(m_hi[:, bass.ds(i, 1), t * TILE:(t + 1) * TILE],
                                                 mg[t % 2][:, None, :], ACT.Copy).then_inc(mhi_ready, 1)

            @block.vector
            def _(dve):
                with dve.Fori(0, KD // 2) as ii:
                    for b in range(2):
                        i = ii * 2 + b
                        dve.wait_ge(hi_ready, i * 2 + 1)
                        nc.vector.scalar_tensor_tensor(out=w_lo[b][:], in0=w_raw[0][:], scalar=WSCALE,
                                                       in1=w_hi[b][:], op0=ALU.mult,
                                                       op1=ALU.subtract).then_inc(lo_ready, 1)
                        dve.wait_ge(hi_ready, i * 2 + 2)
                        c = bass.ds(i * P, P)
                        nc.vector.scalar_tensor_tensor(out=wo_lo[:, :, c], in0=w_raw[1][:], scalar=WSCALE,
                                                       in1=wo_hi[:, :, c], op0=ALU.mult,
                                                       op1=ALU.subtract).then_inc(lo_ready, 1)
                        for t in range(NTILE):
                            dve.wait_ge(z_ready, i * NTILE + t + 1)
                            dve.wait_ge(t_loaded[t % 2], (i * 2 + t // 2 + 1) * 32)
                            nc.vector.scalar_tensor_tensor(out=ya[t % 2][:], in0=pz[t][:], scalar=1.0 / WSCALE,
                                                           in1=ga[t % 2][:], op0=ALU.mult,
                                                           op1=ALU.mult).then_inc(ya_ready, 1)

            @block.tensor
            def _(pe):
                with pe.Fori(0, KD // 2) as ii:
                    for b in range(2):
                        i = ii * 2 + b
                        pe.wait_ge(lo_ready, i * 2 + 1)
                        for t in range(NTILE):
                            pe.wait_ge(ya_ready, i * NTILE)
                            n = 0
                            for k in range(KD):
                                c = slice(k * SEQ + t * TILE, k * SEQ + (t + 1) * TILE)
                                for w, m in ((w_hi, og_hi), (w_hi, og_lo), (w_lo, og_hi)):
                                    mm = nc.tensor.matmul(pz[t][:], w[b][:, k, :], m[:, c],
                                                          start=n == 0, stop=n == 3 * KD - 1)
                                    n += 1
                            mm.then_inc(z_ready, 1)

        with nc.Block() as block:
            @block.sync
            def _(sp):
                with sp.Fori(0, SEQ // P // 2) as ii:
                    for b in range(2):
                        w = ii * 2 + b
                        sp.wait_ge(stored[b], ii * 16)
                        sp.dma_start(xw[b][:], x[bass.ds(w * P, P), :]).then_inc(x_loaded[b], 16)

            @block.scalar
            def _(act):
                with act.Fori(0, SEQ // P // 2) as ii:
                    for b in range(2):
                        w = ii * 2 + b
                        act.wait_ge(y_ready, w * 2 + 2)
                        act.dma_start(out[bass.ds(w * P, P), :], xw[b][:]).then_inc(stored[b], 16)
                for b in range(2):
                    act.wait_ge(stored[b], SEQ // P // 2 * 16)

            @block.vector
            def _(dve):
                with dve.Fori(0, SEQ // P // 2) as ii:
                    for b in range(2):
                        w = ii * 2 + b
                        dve.wait_ge(x_loaded[b], (ii + 1) * 16)
                        for j in range(2):
                            dve.wait_ge(o_ready, w * 2 + j + 1)
                            c = slice(j * TILE, (j + 1) * TILE)
                            nc.vector.scalar_tensor_tensor(out=xw[b][:, c], in0=pz[2 * b + j][:],
                                                           scalar=1.0 / WSCALE, in1=xw[b][:, c], op0=ALU.mult,
                                                           op1=ALU.add).then_inc(y_ready, 1)

            @block.tensor
            def _(pe):
                with pe.Fori(0, SEQ // P // 2) as ii:
                    for b in range(2):
                        w = ii * 2 + b
                        for j in range(2):
                            pe.wait_ge(y_ready, ii * 4)
                            n = 0
                            for k in range(KD):
                                c = bass.ds(w * P, P)
                                for m, wo in ((m_hi, wo_hi), (m_hi, wo_lo), (m_lo, wo_hi)):
                                    mm = nc.tensor.matmul(pz[2 * b + j][:], m[:, k, c],
                                                          wo[:, k, j * TILE:(j + 1) * TILE],
                                                          start=n == 0, stop=n == 3 * KD - 1)
                                    n += 1
                            mm.then_inc(o_ready, 1)


def hybrid_layer(nc, x, meta, norm_g, w_in, lb_logits, r_norm_g, q_norm_g, k_norm_g, w_r, w_a, w_out, out):
    w_cols = w_in[0].rearrange("(k p) n -> p k n", p=P)
    x, w_r, w_a, w_out, out = x[0], w_r[0], w_a[0], w_out[0], out[0]

    def scratch(name, shape, dt):
        return nc.dram_tensor(name, shape, dt).ap()

    or_parts = scratch("or_parts", [2, P, RH * SEQ], F16)
    merged_r = scratch("merged_r", [P, KD * SEQ], F32)
    gate_a = scratch("gate_a", [P, KD * SEQ], F32)
    aq_parts = scratch("aq_parts", [2, P, AH * SEQ], F16)
    iq_parts = scratch("iq_parts", [2, P, IH // 2 * SEQ], F16)
    ag = scratch("ag", [P, AH * SEQ], F32)
    oa_parts = scratch("oa_parts", [2, P, AH * SEQ], F16)

    with ExitStack() as ctx:
        def sb(name, shape, dt):
            return ctx.enter_context(nc.sbuf_tensor(name, shape, dt))

        ident = sb("ident", [P, P], F32)
        with ExitStack() as keys_live:
            with nc.sbuf_tensor("ut_hi", [P, KD, T], F16) as ut_hi, nc.sbuf_tensor("ut_lo", [P, KD, T], F16) as ut_lo:
                normed_input(nc, x, meta, norm_g, ut_hi, ut_lo, ident)
                recurrence(nc, w_cols, lb_logits, r_norm_g, ut_hi, ut_lo, or_parts, ident)
                merge_recurrent(nc, w_cols, w_r, ut_hi, ut_lo, or_parts, merged_r, gate_a)

                def keyed(name, shape, dt):
                    return keys_live.enter_context(nc.sbuf_tensor(name, shape, dt, side="right"))
                kt_hi, kt_lo = keyed("kt_hi", [P, KVH, T], F16), keyed("kt_lo", [P, KVH, T], F16)
                v_all = keyed("v_all", [P, NW, KVH * P], F32)
                ik_hi, ik_lo = keyed("ik_hi", [P, T], F16), keyed("ik_lo", [ID, T], F16)
                iw_all = keyed("iw_all", [P, NW, IH], F32)
                keys_values(nc, w_cols, k_norm_g, ut_hi, ut_lo, kt_hi, kt_lo, v_all, ik_hi, ik_lo, iw_all)
                queries(nc, w_cols, q_norm_g, ut_hi, ut_lo, aq_parts, iq_parts, ag)
            attention(nc, aq_parts, iq_parts, ag, kt_hi, kt_lo, v_all, ik_hi, ik_lo, iw_all, oa_parts, ident)
        merge_and_project(nc, x, w_a, w_out, oa_parts, merged_r, gate_a, out)


_INS = ["x", "meta", "norm_g", "w_in", "lb_logits", "r_norm_g", "q_norm_g", "k_norm_g", "w_r", "w_a", "w_out"]


def kernel(**inputs):
    import numpy as np
    from concourse import bacc
    from concourse.bass_utils import run_bass_kernel_spmd

    nc = bacc.Bacc("TRN2", target_bir_lowering=False, num_devices=1)
    arrays, args = {}, []
    for name in _INS:
        a = np.ascontiguousarray(inputs[name])
        arrays[f"in_{name}"] = a
        args.append(nc.dram_tensor(f"in_{name}", a.shape, mybir.dt.from_np(a.dtype), kind="ExternalInput").ap())
    out = nc.dram_tensor("out0", (1, SEQ, D), F32, kind="ExternalOutput").ap()
    hybrid_layer(nc, *args, out)
    return run_bass_kernel_spmd(nc, [arrays], core_ids=[0]).results[0]["out0"]
```

```python
import concourse.bass as bass
from concourse import mybir
from contextlib import ExitStack

F32 = mybir.dt.float32
F16 = mybir.dt.float16
I16 = mybir.dt.int16
U16 = mybir.dt.uint16
I8 = mybir.dt.int8
ALU = mybir.AluOpType
ACT = mybir.ActivationFunctionType
AX = mybir.AxisListType

P = 128
D = 1024
KD = D // P
SEQ = 2048
META = 16
PAD = P - META
T = SEQ + P
NW = T // P
TILE = 512
WPT = TILE // P
NTILE = SEQ // TILE
RH = 8
AH, KVH, AG = 8, 2, 4
IH, ID = 8, 64
TOPK = 256
EPS = 1e-6
FROM = 1
WSCALE = 64.0
C_RQ, C_RF, C_RI, C_RG = 0, 1024, 2048, 3072
C_AQ, C_AK, C_AV, C_AG = 4096, 5120, 5376, 5632
C_IQ, C_IK, C_IW = 6656, 7168, 7232
C_MR, C_MA = 7240, 8264


class Semaphores:

    def __init__(self, nc, ctx, prefix):
        self.nc, self.prefix, self.taken = nc, prefix, []
        ctx.callback(self.clear)

    def __call__(self, name):
        self.taken.append(self.nc.alloc_semaphore(self.prefix + name))
        return self.taken[-1]

    def start(self):
        for taken in self.taken:
            self.nc.gpsimd.sem_inc(taken, FROM)
        self.nc.all_engine_barrier()

    def many(self, names):
        return [self(name) for name in names.split()]

    def two(self, name):
        return [self(f"{name}{b}") for b in range(2)]

    def clear(self):
        self.nc.clear_and_free_semaphores(self.taken)
        self.nc.all_engine_barrier()


def normed_input(nc, x, meta, norm_g, ut_hi, ut_lo, ident):
    XB = 4
    with ExitStack() as ctx:
        def sb(name, shape, dt=F32):
            return ctx.enter_context(nc.sbuf_tensor(name, shape, dt))

        sem = Semaphores(nc, ctx, "n_")

        xw = [sb(f"xw{b}", [P, D]) for b in range(XB)]
        xsq = sb("xsq", [P, D])
        xn = [sb(f"xn{b}", [P, D]) for b in range(2)]
        u32 = [sb(f"u32_{b}", [P, KD, P]) for b in range(2)]
        stat = sb("stat", [P, XB, 4])
        eps = sb("eps0", [P, 1])
        g = sb("g0", [P, KD])
        pt = [ctx.enter_context(nc.psum_tensor(f"pt{b}", [P, KD, P], F32)) for b in range(2)]
        meta_ready, load_turn = sem("meta_ready"), sem("load_turn")
        const_ready = sem("const_ready")
        g_loaded = sem("g_loaded")
        x_loaded = [sem(f"x_loaded{b}") for b in range(XB)]
        ssq_ready = sem("ssq_ready")
        sd_ready = sem("sd_ready")
        rstd_ready = sem("rstd_ready")
        xn_ready = sem("xn_ready")
        xt_ready = sem("xt_ready")
        u32_ready = sem("u32_ready")
        hi_ready = sem("hi_ready")
        lo_ready = sem("lo_ready")

        def windows(eng, first, second):
            if first:
                first(0, 0, 0, 1)
            with eng.Fori(0, (NW - 1) // XB) as i:
                for j in range(1, XB + 1):
                    if first:
                        first(i * XB + j, j % 2, j % XB, i + 1 + j // XB)
                    if second:
                        second(i * XB + j - 1, (j - 1) % 2)
            if second:
                second(NW - 1, 0)

        sem.start()
        with nc.Block() as block:
            @block.sync
            def _(sp):
                sp.dma_start(g[:], norm_g.rearrange("o (k p) -> p (o k)", p=P),
                             allow_slow_non_contiguous=True).then_inc(g_loaded, 16)

                def load(n, b):
                    sp.dma_start(xw[b][:], x[bass.ds((n - 1) * P, P), :]).then_inc(x_loaded[b], 16)

                def reload(n, b):
                    sp.wait_ge(xn_ready, FROM + n + 1 - XB)
                    sp.sem_inc(load_turn, 1)
                    load(n, b)

                for n in range(1, XB):
                    load(n, n)
                sp.wait_ge(meta_ready, FROM + 1)
                sp.dma_start(xw[0][PAD:P, :], meta).then_inc(x_loaded[0], 16)
                with sp.Fori(1, (NW - 1) // XB) as i:
                    for b in range(XB):
                        reload(i * XB + b, b)
                reload(NW - 1, 0)

            @block.gpsimd
            def _(pool):
                nc.gpsimd.memset(xw[0][:], 0.0).then_inc(meta_ready, 1)
                nc.gpsimd.memset(eps[:], EPS).then_inc(const_ready, 1)
                nc.gpsimd.memset(ident[:], 0.0).then_inc(const_ready, 1)
                pool.wait_ge(const_ready, FROM + 2)
                nc.gpsimd.affine_select(out=ident[:], in_=ident[:], compare_op=ALU.not_equal, fill=1.0,
                                        base=0, pattern=[[-1, P]], channel_multiplier=1).then_inc(const_ready, 1)

                pool.sem_inc(lo_ready, 2)

                def low(n, b):
                    pool.wait_ge(hi_ready, FROM + n + 1)
                    c = bass.ds(n * P, P)
                    nc.gpsimd.tensor_tensor(out=ut_lo[:, :, c], in0=u32[b][:], in1=ut_hi[:, :, c],
                                            op=ALU.subtract).then_inc(lo_ready, 1)
                windows(pool, None, low)

            @block.scalar
            def _(act):
                act.wait_ge(const_ready, FROM + 1)

                def norm(n, b, xb, visit):
                    act.wait_ge(x_loaded[xb], FROM + visit * 16)
                    nc.scalar.activation(xsq[:], xw[xb][:], ACT.Square,
                                         accum_out=stat[:, xb, 0:1]).then_inc(ssq_ready, 1)
                    act.wait_ge(ssq_ready, FROM + n + 1)
                    nc.scalar.activation(stat[:, xb, 1:2], stat[:, xb, 0:1], ACT.Sqrt,
                                         bias=eps[:], scale=1.0 / D).then_inc(sd_ready, 1)

                def high(n, b):
                    act.wait_ge(u32_ready, FROM + n + 1)
                    nc.scalar.activation(ut_hi[:, :, bass.ds(n * P, P)], u32[b][:], ACT.Copy).then_inc(hi_ready, 1)

                def ahead(i, j):
                    high(i * XB + j - 1, (j - 1) % 2)
                    norm(i * XB + j + 2, (j + 2) % 2, (j + 2) % XB, i + 1 + (j + 2) // XB)

                for n in range(3):
                    norm(n, n % 2, n, 1)
                whole = (NW - 1) // XB - 1
                with act.Fori(0, whole) as i:
                    for j in range(1, XB + 1):
                        ahead(i, j)
                for j in range(1, XB - 1):
                    ahead(whole, j)
                for n in range(NW - 3, NW):
                    high(n, n % 2)

            @block.vector
            def _(dve):
                dve.wait_ge(g_loaded, FROM + 16)

                def scale(n, b, xb, visit):
                    dve.wait_ge(sd_ready, FROM + n + 1)
                    nc.vector.reciprocal(stat[:, xb, 2:3], stat[:, xb, 1:2]).then_inc(rstd_ready, 1)
                    dve.wait_ge(rstd_ready, FROM + n + 1)
                    if not isinstance(n, int):
                        dve.wait_ge(xt_ready, FROM + n - 1)
                    nc.vector.tensor_scalar(xn[b][:], xw[xb][:], stat[:, xb, 2:3], None,
                                            ALU.mult).then_inc(xn_ready, 1)

                def gain(n, b):
                    dve.wait_ge(xt_ready, FROM + n + 1)
                    dve.wait_ge(lo_ready, FROM + n + 1)
                    nc.vector.tensor_tensor(out=u32[b][:], in0=pt[b][:],
                                            in1=g[:, :, None].broadcast_to([P, KD, P]),
                                            op=ALU.mult).then_inc(u32_ready, 1)
                windows(dve, scale, gain)

            @block.tensor
            def _(pe):
                pe.wait_ge(const_ready, FROM + 3)

                def turn(n, b, xb, visit):
                    pe.wait_ge(xn_ready, FROM + n + 1)
                    if not isinstance(n, int):
                        pe.wait_ge(u32_ready, FROM + n - 1)
                    for k in range(KD):
                        mm = nc.tensor.transpose(pt[b][:, k, :], xn[b][:, k * P:(k + 1) * P], ident[:])
                    mm.then_inc(xt_ready, 1)
                windows(pe, turn, None)


def recurrence(nc, w_cols, lb_logits, r_norm_g, ut_hi, ut_lo, og_parts, ident):
    STEPS = 1 + NTILE
    HPI = 2
    SPI = STEPS * HPI
    TPI = NTILE * HPI
    LEVELS = (128, 64, 32)
    LEAF = 16
    CLAMP = 80.0
    HALF = 0.5 / WSCALE
    QSCALE = P ** -0.5 * HALF
    with ExitStack() as ctx:
        def sb(name, shape, dt=F32):
            return ctx.enter_context(nc.sbuf_tensor(name, shape, dt))

        def two(name, shape, dt=F32):
            return [sb(f"{name}{b}", shape, dt) for b in range(2)]

        sem = Semaphores(nc, ctx, "r_")

        w_raw = [sb(f"w_raw{b}", [P, KD, P]) for b in range(2)]
        w_hi = [two(f"w_hi{s}_", [P, KD, P], F16) for s in range(4)]
        w_lo = [two(f"w_lo{s}_", [P, KD, P], F16) for s in range(4)]
        sig = sb("sig", [P, TILE])
        f_ = sb("f_", [P, TILE])
        lf = sb("lf", [P, TILE])
        q_ = two("q_", [P, TILE])
        k_ = sb("k_", [P, TILE])
        b_ = sb("b_", [P, TILE])
        gate = two("gate", [P, TILE])
        v_ = two("v_", [P, WPT, P])
        df = [sb(f"df{i}", [P, TILE]) for i in range(5)]
        ex = [sb(f"ex{i}", [P, TILE]) for i in range(7)]
        lv = [two(f"lv{i}_", [P, TILE]) for i in range(3)]
        lq, lk = two("lq", [P, TILE]), two("lk", [P, TILE])
        qe, ke = two("qe", [P, TILE]), two("ke", [P, TILE])
        eend = two("eend", [P, WPT])
        kt = sb("kt", [P, WPT, P])
        att = sb("att", [P, WPT, P])
        st = [sb(f"st{b}", [P, WPT, P]) for b in range(2)]
        sq = sb("sq", [P, TILE])
        rin = sb("rin", [P, TILE])
        on = sb("on", [P, TILE])
        og = sb("og", [P, TILE])
        oh, ol = two("oh", [P, TILE], F16), two("ol", [P, TILE], F16)
        restart = sb("restart", [P, TILE])
        mask = sb("mask", [P, 4, P], I8)
        mone = sb("mone", [P, P], I8)
        ones = sb("ones", [P, P])
        eps = sb("eps1", [P, 1])
        gq = sb("gq", [P, 1])
        lbl = sb("lbl", [P, 2, RH])
        lbd = sb("lbd", [P, RH])
        lb = sb("lb", [P, RH])
        omlb = sb("omlb", [P, RH])

        def bank(name, dt=F32):
            return ctx.enter_context(nc.psum_tensor("r" + name, [P, TILE], dt))

        pf, pq, pg, pv = bank("pf"), bank("pq"), bank("pg"), bank("pv")
        pa = [bank("pa0"), bank("pa1")]
        pk, po = bank("pk"), bank("po")

        w_loaded = [sem(f"w_loaded{s}") for s in range(4)]
        load_turn, copy_turn = sem("load_turn"), sem("copy_turn")
        whi_ready, wlo_ready = sem("whi_ready"), sem("wlo_ready")
        small_loaded, const_ready = sem("small_loaded"), sem("const_ready")
        lb_step, lb_ready = sem("lb_step"), sem("lb_ready")
        pf_ready, pq_ready, pg_ready, pv_ready = sem.many("pf_ready pq_ready pg_ready pv_ready")
        sig_ready, q_ready, gate_ready, v_ready = sem.many("sig_ready q_ready gate_ready v_ready")
        th_q_ready, th_g_ready = sem("th_q_ready"), sem("th_g_ready")
        f_ready, k_ready, lf_ready, b_ready = sem.many("f_ready k_ready lf_ready b_ready")
        leaf_raw, df_ready, ex_ready, prod_ready = sem.many("leaf_raw df_ready ex_ready prod_ready")
        pk_ready, kt_ready, u_ready, st_ready = sem.many("pk_ready kt_ready u_ready st_ready")
        pa_ready, att_ready = sem("pa_ready"), sem("att_ready")
        o_ready, sq_ready, ms_ready = sem("o_ready"), sem("sq_ready"), sem("ms_ready")
        ms_copied, ln_ready, rin_ready = sem("ms_copied"), sem("ln_ready"), sem("rin_ready")
        o_stored = [sem(f"o_stored{b}") for b in range(2)]
        on_ready, og_ready, ohi_ready, olo_ready = sem.many("on_ready og_ready ohi_ready olo_ready")

        class Step:

            def __init__(self, i, s):
                self.n = i * SPI + s
                self.head = i * HPI + s // STEPS
                self.full = s % STEPS > 0
                self.m = i * TPI + (s // STEPS * NTILE + max(0, s % STEPS - 1))
                self.hb = s // STEPS % 2
                self.b = s % 2
                self.tile = s % STEPS - 1
                self.t0 = P + TILE * self.tile if self.full else 0
                self.stores = self.head * NTILE + self.tile // 2 * 2
                self.wins = WPT if self.full else 1
                self.cols = self.wins * P

        def run(eng, body):
            last = RH // HPI - 1
            body(Step(0, 0), None, None)
            body(Step(0, 1), Step(0, 0), None)
            with eng.Fori(0, last) as i:
                for s in range(2, SPI + 2):
                    body(Step(i, s), Step(i, s - 1), Step(i, s - 2))
            for s in range(2, SPI):
                body(Step(last, s), Step(last, s - 1), Step(last, s - 2))
            body(None, Step(last, SPI - 1), Step(last, SPI - 2))
            body(None, None, Step(last, SPI - 1))

        def splits(x):
            return x.full and not (isinstance(x.head, int) and x.head == RH - 1)

        def level(ap, L, cols):
            return ap[:, 0:cols].rearrange("p (n l) -> p n l", l=L)

        sem.start()
        def upper_halves(ap, L):
            return ap.rearrange("p (n l) -> p n l", l=L)[:, :, L // 2:L]

        with nc.Block() as block:
            @block.sync
            def _(sp):
                sp.dma_start(lbl[:], lb_logits.rearrange("r (h p) -> p r h", p=P),
                             allow_slow_non_contiguous=True).then_inc(small_loaded, 16)
                sp.dma_start(gq[:], r_norm_g.rearrange("o p -> p o"),
                             allow_slow_non_contiguous=True).then_inc(small_loaded, 16)
                def load(h, s):
                    c = (C_RF, C_RQ, C_RG, C_RI)[s]
                    sp.wait_ge(wlo_ready, FROM + h * 4 + s - 1)
                    sp.sem_inc(load_turn, 1)
                    sp.dma_start(w_raw[s % 2][:], w_cols[:, :, bass.ds(h * P + c, P)]).then_inc(w_loaded[s], 16)

                for s, c in enumerate((C_RF, C_RQ)):
                    sp.dma_start(w_raw[s][:], w_cols[:, :, c:c + P]).then_inc(w_loaded[s], 16)
                load(0, 2)
                load(0, 3)

                def store(h, tiles):
                    for j in tiles:
                        sp.wait_ge(olo_ready, FROM + h * NTILE + j + 1)
                        for part, o in enumerate((oh, ol)):
                            sp.dma_start(og_parts[part, :, bass.ds(h * SEQ + j * TILE, TILE)],
                                         o[j % 2][:]).then_inc(o_stored[j % 2], 16)

                def head(h, first):
                    load(h + 1, 0)
                    load(h + 1, 1)
                    if not first:
                        store(h - 1, [NTILE - 1])
                    load(h + 1, 2)
                    load(h + 1, 3)
                    store(h, range(NTILE - 1))

                head(0, True)
                with sp.Fori(0, RH - 2) as i:
                    head(i + 1, False)
                store(RH - 2, [NTILE - 1])
                store(RH - 1, range(NTILE))
                for b in range(2):
                    sp.wait_ge(o_stored[b], FROM + RH * NTILE * 16)

            @block.gpsimd
            def _(pool):
                nc.gpsimd.memset(restart[:], 1.0).then_inc(const_ready, 1)
                nc.gpsimd.memset(ones[:], 1.0 / P).then_inc(const_ready, 1)
                nc.gpsimd.memset(eps[:], EPS).then_inc(const_ready, 1)
                nc.gpsimd.memset(att[:], 0.0).then_inc(const_ready, 1)
                nc.gpsimd.memset(mone[:], 1).then_inc(const_ready, 1)
                nc.gpsimd.memset(mask[:], 0).then_inc(const_ready, 1)
                pool.wait_ge(const_ready, FROM + 6)
                nc.gpsimd.memset(restart[:].rearrange("p (w t) -> p w t", t=P)[:, :, 0], 0.0).then_inc(const_ready, 1)
                count = 7
                for j, L in enumerate(LEVELS):
                    H = L // 2
                    for blk in range(P // L):
                        sub = mask[:, j, blk * L + H:(blk + 1) * L]
                        nc.gpsimd.affine_select(out=sub, in_=mone[:, 0:H], compare_op=ALU.is_ge, fill=0.0,
                                                base=-blk * L, pattern=[[0, H]], channel_multiplier=1
                                                ).then_inc(const_ready, 1)
                        count += 1
                        pool.wait_ge(const_ready, FROM + count)
                        nc.gpsimd.affine_select(out=sub, in_=sub, compare_op=ALU.is_gt, fill=0.0,
                                                base=blk * L + H, pattern=[[0, H]], channel_multiplier=-1
                                                ).then_inc(const_ready, 1)
                        count += 1
                for blk in range(P // LEAF):
                    sub = mask[:, 3, blk * LEAF:(blk + 1) * LEAF]
                    nc.gpsimd.affine_select(out=sub, in_=mone[:, 0:LEAF], compare_op=ALU.is_ge, fill=0.0,
                                            base=-blk * LEAF, pattern=[[0, LEAF]], channel_multiplier=1
                                            ).then_inc(const_ready, 1)
                    count += 1
                    pool.wait_ge(const_ready, FROM + count)
                    nc.gpsimd.affine_select(out=sub, in_=sub, compare_op=ALU.is_ge, fill=0.0,
                                            base=blk * LEAF, pattern=[[1, LEAF]], channel_multiplier=-1
                                            ).then_inc(const_ready, 1)
                    count += 1
                assert count == CONSTS
                pool.wait_ge(const_ready, FROM + CONSTS)
                pool.sem_inc(prod_ready, 2)

                def products(x):
                    b, c = x.b, x.cols
                    pool.wait_ge(k_ready, FROM + x.n + 1)
                    pool.wait_ge(ex_ready, FROM + x.n + 1)
                    if x.full:
                        pool.wait_ge(q_ready, FROM + x.m + 1)
                        pool.wait_ge(o_ready, FROM + x.m - (x.tile > 0))
                        for j, L in enumerate(LEVELS):
                            H = L // 2
                            e, o = level(ex[j], L, c), level(lv[j][b], L, c)
                            nc.gpsimd.tensor_tensor(out=o[:, :, 0:H], in0=e[:, :, 0:H],
                                                    in1=level(k_, L, c)[:, :, 0:H], op=ALU.mult)
                            nc.gpsimd.tensor_tensor(out=o[:, :, H:L], in0=e[:, :, H:L],
                                                    in1=level(q_[b], L, c)[:, :, H:L], op=ALU.mult)
                        nc.gpsimd.tensor_tensor(out=lq[b][:], in0=ex[3][:], in1=q_[b][:], op=ALU.mult)
                        nc.gpsimd.tensor_tensor(out=lk[b][:], in0=ex[4][:], in1=k_[:], op=ALU.mult)
                        nc.gpsimd.tensor_tensor(out=qe[b][:], in0=ex[5][:], in1=q_[b][:], op=ALU.mult)
                    nc.gpsimd.tensor_tensor(out=ke[b][:, 0:c], in0=ex[6][:, 0:c], in1=k_[:, 0:c],
                                            op=ALU.mult).then_inc(prod_ready, 1)

                def out_low(x):
                    if x.full:
                        pool.wait_ge(ohi_ready, FROM + x.m + 1)
                        pool.wait_ge(o_stored[x.tile % 2], FROM + x.stores * 16)
                        nc.gpsimd.tensor_tensor(out=ol[x.tile % 2][:], in0=og[:], in1=oh[x.tile % 2][:],
                                                op=ALU.subtract).then_inc(olo_ready, 1)
                def body(x, y, z):
                    if x:
                        products(x)
                    if z:
                        out_low(z)
                run(pool, body)

            @block.scalar
            def _(act):
                def weights(h, s, hb):
                    act.wait_ge(w_loaded[s], FROM + (h + 1) * 16)
                    nc.scalar.activation(w_hi[s][hb][:], w_raw[s % 2][:], ACT.Copy,
                                         scale=WSCALE).then_inc(whi_ready, 1)

                def sigmoid(x):
                    c = x.cols
                    act.wait_ge(pf_ready, FROM + x.n + 1)
                    act.wait_ge(f_ready, FROM + x.n)
                    nc.scalar.activation(sig[:, 0:c], pf[:, 0:c], ACT.Sigmoid,
                                         scale=1.0 / WSCALE).then_inc(sig_ready, 1)

                def tanhs(x):
                    act.wait_ge(pq_ready, FROM + x.m + 1)
                    nc.scalar.activation(q_[x.b][:], pq[:], ACT.Tanh, scale=HALF).then_inc(th_q_ready, 1)
                    if splits(x):
                        weights(x.head + 1, x.tile, 1 - x.hb)
                    act.wait_ge(pg_ready, FROM + x.m + 1)
                    nc.scalar.activation(gate[x.b][:], pg[:], ACT.Tanh, scale=HALF).then_inc(th_g_ready, 1)

                def squares(x):
                    act.wait_ge(o_ready, FROM + x.m + 1)
                    act.wait_ge(ln_ready, FROM + x.m)
                    nc.scalar.activation(sq[:], po[:], ACT.Square, scale=QSCALE).then_inc(sq_ready, 1)
                    act.wait_ge(ms_ready, FROM + x.m + 1)
                    nc.scalar.activation(sq[:], pk[:], ACT.Copy).then_inc(ms_copied, 1)

                def high(x):
                    act.wait_ge(og_ready, FROM + x.m + 1)
                    act.wait_ge(o_stored[x.tile % 2], FROM + x.stores * 16)
                    nc.scalar.activation(oh[x.tile % 2][:], og[:], ACT.Copy).then_inc(ohi_ready, 1)

                def decays(x, z):
                    if x:
                        c = x.cols
                        act.wait_ge(f_ready, FROM + x.n + 1)
                        nc.scalar.activation(lf[:, 0:c], f_[:, 0:c], ACT.Ln).then_inc(lf_ready, 1)
                    if z:
                        act.wait_ge(ms_copied, FROM + z.m + 1)
                        act.wait_ge(og_ready, FROM + z.m)
                        nc.scalar.activation(rin[:], sq[:], ACT.Ln, bias=eps[:]).then_inc(ln_ready, 1)
                        act.wait_ge(ln_ready, FROM + z.m + 1)
                        nc.scalar.activation(rin[:], rin[:], ACT.Exp, scale=-0.5).then_inc(rin_ready, 1)
                    if not x:
                        return
                    act.wait_ge(df_ready, FROM + x.n + 1)
                    act.wait_ge(prod_ready, FROM + x.n + 2)
                    if x.full:
                        for j, L in enumerate(LEVELS):
                            H = L // 2
                            d, e = level(df[j], L, c), level(ex[j], L, c)
                            nc.scalar.activation(e[:, :, 0:H], d[:, :, 0:H], ACT.Exp, scale=-1.0)
                            nc.scalar.activation(e[:, :, H:L], d[:, :, H:L], ACT.Exp)
                        nc.scalar.activation(ex[3][:], df[3][:], ACT.Exp)
                        nc.scalar.activation(ex[4][:], df[3][:], ACT.Exp, scale=-1.0)
                        nc.scalar.activation(ex[5][:], b_[:], ACT.Exp)
                        nc.scalar.activation(eend[x.b][:], b_[:].rearrange("p (w t) -> p w t", t=P)[:, :, P - 1],
                                             ACT.Exp)
                    nc.scalar.activation(ex[6][:, 0:c], df[4][:, 0:c], ACT.Exp, scale=-1.0).then_inc(ex_ready, 1)

                def body(x, y, z):
                    z = z if z and z.full else None
                    if x:
                        sigmoid(x)
                    decays(x, z)
                    if x and x.full:
                        tanhs(x)
                    if z:
                        high(z)
                    if y and y.full:
                        squares(y)

                for s in range(4):
                    weights(0, s, 0)
                act.wait_ge(small_loaded, FROM + 32)
                nc.scalar.activation(gq[:], gq[:], ACT.Copy, scale=QSCALE * HALF).then_inc(lb_ready, 1)
                act.wait_ge(lb_step, FROM + 1)
                nc.scalar.activation(lb[:], lbd[:], ACT.Sigmoid).then_inc(lb_ready, 1)
                nc.scalar.activation(omlb[:], lbd[:], ACT.Sigmoid, scale=-1.0).then_inc(lb_ready, 1)
                act.wait_ge(const_ready, FROM + CONSTS)
                run(act, body)

            @block.vector
            def _(dve):
                def weights(h, s, hb):
                    dve.wait_ge(whi_ready, FROM + h * 4 + s + 1)
                    nc.vector.scalar_tensor_tensor(out=w_lo[s][hb][:], in0=w_raw[s % 2][:], scalar=WSCALE,
                                                   in1=w_hi[s][hb][:], op0=ALU.mult,
                                                   op1=ALU.subtract).then_inc(wlo_ready, 1)

                def forget(x):
                    c = x.cols
                    h = x.head
                    dve.wait_ge(sig_ready, FROM + x.n + 1)
                    dve.wait_ge(lf_ready, FROM + x.n)
                    nc.vector.tensor_scalar(f_[:, 0:c], sig[:, 0:c], omlb[:, bass.ds(h, 1)], lb[:, bass.ds(h, 1)],
                                            ALU.mult, ALU.add).then_inc(f_ready, 1)
                    dve.wait_ge(f_ready, FROM + x.n + 1)
                    dve.wait_ge(prod_ready, FROM + x.n + 2)
                    nc.vector.tensor_scalar(k_[:, 0:c], f_[:, 0:c], -1.0, 1.0, ALU.mult, ALU.add).then_inc(k_ready, 1)

                def differences(x):
                    c = x.cols
                    dve.wait_ge(lf_ready, FROM + x.n + 1)
                    nc.vector.tensor_tensor_scan(out=b_[:, 0:c], data0=restart[:, 0:c], data1=lf[:, 0:c],
                                                 initial=0.0, op0=ALU.mult, op1=ALU.add).then_inc(b_ready, 1)
                    dve.wait_ge(b_ready, FROM + x.n + 1)
                    if x.full:
                        a = level(b_, LEAF, c)[:, :, LEAF // 2 - 1:LEAF // 2].broadcast_to([P, c // LEAF, LEAF])
                        nc.vector.tensor_tensor(out=level(df[3], LEAF, c), in0=level(b_, LEAF, c), in1=a,
                                                op=ALU.subtract).then_inc(leaf_raw, 1)
                        for j, L in enumerate(LEVELS):
                            a = level(b_, L, c)[:, :, L // 2 - 1:L // 2].broadcast_to([P, c // L, L])
                            nc.vector.tensor_tensor(out=level(df[j], L, c), in0=level(b_, L, c), in1=a,
                                                    op=ALU.subtract)
                        dve.wait_ge(leaf_raw, FROM + x.m + 1)
                        nc.vector.tensor_scalar(df[3][:], df[3][:], CLAMP, -CLAMP, ALU.min, ALU.max)
                    a = level(b_, P, c)[:, :, P - 1:P].broadcast_to([P, c // P, P])
                    nc.vector.tensor_tensor(out=level(df[4], P, c), in0=level(b_, P, c), in1=a,
                                            op=ALU.subtract).then_inc(df_ready, 1)

                def gates(x):
                    dve.wait_ge(th_q_ready, FROM + x.m + 1)
                    nc.vector.scalar_tensor_tensor(out=q_[x.b][:], in0=q_[x.b][:], scalar=1.0, in1=pq[:],
                                                   op0=ALU.add, op1=ALU.mult).then_inc(q_ready, 1)
                    dve.wait_ge(th_g_ready, FROM + x.m + 1)
                    nc.vector.scalar_tensor_tensor(out=gate[x.b][:], in0=gate[x.b][:], scalar=1.0, in1=pg[:],
                                                   op0=ALU.add, op1=ALU.mult).then_inc(gate_ready, 1)

                def values(x):
                    c = x.cols
                    dve.wait_ge(pv_ready, FROM + x.n + 1)
                    nc.vector.tensor_scalar(v_[x.b][:, 0:x.wins, :], pv[:, 0:c].rearrange("p (w t) -> p w t", t=P),
                                            1.0 / WSCALE, None, ALU.mult).then_inc(v_ready, 1)

                def masked(x, j):
                    out, where = att[:], mask[:, j:j + 1, :].broadcast_to([P, WPT, P])
                    scores = pa[j % 2][:].rearrange("p (w t) -> p w t", t=P)
                    if j < 3:
                        L = LEVELS[j]
                        out, where, scores = (a.rearrange("p w (n l) -> p w n l", l=L)[:, :, :, L // 2:L]
                                              for a in (out, where, scores))
                    nc.vector.copy_predicated(out, where, scores).then_inc(att_ready, 1)

                def keys(x):
                    dve.wait_ge(pk_ready, FROM + x.n + 1)
                    if x.full:
                        dve.wait_ge(pa_ready, FROM + x.m * 4 + 1)
                    nc.vector.tensor_copy(kt[:, 0:x.wins, :], pk[:, 0:x.cols].rearrange("p (w t) -> p w t", t=P)
                                          ).then_inc(kt_ready, 1)
                    if x.full:
                        masked(x, 0)

                def window(x):
                    b = x.b
                    if not x.full:
                        dve.wait_ge(u_ready, FROM + x.n + 1)
                        nc.vector.tensor_copy(st[1 - b][:, 0, :], po[:, 0:P]).then_inc(st_ready, 1)
                        return
                    dve.wait_ge(pa_ready, FROM + x.m * 4 + 2)
                    dve.wait_ge(att_ready, FROM + x.m * 4 + 1)
                    dve.sem_inc(copy_turn, 1)
                    masked(x, 1)
                    dve.wait_ge(u_ready, FROM + x.n + 1)
                    for w in range(WPT):
                        if w >= 2:
                            dve.wait_ge(pa_ready, FROM + x.m * 4 + w + 1)
                            dve.wait_ge(att_ready, FROM + x.m * 4 + w)
                        dve.wait_ge(st_ready, FROM + x.m * WPT + w + x.head + 1)
                        nxt = st[1 - b][:, 0, :] if w == WPT - 1 else st[b][:, w + 1, :]
                        nc.vector.scalar_tensor_tensor(out=nxt, in0=st[b][:, w, :], scalar=eend[b][:, w:w + 1],
                                                       in1=po[:, w * P:(w + 1) * P], op0=ALU.mult,
                                                       op1=ALU.add).then_inc(st_ready, 1)
                        if w >= 2:
                            masked(x, w)

                def scaled(x):
                    dve.wait_ge(sq_ready, FROM + x.m + 1)
                    dve.wait_ge(gate_ready, FROM + x.m + 1)
                    dve.wait_ge(og_ready, FROM + x.m)
                    nc.vector.scalar_tensor_tensor(out=on[:], in0=po[:], scalar=gq[:], in1=gate[x.b][:],
                                                   op0=ALU.mult, op1=ALU.mult).then_inc(on_ready, 1)

                def normed(x):
                    dve.wait_ge(rin_ready, FROM + x.m + 1)
                    dve.wait_ge(on_ready, FROM + x.m + 1)
                    dve.wait_ge(olo_ready, FROM + x.m)
                    nc.vector.tensor_tensor(out=og[:], in0=on[:], in1=rin[:], op=ALU.mult).then_inc(og_ready, 1)

                def body(x, y, z):
                    if x:
                        forget(x)
                    if y:
                        keys(y)
                    if x:
                        differences(x)
                    if y:
                        window(y)
                    if z and z.full:
                        normed(z)
                    if x and splits(x):
                        weights(x.head + 1, x.tile, 1 - x.hb)
                    if x and x.full:
                        gates(x)
                    if y and y.full:
                        scaled(y)
                    if x:
                        values(x)

                dve.wait_ge(small_loaded, FROM + 32)
                nc.vector.tensor_tensor(out=lbd[:], in0=lbl[:, 0, :], in1=lbl[:, 1, :],
                                        op=ALU.subtract).then_inc(lb_step, 1)
                for s in range(4):
                    weights(0, s, 0)
                dve.wait_ge(lb_ready, FROM + 3)
                dve.wait_ge(const_ready, FROM + CONSTS)
                run(dve, body)

            @block.tensor
            def _(pe):
                def project(out, s, x):
                    n = 0
                    for k in range(KD):
                        u = slice(x.t0, x.t0 + x.cols)
                        for w, m in ((w_hi, ut_hi), (w_hi, ut_lo), (w_lo, ut_hi)):
                            mm = nc.tensor.matmul(out[:, 0:x.cols], w[s][x.hb][:, k, :], m[:, k, u],
                                                  start=n == 0, stop=n == 3 * KD - 1)
                            n += 1
                    return mm

                def values(x):
                    if not x.full:
                        pe.wait_ge(wlo_ready, FROM + (x.head + 1) * 4)
                    pe.wait_ge(v_ready, FROM + x.n)
                    for w in range(x.wins):
                        n = 0
                        for k in range(KD):
                            u = slice(x.t0 + w * P, x.t0 + (w + 1) * P)
                            for m, wt in ((ut_hi, w_hi), (ut_hi, w_lo), (ut_lo, w_hi)):
                                mm = nc.tensor.matmul(pv[:, w * P:(w + 1) * P], m[:, k, u], wt[3][x.hb][:, k, :],
                                                      start=n == 0, stop=n == 3 * KD - 1)
                                n += 1
                    mm.then_inc(pv_ready, 1)

                def turned_keys(x):
                    pe.wait_ge(prod_ready, FROM + x.n + 3)
                    pe.wait_ge(ms_copied, FROM + x.m)
                    for w in range(x.wins):
                        c = slice(w * P, (w + 1) * P)
                        mm = nc.tensor.transpose(pk[:, c], ke[x.b][:, c], ident[:])
                    mm.then_inc(pk_ready, 1)

                def scores(x, j):
                    pe.wait_ge(att_ready, FROM + x.m * 4 + max(0, j - 1))
                    s_part, t_part = (lv[j][x.b], lv[j][x.b]) if j < 3 else (lk[x.b], lq[x.b])
                    for w in range(WPT):
                        c = slice(w * P, (w + 1) * P)
                        out, moved = pa[j % 2][:, c], t_part[:, c]
                        if j < 3:
                            out, moved = upper_halves(out, LEVELS[j]), upper_halves(moved, LEVELS[j])
                        mm = nc.tensor.matmul(out, s_part[:, c], moved, start=True, stop=True)
                    mm.then_inc(pa_ready, 1)

                def key_values(x):
                    pe.wait_ge(kt_ready, FROM + x.n + 1)
                    pe.wait_ge(v_ready, FROM + x.n + 1)
                    pe.wait_ge(on_ready, FROM + x.m)
                    for w in range(x.wins):
                        mm = nc.tensor.matmul(po[:, w * P:(w + 1) * P], kt[:, w, :], v_[x.b][:, w, :],
                                              start=True, stop=True)
                    mm.then_inc(u_ready, 1)

                def outputs(x):
                    b = x.b
                    pe.wait_ge(att_ready, FROM + (x.m + 1) * 4)
                    pe.wait_ge(st_ready, FROM + (x.m + 1) * WPT + x.head + 1)
                    for w in range(WPT):
                        c = slice(w * P, (w + 1) * P)
                        nc.tensor.matmul(po[:, c], st[b][:, w, :], qe[b][:, c], start=True, stop=False)
                        mm = nc.tensor.matmul(po[:, c], v_[b][:, w, :], att[:, w, :], start=False, stop=True)
                    mm.then_inc(o_ready, 1)

                def mean_squares(x):
                    pe.wait_ge(const_ready, FROM + CONSTS)
                    pe.wait_ge(sq_ready, FROM + x.m + 1)
                    nc.tensor.matmul(pk[:], ones[:], sq[:], start=True, stop=True).then_inc(ms_ready, 1)

                def forget(x):
                    pe.wait_ge(wlo_ready, FROM + x.head * 4 + 1)
                    pe.wait_ge(sig_ready, FROM + x.n)
                    project(pf, 0, x).then_inc(pf_ready, 1)

                def query(x):
                    pe.wait_ge(wlo_ready, FROM + x.head * 4 + 2)
                    pe.wait_ge(q_ready, FROM + x.m)
                    project(pq, 1, x).then_inc(pq_ready, 1)

                def gate_logits(x):
                    pe.wait_ge(wlo_ready, FROM + x.head * 4 + 3)
                    pe.wait_ge(gate_ready, FROM + x.m)
                    project(pg, 2, x).then_inc(pg_ready, 1)

                def body(x, y, z):
                    tile = y and y.full
                    if x:
                        forget(x)
                    if x and not x.full:
                        values(x)
                    if y:
                        turned_keys(y)
                    if tile:
                        scores(y, 0)
                        scores(y, 1)
                    if x and x.full:
                        query(x)
                    if y:
                        key_values(y)
                    if tile:
                        scores(y, 2)
                        scores(y, 3)
                    if x and x.full:
                        gate_logits(x)
                    if tile:
                        outputs(y)
                    if x and x.full:
                        values(x)
                    if tile:
                        mean_squares(y)
                run(pe, body)


CONSTS = 7 + 2 * sum(P // L for L in (128, 64, 32)) + 2 * (P // 16)


def keys_values(nc, w_cols, k_norm_g, ut_hi, ut_lo, kt_hi, kt_lo, v_all, ik_hi, ik_lo, iw_all):
    TILES = [(0, P)] + [(P + j * TILE, TILE) for j in range(NTILE)]
    IW_SCALE = IH ** -0.5 * ID ** -0.5
    with ExitStack() as ctx:
        def sb(name, shape, dt=F32):
            return ctx.enter_context(nc.sbuf_tensor("kv_" + name, shape, dt))

        sem = Semaphores(nc, ctx, "kv_")

        slices = 5
        w_raw = [sb(f"w_raw{b}", [P, KD, P]) for b in range(slices)]
        w_hi = [sb(f"w_hi{b}", [P, KD, P], F16) for b in range(3)]
        w_lo = [sb(f"w_lo{b}", [P, KD, P], F16) for b in range(3)]
        wv_hi, wv_lo = sb("wv_hi", [P, KD, KVH * P], F16), sb("wv_lo", [P, KD, KVH * P], F16)
        wi_raw = sb("wi_raw", [P, KD, IH])
        wi_hi, wi_lo = sb("wi_hi", [P, KD, IH], F16), sb("wi_lo", [P, KD, IH], F16)
        gk = sb("gk", [P, 1])
        gks = sb("gks", [P, 1])
        eps = sb("eps", [P, 1])
        ones = sb("ones", [P, P])
        sq = sb("sq", [P, TILE])
        lnm = sb("lnm", [P, TILE])
        rin = sb("rin", [P, TILE])
        kn = sb("kn", [P, TILE])
        pz = [ctx.enter_context(nc.psum_tensor(f"kv_pz{b}", [P, TILE], F32)) for b in range(4)]
        pm = ctx.enter_context(nc.psum_tensor("kv_pm", [P, TILE], F32))
        pv = [ctx.enter_context(nc.psum_tensor(f"kv_pv{b}", [P, TILE], F32)) for b in range(2)]

        w_loaded, g_loaded = [sem(f"w_loaded{s}") for s in range(slices + 1)], sem("g_loaded")
        hi_ready, lo_ready = sem("hi_ready"), sem("lo_ready")
        const_ready, gks_ready = sem("const_ready"), sem("gks_ready")
        z_ready, sq_ready, ms_ready, ln_ready, rin_ready = sem.many("z_ready sq_ready ms_ready ln_ready rin_ready")
        kn_ready, khi_ready, klo_ready = sem.many("kn_ready khi_ready klo_ready")
        ihi_ready, ilo_ready = sem("ihi_ready"), sem("ilo_ready")
        v_ready, vcopy_ready = sem("v_ready"), sem("vcopy_ready")
        NK = KVH * len(TILES)

        with nc.Block() as block:
            @block.sync
            def _(sp):
                for s in range(KVH):
                    sp.dma_start(w_raw[s][:], w_cols[:, :, C_AK + s * P:C_AK + (s + 1) * P]).then_inc(w_loaded[s], 16)
                for half in range(2):
                    sp.dma_start(w_raw[2][:, :, half * ID:(half + 1) * ID],
                                 w_cols[:, :, C_IK:C_IK + ID]).then_inc(w_loaded[2], 16)
                for s in range(KVH):
                    sp.dma_start(w_raw[3 + s][:], w_cols[:, :, C_AV + s * P:C_AV + (s + 1) * P]
                                 ).then_inc(w_loaded[3 + s], 16)
                sp.dma_start(wi_raw[:], w_cols[:, :, C_IW:C_IW + IH]).then_inc(w_loaded[slices], 16)
                sp.dma_start(gk[:], k_norm_g.rearrange("o p -> p o"),
                             allow_slow_non_contiguous=True).then_inc(g_loaded, 16)

            def parts():
                for s in range(3):
                    yield w_raw[s][:], w_hi[s][:], w_lo[s][:]
                for s in range(KVH):
                    c = slice(s * P, (s + 1) * P)
                    yield w_raw[3 + s][:], wv_hi[:, :, c], wv_lo[:, :, c]
                yield wi_raw[:], wi_hi[:], wi_lo[:]

            @block.gpsimd
            def _(pool):
                nc.gpsimd.memset(eps[:], EPS).then_inc(const_ready, 1)
                nc.gpsimd.memset(ones[:], 1.0 / P).then_inc(const_ready, 1)
                for n in range(NK):
                    h, (t0, c) = n // len(TILES), TILES[n % len(TILES)]
                    pool.wait_ge(khi_ready, n + 1)
                    nc.gpsimd.tensor_tensor(out=kt_lo[:, h, t0:t0 + c], in0=kn[:, 0:c],
                                            in1=kt_hi[:, h, t0:t0 + c], op=ALU.subtract).then_inc(klo_ready, 1)

            @block.scalar
            def _(act):
                act.wait_ge(const_ready, 2)
                for n, (raw, hi, _) in enumerate(parts()):
                    act.wait_ge(w_loaded[n], 32 if n == 2 else 16)
                    nc.scalar.activation(hi, raw, ACT.Copy, scale=WSCALE).then_inc(hi_ready, 1)
                act.wait_ge(g_loaded, 16)
                nc.scalar.activation(gks[:], gk[:], ACT.Copy, scale=1.0 / WSCALE).then_inc(gks_ready, 1)
                for n in range(NK):
                    h, (t0, c) = n // len(TILES), TILES[n % len(TILES)]
                    act.wait_ge(z_ready, n + 1)
                    nc.scalar.activation(sq[:, 0:c], pz[n % 4][:, 0:c], ACT.Square,
                                         scale=1.0 / WSCALE).then_inc(sq_ready, 1)
                    act.wait_ge(ms_ready, n + 1)
                    nc.scalar.activation(lnm[:, 0:c], pm[:, 0:c], ACT.Ln, bias=eps[:]).then_inc(ln_ready, 1)
                    act.wait_ge(ln_ready, n + 1)
                    nc.scalar.activation(rin[:, 0:c], lnm[:, 0:c], ACT.Exp, scale=-0.5).then_inc(rin_ready, 1)
                    act.wait_ge(kn_ready, n + 1)
                    nc.scalar.activation(kt_hi[:, h, t0:t0 + c], kn[:, 0:c], ACT.Copy).then_inc(khi_ready, 1)
                for j, (t0, c) in enumerate(TILES):
                    act.wait_ge(z_ready, NK + j + 1)
                    nc.scalar.activation(ik_hi[:, t0:t0 + c], pz[(NK + j) % 4][:, 0:c], ACT.Copy,
                                         scale=1.0 / WSCALE).then_inc(ihi_ready, 1)

            @block.vector
            def _(dve):
                for n, (raw, hi, lo) in enumerate(parts()):
                    dve.wait_ge(hi_ready, n + 1)
                    nc.vector.scalar_tensor_tensor(out=lo, in0=raw, scalar=WSCALE, in1=hi, op0=ALU.mult,
                                                   op1=ALU.subtract).then_inc(lo_ready, 1)
                dve.wait_ge(gks_ready, 1)
                for n in range(NK):
                    c = TILES[n % len(TILES)][1]
                    dve.wait_ge(rin_ready, n + 1)
                    dve.wait_ge(klo_ready, n)
                    nc.vector.scalar_tensor_tensor(out=kn[:, 0:c], in0=pz[n % 4][:, 0:c], scalar=gks[:],
                                                   in1=rin[:, 0:c], op0=ALU.mult,
                                                   op1=ALU.mult).then_inc(kn_ready, 1)
                for j, (t0, c) in enumerate(TILES):
                    dve.wait_ge(ihi_ready, j + 1)
                    nc.vector.scalar_tensor_tensor(out=ik_lo[:, t0:t0 + c], in0=pz[(NK + j) % 4][0:ID, 0:c],
                                                   scalar=1.0 / WSCALE, in1=ik_hi[0:ID, t0:t0 + c],
                                                   op0=ALU.mult, op1=ALU.subtract).then_inc(ilo_ready, 1)
                for w in range(NW):
                    dve.wait_ge(v_ready, w + 1)
                    nc.vector.tensor_scalar(v_all[:, w, :], pv[w % 2][:, 0:KVH * P], 1.0 / WSCALE, None, ALU.mult)
                    nc.vector.tensor_scalar(iw_all[:, w, :], pv[w % 2][:, KVH * P:KVH * P + IH],
                                            IW_SCALE / WSCALE, None, ALU.mult).then_inc(vcopy_ready, 1)

            @block.tensor
            def _(pe):
                def project(out, hi, lo, t0, c):
                    n = 0
                    for k in range(KD):
                        for w, m in ((hi, ut_hi), (hi, ut_lo), (lo, ut_hi)):
                            mm = nc.tensor.matmul(out[:, 0:c], w[:, k, :], m[:, k, t0:t0 + c],
                                                  start=n == 0, stop=n == 3 * KD - 1)
                            n += 1
                    return mm

                pe.wait_ge(const_ready, 2)
                for n in range(NK + len(TILES)):
                    h, (t0, c) = n // len(TILES), TILES[n % len(TILES)]
                    if n % len(TILES) == 0:
                        pe.wait_ge(lo_ready, h + 1)
                    if 4 <= n < NK + 4:
                        pe.wait_ge(kn_ready, n - 3)
                    if n >= NK + 4:
                        pe.wait_ge(ilo_ready, n - NK - 3)
                    project(pz[n % 4], w_hi[h], w_lo[h], t0, c).then_inc(z_ready, 1)
                    if 1 <= n <= NK:
                        c = TILES[(n - 1) % len(TILES)][1]
                        pe.wait_ge(sq_ready, n)
                        nc.tensor.matmul(pm[:, 0:c], ones[:], sq[:, 0:c], start=True, stop=True).then_inc(ms_ready, 1)
                pe.wait_ge(lo_ready, slices + 1)
                for w in range(NW):
                    if w >= 2:
                        pe.wait_ge(vcopy_ready, w - 1)
                    for o, hi, lo in ((pv[w % 2][:, 0:KVH * P], wv_hi, wv_lo),
                                      (pv[w % 2][:, KVH * P:KVH * P + IH], wi_hi, wi_lo)):
                        n = 0
                        for k in range(KD):
                            for m, wt in ((ut_hi, hi), (ut_hi, lo), (ut_lo, hi)):
                                mm = nc.tensor.matmul(o, m[:, k, w * P:(w + 1) * P], wt[:, k, :],
                                                      start=n == 0, stop=n == 3 * KD - 1)
                                n += 1
                    mm.then_inc(v_ready, 1)


def queries(nc, w_cols, q_norm_g, ut_hi, ut_lo, aq_parts, iq_parts, ag):
    ITER = 4
    HPI = AH // ITER
    items = [(kind, h, t) for h in range(HPI) for t in range(NTILE) for kind in "qg"]
    items += [("i", 0, t) for t in range(NTILE)]
    NI = len(items)
    QPI = HPI * NTILE
    slot = {("q", 0): 0, ("g", 0): 1, ("q", 1): 2, ("g", 1): 3, ("i", 0): 4}
    with ExitStack() as ctx:
        def sb(name, shape, dt=F32):
            return ctx.enter_context(nc.sbuf_tensor("q_" + name, shape, dt))

        def two(name, shape, dt=F32):
            return [sb(f"{name}{b}", shape, dt) for b in range(2)]

        sem = Semaphores(nc, ctx, "q_")

        w_raw = two("w_raw", [P, KD, P])
        w_hi = [sb(f"w_hi{b}", [P, KD, P], F16) for b in range(5)]
        w_lo = [sb(f"w_lo{b}", [P, KD, P], F16) for b in range(5)]
        gq = sb("gq", [P, 1])
        gqs = sb("gqs", [P, AH])
        eps = sb("eps", [P, 1])
        ones = sb("ones", [P, P])
        sq, lnm, rin, qn = two("sq", [P, TILE]), sb("lnm", [P, TILE]), two("rin", [P, TILE]), two("qn", [P, TILE])
        qh, ql = two("qh", [P, TILE], F16), two("ql", [P, TILE], F16)
        ih, il = two("ih", [P, TILE], F16), two("il", [P, TILE], F16)
        gs = two("gs", [P, TILE])
        pz = [ctx.enter_context(nc.psum_tensor(f"q_pz{b}", [P, TILE], F32)) for b in range(4)]
        pm = [ctx.enter_context(nc.psum_tensor(f"q_pm{b}", [P, TILE], F32)) for b in range(2)]

        g_loaded, w_loaded = sem("g_loaded"), sem.two("w_loaded")
        hi_ready, lo_ready, const_ready, gqs_ready = sem.many("hi_ready lo_ready const_ready gqs_ready")
        z_ready, sq_ready, ms_ready, ln_ready, rin_ready = sem.many("z_ready sq_ready ms_ready ln_ready rin_ready")
        qn_ready, qhi_ready, qlo_ready = sem.many("qn_ready qhi_ready qlo_ready")
        gs_ready, ihi_ready, ilo_ready = sem.many("gs_ready ihi_ready ilo_ready")
        store_turn = sem("store_turn")
        q_stored, g_stored, i_stored = (sem.two(n) for n in ("q_stored", "g_stored", "i_stored"))

        class Item:

            def __init__(self, i, s):
                self.kind, self.h, self.t = items[s]
                self.s, self.n = s, i * NI + s
                before = sum(1 for k, _, _ in items[:s] if k == self.kind)
                per = sum(1 for k, _, _ in items if k == self.kind)
                self.m = i * per + before
                self.b = before % 2
                self.uses = i * (per // 2) + before // 2
                self.head = i * HPI + self.h
                self.pair = i
                self.t0 = P + self.t * TILE

        BEFORE = [0, 1, 2, 3]
        INSIDE = {2: [(0, 4)], 9: [(1, 0), (1, 1)], 17: [(1, 2), (1, 3)]}
        SPLITS = 5

        def column(i, sl):
            return {0: C_AQ + i * HPI * P, 1: C_AG + i * HPI * P, 2: C_AQ + i * HPI * P + P,
                    3: C_AG + i * HPI * P + P, 4: C_IQ + i * P}[sl]

        sem.start()
        with nc.Block() as block:
            @block.sync
            def _(sp):
                sp.dma_start(gq[:], q_norm_g.rearrange("o p -> p o"),
                             allow_slow_non_contiguous=True).then_inc(g_loaded, 16)
                for n, sl in enumerate(BEFORE):
                    if n >= 2:
                        sp.wait_ge(lo_ready, FROM + n - 1)
                    sp.dma_start(w_raw[n % 2][:], w_cols[:, :, column(0, sl):column(0, sl) + P]
                                 ).then_inc(w_loaded[n % 2], 16)
                with sp.Fori(0, ITER // 2) as ii:
                    for half in range(2):
                        i = ii * 2 + half
                        at = 0
                        for s in range(NI):
                            for ahead, sl in INSIDE.get({0: 2, 5: 9, 13: 17}.get(s), ()):
                                b = (half * SPLITS + at) % 2
                                sp.wait_ge(lo_ready, FROM + i * SPLITS + at + 3)
                                sp.dma_start(w_raw[b][:], w_cols[:, :, bass.ds(column(i + ahead, sl), P)]
                                             ).then_inc(w_loaded[b], 16)
                                at += 1
                            x = Item(i, s)
                            if x.kind == "q":
                                sp.wait_ge(qlo_ready, FROM + x.m + 1)
                                for part, o in enumerate((qh, ql)):
                                    sp.dma_start(aq_parts[part, :, bass.ds(x.head * SEQ + x.t * TILE, TILE)],
                                                 o[x.b][:]).then_inc(q_stored[x.b], 16)
                            elif x.kind == "g":
                                sp.wait_ge(gs_ready, FROM + x.m + 1)
                                sp.sem_inc(store_turn, 1)
                                sp.dma_start(ag[:, bass.ds(x.head * SEQ + x.t * TILE, TILE)],
                                             gs[x.b][:]).then_inc(g_stored[x.b], 16)
                            else:
                                sp.wait_ge(ilo_ready, FROM + x.m + 1)
                                for part, o in enumerate((ih, il)):
                                    sp.dma_start(iq_parts[part, :, bass.ds(x.pair * SEQ + x.t * TILE, TILE)],
                                                 o[x.b][:]).then_inc(i_stored[x.b], 16)
                for b in range(2):
                    sp.wait_ge(q_stored[b], FROM + ITER * QPI * 16)
                    sp.wait_ge(g_stored[b], FROM + ITER * QPI // 2 * 16)
                    sp.wait_ge(i_stored[b], FROM + ITER * NTILE * 16)

            @block.gpsimd
            def _(pool):
                nc.gpsimd.memset(eps[:], EPS).then_inc(const_ready, 1)
                nc.gpsimd.memset(ones[:], 1.0 / P).then_inc(const_ready, 1)
                with pool.Fori(0, ITER) as i:
                    for s in range(NI):
                        x = Item(i, s)
                        if x.kind == "q":
                            pool.wait_ge(qhi_ready, FROM + x.m + 1)
                            pool.wait_ge(q_stored[x.b], FROM + x.uses * 32)
                            nc.gpsimd.tensor_tensor(out=ql[x.b][:], in0=qn[x.b][:], in1=qh[x.b][:],
                                                    op=ALU.subtract).then_inc(qlo_ready, 1)

            def split_positions():
                at = 0
                for s in sorted(INSIDE):
                    for _, sl in INSIDE[s]:
                        yield s, at, sl, {4: 0, 0: 8, 1: 8, 2: 16, 3: 16}[sl]
                        at += 1

            @block.scalar
            def _(act):
                act.wait_ge(const_ready, FROM + 2)
                act.wait_ge(g_loaded, FROM + 16)
                for h in range(AH):
                    nc.scalar.activation(gqs[:, h:h + 1], gq[:], ACT.Copy,
                                         scale=P ** -0.5 * 2.0 ** (h + 1) / WSCALE).then_inc(gqs_ready, 1)

                def split(sl, b, loads, done):
                    act.wait_ge(w_loaded[b], FROM + loads)
                    if done is not None:
                        act.wait_ge(z_ready, FROM + done)
                    nc.scalar.activation(w_hi[sl][:], w_raw[b][:], ACT.Copy, scale=WSCALE).then_inc(hi_ready, 1)

                def norm_tail(x):
                    act.wait_ge(ms_ready, FROM + x.m + 1)
                    act.wait_ge(rin_ready, FROM + x.m)
                    nc.scalar.activation(lnm[:], pm[x.b][:], ACT.Ln, bias=eps[:]).then_inc(ln_ready, 1)
                    act.wait_ge(ln_ready, FROM + x.m + 1)
                    nc.scalar.activation(rin[x.b][:], lnm[:], ACT.Exp, scale=-0.5).then_inc(rin_ready, 1)
                    act.wait_ge(qn_ready, FROM + x.m + 1)
                    act.wait_ge(q_stored[x.b], FROM + x.uses * 32)
                    nc.scalar.activation(qh[x.b][:], qn[x.b][:], ACT.Copy).then_inc(qhi_ready, 1)

                for n, sl in enumerate(BEFORE):
                    split(sl, n % 2, (n // 2 + 1) * 16, None)
                with act.Fori(0, ITER // 2) as ii:
                    for half in range(2):
                        i = ii * 2 + half
                        for s in range(NI):
                            for s_, at, sl, done in split_positions():
                                if s_ == s:
                                    k = half * SPLITS + at
                                    split(sl, k % 2, (2 + ii * SPLITS + k // 2 + 1) * 16, i * NI + done)
                            x = Item(i, s)
                            act.wait_ge(z_ready, FROM + x.n + 1)
                            if x.kind == "q":
                                nc.scalar.activation(sq[x.b][:], pz[s % 4][:], ACT.Square,
                                                     scale=1.0 / WSCALE).then_inc(sq_ready, 1)
                            elif x.kind == "g":
                                act.wait_ge(g_stored[x.b], FROM + x.uses * 16)
                                nc.scalar.activation(gs[x.b][:], pz[s % 4][:], ACT.Silu,
                                                     scale=1.0 / WSCALE).then_inc(gs_ready, 1)
                                norm_tail(Item(i, s - 1))
                            else:
                                act.wait_ge(i_stored[x.b], FROM + x.uses * 32)
                                nc.scalar.activation(ih[x.b][:], pz[s % 4][:], ACT.Copy,
                                                     scale=1.0 / WSCALE).then_inc(ihi_ready, 1)

            @block.vector
            def _(dve):
                def split(sl, b, count):
                    dve.wait_ge(hi_ready, FROM + count + 1)
                    nc.vector.scalar_tensor_tensor(out=w_lo[sl][:], in0=w_raw[b][:], scalar=WSCALE,
                                                   in1=w_hi[sl][:], op0=ALU.mult,
                                                   op1=ALU.subtract).then_inc(lo_ready, 1)

                for n, sl in enumerate(BEFORE):
                    split(sl, n % 2, n)
                dve.wait_ge(gqs_ready, FROM + AH)
                with dve.Fori(0, ITER // 2) as ii:
                    for half in range(2):
                        i = ii * 2 + half
                        for s in range(NI):
                            for s_, at, sl, done in split_positions():
                                if s_ == s:
                                    split(sl, (half * SPLITS + at) % 2, i * SPLITS + at + 4)
                            x = Item(i, s)
                            if x.kind == "g":
                                y = Item(i, s - 1)
                                dve.wait_ge(rin_ready, FROM + y.m + 1)
                                nc.vector.scalar_tensor_tensor(
                                    out=qn[y.b][:], in0=pz[(s - 1) % 4][:], scalar=gqs[:, bass.ds(y.head, 1)],
                                    in1=rin[y.b][:], op0=ALU.mult, op1=ALU.mult).then_inc(qn_ready, 1)
                            elif x.kind == "i":
                                dve.wait_ge(ihi_ready, FROM + x.m + 1)
                                nc.vector.scalar_tensor_tensor(
                                    out=il[x.b][:], in0=pz[s % 4][:], scalar=1.0 / WSCALE, in1=ih[x.b][:],
                                    op0=ALU.mult, op1=ALU.subtract).then_inc(ilo_ready, 1)

            @block.tensor
            def _(pe):
                pe.wait_ge(const_ready, FROM + 2)
                used = {"q": qn_ready, "g": gs_ready, "i": ilo_ready}
                with pe.Fori(0, ITER) as i:
                    for s in range(NI):
                        x = Item(i, s)
                        need = {0: i * SPLITS + 2, 8: i * SPLITS + 4, 16: i * SPLITS + 5}
                        if s in need:
                            pe.wait_ge(lo_ready, FROM + need[s])
                        if s == 0:
                            pe.wait_ge(ilo_ready, FROM + i * NTILE)
                        if s >= 4:
                            y = Item(i, s - 4)
                            pe.wait_ge(used[y.kind], FROM + y.m + 1)
                        n = 0
                        sl = slot[x.kind, x.h]
                        for k in range(KD):
                            for w, m in ((w_hi, ut_hi), (w_hi, ut_lo), (w_lo, ut_hi)):
                                mm = nc.tensor.matmul(pz[s % 4][:], w[sl][:, k, :], m[:, k, x.t0:x.t0 + TILE],
                                                      start=n == 0, stop=n == 3 * KD - 1)
                                n += 1
                        mm.then_inc(z_ready, 1)
                        if x.kind == "g":
                            y = Item(i, s - 1)
                            pe.wait_ge(sq_ready, FROM + y.m + 1)
                            nc.tensor.matmul(pm[y.b][:], ones[:], sq[y.b][:], start=True,
                                             stop=True).then_inc(ms_ready, 1)


def attention(nc, aq_parts, iq_parts, ag, kt_hi, kt_lo, v_all, ik_hi, ik_lo, iw_all, oa_parts, ident):
    NB = SEQ // P
    NEG = -1.0e30
    LOWEST = -3.0e38

    def keys(n):
        return (n + 1) * P

    def tiles(n):
        return [(max(c, PAD), min(c + TILE, keys(n))) for c in range(0, keys(n), TILE)]

    attended = [(1,)] + [tuple(m for m in (n, n + 1) if m <= NB) for n in range(2, NB + 1, 2)]
    STEPS = [(a, s) for a, s in zip(attended, attended[1:] + [()])]

    def dotted_before(n):
        return sum(AH * len(tiles(m)) for m in range(1, n))

    def is_second(n):
        return any(n in a[1:] for a in attended)

    def dot_bank(n, i):
        return (qk + lg)[(i - dotted_before(n)) % 4] if is_second(n) else qk[i % 2]

    def row_of_set(n):
        mates = next(a for a in attended if n in a)
        before = sum(IH * len(tiles(m)) for m in range(2, mates[0]))
        return before + sum(len(tiles(m)) for m in mates if m < n), sum(len(tiles(m)) for m in mates)

    def scored_of_step(n):
        return next(scored_through(s or (NB,)) for a, s in STEPS if n in a)

    def scored_through(searched):
        return sum(IH * len(tiles(m)) for m in range(2, searched[-1] + 1))

    def split(n):
        return PAD + (keys(n) - PAD) * 9 // 16

    UPPER_BITS, LOWER_BITS = range(14, -1, -1), range(15, -1, -1)
    CANDS = len(UPPER_BITS) + len(LOWER_BITS) + 2
    PARTS = len(UPPER_BITS) + len(LOWER_BITS)

    def set_of(n):
        return n // 2 - 1

    def products_before(n):
        return sum(KVH * (m + 1) for m in range(1, n))

    def turned_before(n):
        return sum(KVH * (m + 2) for m in range(1, n))

    with ExitStack() as ctx:
        def sb(name, shape, dt=F32):
            return ctx.enter_context(nc.sbuf_tensor("a_" + name, shape, dt))

        def two(name, shape, dt=F32):
            return [sb(f"{name}{b}", shape, dt) for b in range(2)]

        sem = Semaphores(nc, ctx, "a_")

        def bank(name):
            return ctx.enter_context(nc.psum_tensor("a_" + name, [P, TILE], F32))

        q_hi, q_lo = two("q_hi", [P, AH, P], F16), two("q_lo", [P, AH, P], F16)
        iq = two("iq", [P, 2, IH // 2, P], F16)
        gate = two("gate", [P, AH, P])
        relu = [sb(f"relu{b}", [P, TILE]) for b in range(4)]
        score = two("score", [P, T])
        agree = two("agree", [P, T], I8)
        low = two("low", [P, T])
        junk = two("junk", [P, T], I8)
        bias = sb("bias", [P, T])
        prob = sb("prob", [P, AH, T])
        pt = two("pt", [P, TILE])
        mx = sb("mx", [P, AH, 5])
        mxr = sb("mxr", [P, AH])
        nb = sb("nb", [P, AH])
        nslope = sb("nslope", [P, AH])
        rows = sb("rows", [P, AH])
        rinv = sb("rinv", [P, AH])
        diag = sb("diag", [P, AG, P])
        rb = two("rb", [P, TILE])
        og = rb
        oh, ol = two("oh", [P, TILE], F16), two("ol", [P, TILE], F16)
        ones = sb("ones", [P, P])
        cnt, part, total, neg, sgn = (two(n, [P, 1]) for n in ("cnt", "part", "total", "neg", "sgn"))
        want, wanted, keep, cand, up = (two(n, [P, 1]) for n in ("want", "wanted", "keep", "cand", "up"))
        need, thr, sthr = (two(n, [P, 1]) for n in ("need", "thr", "sthr"))

        qk = [bank("qk0"), bank("qk1")]
        lg = [bank("lg0"), bank("lg1")]
        tp = [bank("tp0"), bank("tp1")]
        po = [bank("po0"), bank("po1")]

        q_loaded, iq_loaded = sem.two("q_loaded"), sem.two("iq_loaded")
        const_ready = sem("const_ready")
        lg_ready, relu_ready, sc_ready, sfill_ready = sem.many("lg_ready relu_ready sc_ready sfill_ready")
        dist_ready, bias_ready, bfill_ready = sem("dist_ready"), sem("bias_ready"), sem("bfill_ready")
        qk_ready, biased_ready, nb_ready, prob_ready = sem.many("qk_ready biased_ready nb_ready prob_ready")
        rinv_ready, diag_ready, tp_ready, pt_ready = sem.many("rinv_ready diag_ready tp_ready pt_ready")
        gr_ready, og_ready, ohi_ready, olo_ready = sem.many("gr_ready og_ready ohi_ready olo_ready")
        pv_done, step, stored = sem("pv_done"), sem("step"), sem.two("stored")
        found, cand_ready, part_ready = sem.two("found"), sem.two("cand_ready"), sem.two("part_ready")

        with nc.Block() as block:
            @block.sync
            def _(sp):
                def load(n):
                    b = n % 2
                    if n > 2:
                        sp.wait_ge(pv_done, products_before(n - 1))
                        sp.wait_ge(og_ready, KVH * (n - 2))
                    t = slice((n - 1) * P, n * P)
                    for src, dst in ((0, q_hi), (1, q_lo)):
                        sp.dma_start(dst[b][:], aq_parts[src].rearrange("p (h t) -> p h t", t=SEQ)[:, :, t]
                                     ).then_inc(q_loaded[b], 16)
                    sp.dma_start(gate[b][:], ag.rearrange("p (h t) -> p h t", t=SEQ)[:, :, t]
                                 ).then_inc(q_loaded[b], 16)

                def load_indexer(n):
                    b = n % 2
                    t = slice((n - 1) * P, n * P)
                    for half in range(2):
                        for odd in range(2):
                            sp.dma_start(iq[b][half * ID:(half + 1) * ID, odd, :, :],
                                         iq_parts[half, odd * ID:(odd + 1) * ID].rearrange(
                                             "p (h t) -> p h t", t=SEQ)[:, :, t]).then_inc(iq_loaded[b], 16)

                load_indexer(2)
                load(1)
                load_indexer(3)
                load(2)
                for (blocks, searched), (_, after) in zip(STEPS, STEPS[1:] + [((), ())]):
                    for n in after:
                        sp.wait_ge(lg_ready, scored_through(searched))
                        load_indexer(n)
                    for n in blocks:
                        for g in range(KVH):
                            sp.wait_ge(olo_ready, KVH * (n - 1) + g + 1)
                            for part_, o in enumerate((oh, ol)):
                                dst = oa_parts[part_].rearrange("p (h t) -> p h t", t=SEQ)
                                sp.dma_start(dst[:, g * AG:(g + 1) * AG, (n - 1) * P:n * P],
                                             o[g][:].rearrange("p (h t) -> p h t", t=P)).then_inc(stored[g], 16)
                        if n + 2 <= NB:
                            load(n + 2)
                for g in range(KVH):
                    sp.wait_ge(stored[g], NB * 32)

            LOADS, INDEXER_LOADS = 3 * 16, 4 * 16

            @block.gpsimd
            def _(pool):
                for h in range(AH):
                    nc.gpsimd.memset(nslope[:, h:h + 1], -2.0 ** -(h + 1)).then_inc(const_ready, 1)
                nc.gpsimd.memset(ones[:], 1.0).then_inc(const_ready, 1)
                nc.gpsimd.memset(prob[:, :, 0:PAD], 0.0).then_inc(const_ready, 1)

                def distances(n):
                    c = keys(n) - PAD
                    nc.gpsimd.iota(bias[:, PAD:keys(n)], pattern=[[1, c]], base=PAD - n * P, channel_multiplier=-1,
                                   allow_small_or_imprecise_dtypes=True).then_inc(dist_ready, 1)

                def causal(buf, n, fill):
                    d = buf[:, n * P:keys(n)]
                    return nc.gpsimd.affine_select(out=d, in_=d, compare_op=ALU.is_ge, fill=fill, base=0,
                                                   pattern=[[-1, P]], channel_multiplier=1)

                distances(1)
                pool.wait_ge(dist_ready, 1)
                causal(bias, 1, NEG).then_inc(bfill_ready, 1)

                def gated(n):
                    pool.wait_ge(rinv_ready, n)
                    if n == 1:
                        pool.wait_ge(const_ready, AH + 2)
                    for g in range(KVH):
                        if g:
                            pool.wait_ge(tp_ready, turned_before(n + 1) - KVH + g)
                        elif n > 1:
                            pool.wait_ge(tp_ready, turned_before(n))
                        h = slice(g * AG, (g + 1) * AG)
                        nc.gpsimd.tensor_tensor(out=diag[:], in0=ident[:, None, :].broadcast_to([P, AG, P]),
                                                in1=rinv[:, h, None].broadcast_to([P, AG, P]),
                                                op=ALU.mult).then_inc(diag_ready, 1)
                    for g in range(KVH):
                        pool.wait_ge(pt_ready, turned_before(n + 1) - KVH + g + 1)
                        pool.wait_ge(q_loaded[n % 2], (n + 1) // 2 * LOADS)
                        gr = gate[n % 2][:, g * AG:(g + 1) * AG, :]
                        nc.gpsimd.tensor_tensor(out=gr, in0=rb[g][:].rearrange("p (h t) -> p h t", t=P), in1=gr,
                                                op=ALU.mult).then_inc(gr_ready, 1)
                    for g in range(KVH):
                        pool.wait_ge(ohi_ready, KVH * (n - 1) + g + 1)
                        pool.wait_ge(stored[g], (n - 1) * 32)
                        nc.gpsimd.tensor_tensor(out=ol[g][:], in0=og[g][:], in1=oh[g][:],
                                                op=ALU.subtract).then_inc(olo_ready, 1)

                for blocks, searched in STEPS:
                    for n in blocks[1:]:
                        pool.wait_ge(biased_ready, dotted_before(n))
                        distances(n)
                    for n in searched:
                        pool.wait_ge(sc_ready, scored_through(searched))
                        causal(score[n % 2], n, LOWEST).then_inc(sfill_ready, 1)
                    for n in blocks[1:]:
                        pool.wait_ge(bias_ready, n - 1)
                        causal(bias, n, NEG).then_inc(bfill_ready, 1)
                    gated(blocks[0])
                    for n in searched[:1]:
                        pool.wait_ge(biased_ready, dotted_before(n))
                        distances(n)
                    for n in blocks[1:]:
                        gated(n)
                    for n in searched[:1]:
                        pool.wait_ge(bias_ready, n - 1)
                        causal(bias, n, NEG).then_inc(bfill_ready, 1)

            @block.scalar
            def _(act):
                def relus(n, h):
                    first, row = row_of_set(n)
                    for t, (a, b) in enumerate(tiles(n)):
                        i = first + h * row + t
                        act.wait_ge(lg_ready, i + 1)
                        if i >= 4:
                            act.wait_ge(sc_ready, i - 3)
                        nc.scalar.activation(relu[i % 4][:, 0:b - a], lg[i % 2][:, 0:b - a],
                                             ACT.Relu).then_inc(relu_ready, 1)

                def exponentials(n, h):
                    act.wait_ge(nb_ready, KVH * (n - 1) + h // AG + 1)
                    p = prob[:, h, PAD:keys(n)]
                    nc.scalar.activation(p, p, ACT.Exp, bias=nb[:, h:h + 1], scale=2.0 ** -(h + 1),
                                         accum_out=rows[:, h:h + 1]).then_inc(prob_ready, 1)

                def turned(n, items):
                    for j in items:
                        i = turned_before(n) + j
                        act.wait_ge(tp_ready, i + 1)
                        if j < KVH * (n + 1):
                            if j >= 2:
                                act.wait_ge(pv_done, products_before(n) + j - 1)
                            elif n > 1:
                                act.wait_ge(pv_done, products_before(n))
                            nc.scalar.activation(pt[i % 2][:], tp[i % 2][:], ACT.Copy).then_inc(pt_ready, 1)
                        else:
                            if n > 1:
                                act.wait_ge(olo_ready, KVH * (n - 1))
                            nc.scalar.activation(rb[j - KVH * (n + 1)][:], tp[i % 2][:],
                                                 ACT.Copy).then_inc(pt_ready, 1)

                def passes(searched, n, bits, cands):
                    items = KVH * (n + 2) if n else 0
                    for q in range(len(bits)):
                        for m in searched:
                            ch = m % 2
                            act.wait_ge(cand_ready[ch], set_of(m) * CANDS + cands + q + 1)
                            view = low[ch] if bits is LOWER_BITS else score[ch]
                            part_keys = view[:, split(m):keys(m)]
                            if bits is UPPER_BITS:
                                part_keys = part_keys.bitcast(I16).rearrange("p (c two) -> p c two", two=2)[:, :, 1]
                            nc.scalar.activation(junk[ch][:, split(m):keys(m)], part_keys, ACT.Sign,
                                                 bias=cand[ch][:], scale=-1.0,
                                                 accum_out=part[ch][:]).then_inc(part_ready[ch], 1)
                        turned(n, range(items * q // len(bits), items * (q + 1) // len(bits)))

                def upper_outputs(n):
                    for g in range(KVH):
                        act.wait_ge(og_ready, KVH * (n - 1) + g + 1)
                        act.wait_ge(stored[g], (n - 1) * 32)
                        nc.scalar.activation(oh[g][:], og[g][:], ACT.Copy).then_inc(ohi_ready, 1)

                for blocks, searched in STEPS:
                    n = blocks[0]
                    for h in range(IH):
                        for m in searched:
                            relus(m, h)
                        if h > AG:
                            exponentials(n, h - AG - 1)
                    for h in range(AG - 1, AH):
                        exponentials(n, h)
                    passes(searched, n, UPPER_BITS, 0)
                    upper_outputs(n)
                    for n in blocks[1:]:
                        for h in range(AH):
                            exponentials(n, h)
                    n = blocks[1] if blocks[1:] else None
                    passes(searched, n, LOWER_BITS, len(UPPER_BITS) + 1)
                    if n:
                        upper_outputs(n)

            @block.vector
            def _(dve):
                done = [0]

                def then(ins):
                    done[0] += 1
                    ins.then_inc(step, 1)
                    dve.wait_ge(step, done[0])

                V = nc.vector
                dve.wait_ge(const_ready, AH + 2)

                def scores(n, h):
                    first, row = row_of_set(n)
                    s = score[n % 2]
                    for t, (a, b) in enumerate(tiles(n)):
                        i = first + h * row + t
                        dve.wait_ge(relu_ready, i + 1)
                        iw = iw_all[:, n, h:h + 1]
                        r = relu[i % 4][:, 0:b - a]
                        if h == 0:
                            V.tensor_scalar(s[:, a:b], r, iw, None, ALU.mult).then_inc(sc_ready, 1)
                        else:
                            dve.wait_ge(sc_ready, i - row + 1)
                            V.scalar_tensor_tensor(out=s[:, a:b], in0=r, scalar=iw, in1=s[:, a:b],
                                                   op0=ALU.mult, op1=ALU.add).then_inc(sc_ready, 1)

                def reciprocals(n):
                    dve.wait_ge(prob_ready, AH * n)
                    dve.wait_ge(diag_ready, KVH * (n - 1))
                    V.reciprocal(rinv[:], rows[:]).then_inc(rinv_ready, 1)

                results = [0, 0]

                def last(ch):
                    dve.wait_ge(found[ch], results[ch])

                def result(ch, ins):
                    results[ch] += 1
                    ins.then_inc(found[ch], 1)

                def count(ch, x, limit, op):
                    result(ch, V.tensor_scalar(junk[ch][:, PAD:PAD + x.shape[1]], x, limit, None, op, ALU.add,
                                               accum_out=cnt[ch][:]))

                def halves(n):
                    s = score[n % 2][:, PAD:keys(n)]
                    return (s.bitcast(I16).rearrange("p (c two) -> p c two", two=2)[:, :, 1],
                            s.bitcast(U16).rearrange("p (c two) -> p c two", two=2)[:, :, 0])

                def signs(searched):
                    both = [(n % 2, n, keys(n) - PAD) for n in searched]
                    for ch, n, c in both:
                        dve.wait_ge(sfill_ready, n - 1)
                        count(ch, score[ch][:, PAD:keys(n)], 0.0, ALU.is_ge)
                    for ch, n, c in both:
                        last(ch)
                        result(ch, V.tensor_scalar(neg[ch][:], cnt[ch][:], float(TOPK), None, ALU.is_lt))
                    for ch, n, c in both:
                        last(ch)
                        V.tensor_scalar(want[ch][:], neg[ch][:], float(c + 1 - 2 * TOPK), float(TOPK),
                                        ALU.mult, ALU.add)
                        result(ch, V.tensor_scalar(sgn[ch][:], neg[ch][:], -2.0, 1.0, ALU.mult, ALU.add))
                    for ch, n, c in both:
                        last(ch)
                        V.tensor_scalar(wanted[ch][:], want[ch][:], 0.5 * (keys(n) - split(n)), None, ALU.subtract)
                        s = score[ch][:, PAD:keys(n)]
                        result(ch, V.tensor_scalar(s, s, sgn[ch][:], 0.0, ALU.mult, ALU.add))
                    for ch, n, c in both:
                        last(ch)
                        V.memset(cand[ch][:], 2.0 ** 14 - 0.5).then_inc(cand_ready[ch], 1)

                def bits_of(searched, bits, cands, parts, n):
                    for q, bit in enumerate(bits):
                        for m in searched:
                            ch = m % 2
                            dve.wait_ge(cand_ready[ch], set_of(m) * CANDS + cands + q + 1)
                            x = halves(m)[0] if bits is UPPER_BITS else low[ch][:, PAD:keys(m)]
                            count(ch, x[:, 0:split(m) - PAD], cand[ch][:], ALU.is_ge)
                        for m in searched:
                            ch = m % 2
                            last(ch)
                            dve.wait_ge(part_ready[ch], set_of(m) * PARTS + parts + q + 1)
                            result(ch, V.scalar_tensor_tensor(out=total[ch][:], in0=part[ch][:], scalar=-0.5,
                                                              in1=cnt[ch][:], op0=ALU.mult, op1=ALU.add))
                        for m in searched:
                            ch = m % 2
                            last(ch)
                            result(ch, V.tensor_scalar(keep[ch][:], total[ch][:], wanted[ch][:], 0.5,
                                                       ALU.is_ge, ALU.subtract))
                        for m in searched:
                            ch = m % 2
                            last(ch)
                            V.scalar_tensor_tensor(out=cand[ch][:], in0=keep[ch][:], scalar=2.0 ** bit,
                                                   in1=cand[ch][:], op0=ALU.mult,
                                                   op1=ALU.add).then_inc(cand_ready[ch], 1)
                        if q == RECIPROCALS_AT and n:
                            reciprocals(n)

                def agreeing(searched):
                    for n in searched:
                        ch = n % 2
                        dve.wait_ge(cand_ready[ch], set_of(n) * CANDS + len(UPPER_BITS) + 1)
                        V.tensor_scalar(up[ch][:], cand[ch][:], 1.0, None, ALU.mult)
                        count(ch, halves(n)[0], cand[ch][:], ALU.is_gt)
                    for n in searched:
                        ch = n % 2
                        last(ch)
                        V.scalar_tensor_tensor(out=wanted[ch][:], in0=wanted[ch][:], scalar=1.0, in1=cnt[ch][:],
                                               op0=ALU.mult, op1=ALU.subtract)
                        result(ch, V.tensor_scalar(agree[ch][:, PAD:keys(n)], halves(n)[0], up[ch][:], None,
                                                   ALU.is_equal))
                    for n in searched:
                        ch = n % 2
                        last(ch)
                        result(ch, V.scalar_tensor_tensor(out=low[ch][:, PAD:keys(n)], in0=halves(n)[1], scalar=1.0,
                                                          in1=agree[ch][:, PAD:keys(n)], op0=ALU.add, op1=ALU.mult))
                    for n in searched:
                        ch = n % 2
                        last(ch)
                        V.memset(cand[ch][:], 2.0 ** 15 + 0.5).then_inc(cand_ready[ch], 1)

                def unselected(searched):
                    for n in searched:
                        ch = n % 2
                        dve.wait_ge(cand_ready[ch], (set_of(n) + 1) * CANDS)
                        V.tensor_scalar(thr[ch][:].bitcast(U16)[:, 0:1], cand[ch][:], 1.0, None, ALU.subtract)
                        V.tensor_scalar(thr[ch][:].bitcast(I16)[:, 1:2], up[ch][:], 1.0, None, ALU.mult)
                        s = score[ch][:, PAD:keys(n)]
                        result(ch, V.tensor_scalar(s, s, sgn[ch][:], None, ALU.mult))
                    for n in searched:
                        ch = n % 2
                        last(ch)
                        result(ch, V.tensor_tensor(out=sthr[ch][:], in0=thr[ch][:], in1=sgn[ch][:], op=ALU.mult))
                    for n in searched:
                        ch, e = n % 2, keys(n)
                        last(ch)
                        V.tensor_scalar(agree[ch][:, PAD:e], score[ch][:, PAD:e], sthr[ch][:], None, ALU.is_equal)
                        count(ch, score[ch][:, PAD:e], sthr[ch][:], ALU.is_gt)
                    for n in searched:
                        ch, e = n % 2, keys(n)
                        last(ch)
                        V.tensor_scalar(need[ch][:], cnt[ch][:], -1.0, float(TOPK), ALU.mult, ALU.add)
                        tie = agree[ch][:, PAD:e]
                        result(ch, V.tensor_tensor_scan(out=low[ch][:, PAD:e], data0=tie, data1=tie, initial=0.0,
                                                        op0=ALU.add, op1=ALU.max))
                    for n in searched:
                        ch, e = n % 2, keys(n)
                        last(ch)
                        result(ch, V.scalar_tensor_tensor(out=low[ch][:, PAD:e], in0=low[ch][:, PAD:e],
                                                          scalar=need[ch][:], in1=agree[ch][:, PAD:e],
                                                          op0=ALU.is_gt, op1=ALU.mult))
                    for n in searched:
                        ch, e = n % 2, keys(n)
                        last(ch)
                        result(ch, V.scalar_tensor_tensor(out=low[ch][:, PAD:e], in0=score[ch][:, PAD:e],
                                                          scalar=sthr[ch][:], in1=low[ch][:, PAD:e],
                                                          op0=ALU.is_lt, op1=ALU.add))

                def biases(n):
                    ch, e = n % 2, keys(n)
                    last(ch)
                    dve.wait_ge(dist_ready, n)
                    V.scalar_tensor_tensor(out=bias[:, PAD:e], in0=low[ch][:, PAD:e], scalar=NEG, in1=bias[:, PAD:e],
                                           op0=ALU.mult, op1=ALU.add).then_inc(bias_ready, 1)

                def biased(n, h):
                    if h == 0:
                        dve.wait_ge(bfill_ready, n)
                        if n > 1:
                            dve.wait_ge(pv_done, products_before(n))
                    nt = len(tiles(n))
                    for t, (a, b) in enumerate(tiles(n)):
                        i = dotted_before(n) + h * nt + t
                        dve.wait_ge(qk_ready, i + 1)
                        V.tensor_tensor_reduce(out=prob[:, h, a:b], in0=dot_bank(n, i)[:, 0:b - a],
                                               in1=bias[:, a:b], scale=1.0, scalar=LOWEST, op0=ALU.add,
                                               op1=ALU.max, accum_out=mx[:, h, t:t + 1]
                                               ).then_inc(biased_ready, 1)
                    if h % AG == AG - 1:
                        g = slice(h + 1 - AG, h + 1)
                        dve.wait_ge(biased_ready, dotted_before(n) + (h + 1) * nt)
                        then(V.tensor_reduce(mxr[:, g], mx[:, g, 0:nt], AX.X, ALU.max))
                        V.tensor_tensor(out=nb[:, g], in0=mxr[:, g], in1=nslope[:, g],
                                        op=ALU.mult).then_inc(nb_ready, 1)

                def outputs(n):
                    for g in range(KVH):
                        dve.wait_ge(gr_ready, KVH * (n - 1) + g + 1)
                        dve.wait_ge(pv_done, products_before(n) + (g + 1) * (n + 1))
                        if n > 1:
                            dve.wait_ge(olo_ready, KVH * (n - 1))
                        V.tensor_tensor(out=og[g][:].rearrange("p (h t) -> p h t", t=P),
                                        in0=po[g][:].rearrange("p (h t) -> p h t", t=P),
                                        in1=gate[n % 2][:, g * AG:(g + 1) * AG, :],
                                        op=ALU.mult).then_inc(og_ready, 1)

                RECIPROCALS_AT = 5
                for blocks, searched in STEPS:
                    n = blocks[0]
                    for h in range(AH):
                        biased(n, h)
                        for m in searched:
                            scores(m, h)
                    for m in blocks[1:]:
                        biases(m)
                    if searched:
                        signs(searched)
                        bits_of(searched, UPPER_BITS, 0, 0, n)
                    else:
                        reciprocals(n)
                    outputs(n)
                    n = blocks[1] if blocks[1:] else None
                    if n:
                        for h in range(AH):
                            biased(n, h)
                    if searched:
                        agreeing(searched)
                        bits_of(searched, LOWER_BITS, len(UPPER_BITS) + 1, len(UPPER_BITS), n)
                    elif n:
                        reciprocals(n)
                    if n:
                        outputs(n)
                    if searched:
                        unselected(searched)
                        biases(searched[0])

            @block.tensor
            def _(pe):
                def logits(n, h):
                    first, row = row_of_set(n)
                    if h == 0:
                        pe.wait_ge(iq_loaded[n % 2], n // 2 * INDEXER_LOADS)
                    w = iq[n % 2][:, h % 2, h // 2, :]
                    for t, (a, b) in enumerate(tiles(n)):
                        i = first + h * row + t
                        if i >= 2:
                            pe.wait_ge(relu_ready, i - 1)
                        nc.tensor.matmul(lg[i % 2][:, 0:b - a], w, ik_hi[:, a:b], start=True, stop=False)
                        nc.tensor.matmul(lg[i % 2][:, 0:b - a], w[0:ID], ik_lo[:, a:b],
                                         start=False, stop=True).then_inc(lg_ready, 1)

                def dots(n, h):
                    if h == 0:
                        pe.wait_ge(q_loaded[n % 2], (n + 1) // 2 * LOADS)
                    for t, (a, b) in enumerate(tiles(n)):
                        i = dotted_before(n) + h * len(tiles(n)) + t
                        second = is_second(n)
                        if i - dotted_before(n) < (4 if second else 2):
                            if n > 1:
                                pe.wait_ge(biased_ready, dotted_before(n))
                            if second:
                                pe.wait_ge(relu_ready, scored_of_step(n))
                        else:
                            pe.wait_ge(biased_ready, i - 3 if second else i - 1)
                        o = dot_bank(n, i)[:, 0:b - a]
                        g = h // AG
                        nc.tensor.matmul(o, q_hi[n % 2][:, h, :], kt_hi[:, g, a:b], start=True, stop=False)
                        nc.tensor.matmul(o, q_hi[n % 2][:, h, :], kt_lo[:, g, a:b], start=False, stop=False)
                        nc.tensor.matmul(o, q_lo[n % 2][:, h, :], kt_hi[:, g, a:b],
                                         start=False, stop=True).then_inc(qk_ready, 1)

                def values(n):
                    i = turned_before(n)

                    def turn(j, i):
                        g, k = divmod(j, n + 1)
                        pe.wait_ge(prob_ready, AH * (n - 1) + AG * (g + 1))
                        if i >= 2:
                            pe.wait_ge(pt_ready, i - 1)
                        for h in range(AG):
                            mm = nc.tensor.transpose(tp[i % 2][:, h * P:(h + 1) * P],
                                                     prob[:, g * AG + h, k * P:(k + 1) * P], ident[:])
                        mm.then_inc(tp_ready, 1)

                    total = KVH * (n + 1)
                    turn(0, i)
                    for j in range(total):
                        if j + 1 < total:
                            turn(j + 1, i + j + 1)
                        g, k = divmod(j, n + 1)
                        pe.wait_ge(pt_ready, i + j + 1)
                        if n > 1 and k == 0:
                            pe.wait_ge(og_ready, KVH * (n - 2) + g + 1)
                        mm = nc.tensor.matmul(po[g][:], v_all[:, k, g * P:(g + 1) * P], pt[(i + j) % 2][:],
                                              start=k == 0, stop=k == n)
                        mm.then_inc(pv_done, 1)
                    i += total
                    for g in range(KVH):
                        pe.wait_ge(diag_ready, KVH * (n - 1) + g + 1)
                        pe.wait_ge(pt_ready, i - 1)
                        nc.tensor.matmul(tp[i % 2][:], ones[:], diag[:].rearrange("p h q -> p (h q)"),
                                         start=True, stop=True).then_inc(tp_ready, 1)
                        i += 1

                pe.wait_ge(const_ready, AH + 2)
                for blocks, searched in STEPS:
                    for h in range(AH):
                        dots(blocks[0], h)
                        for m in searched:
                            logits(m, h)
                    values(blocks[0])
                    for n in blocks[1:]:
                        for h in range(AH):
                            dots(n, h)
                        values(n)


def merge_recurrent(nc, w_cols, w_r, ut_hi, ut_lo, ogr, merged_r, gate_a):
    KINDS = "gay"
    NI = len(KINDS) * NTILE
    with ExitStack() as ctx:
        def sb(name, shape, dt=F32):
            return ctx.enter_context(nc.sbuf_tensor("mr_" + name, shape, dt))

        sem = Semaphores(nc, ctx, "mr_")

        og_hi, og_lo = sb("og_hi", [P, RH * SEQ], F16), sb("og_lo", [P, RH * SEQ], F16)
        w_raw = [sb(f"w_raw{s}", [P, KD, P]) for s in range(3)]
        w_hi = [sb(f"w_hi{s}", [P, KD, P], F16) for s in range(3)]
        w_lo = [sb(f"w_lo{s}", [P, KD, P], F16) for s in range(3)]
        sg = [sb(f"sg{b}", [P, TILE]) for b in range(NTILE)]
        sa = [sb(f"sa{b}", [P, TILE]) for b in range(2)]
        mr = [sb(f"mr{b}", [P, TILE]) for b in range(2)]
        pz = [ctx.enter_context(nc.psum_tensor(f"mr_pz{b}", [P, TILE], F32)) for b in range(4)]
        w_loaded = [sem(f"w_loaded{s}") for s in range(3)]
        hi_ready, lo_ready, z_ready = sem("hi_ready"), sem("lo_ready"), sem("z_ready")
        load_turn = sem("load_turn")
        sg_ready, sa_ready, mr_ready = sem("sg_ready"), sem("sa_ready"), sem("mr_ready")
        a_stored, y_stored = sem.two("a_stored"), sem.two("y_stored")

        og_loaded = sem("og_loaded")
        w_rc = w_r.rearrange("(k p) n -> p k n", p=P)
        SOURCE = [(w_cols, C_MR), (w_cols, C_MA), (w_rc, 0)]
        FREED = [NTILE, 2 * NTILE, 3 * NTILE]
        SPLIT_AT = {1: (2, 0), NTILE + 1: (0, 1), 2 * NTILE + 1: (1, 1)}

        def all_steps(eng, body):
            with eng.Fori(0, KD - 1) as i:
                body(i, False)
            body(KD - 1, True)

        sem.start()
        with nc.Block() as block:
            @block.sync
            def _(sp):
                def load(s, i):
                    src, c = SOURCE[s]
                    sp.dma_start(w_raw[s][:], src[:, :, bass.ds(i * P + c, P)]).then_inc(w_loaded[s], 16)

                for s in range(3):
                    load(s, 0)
                for part, dst in enumerate((og_hi, og_lo)):
                    for h in range(RH):
                        c = slice(h * SEQ, (h + 1) * SEQ)
                        sp.dma_start(dst[:, c], ogr[part, :, c]).then_inc(og_loaded, 16)

                def body(i, last):
                    if not last:
                        for s in range(2):
                            sp.wait_ge(lo_ready, FROM + i * 3 + s + 1)
                            load(s, i + 1)
                    for s in range(NI):
                        kind, t = KINDS[s // NTILE], s % NTILE
                        c = bass.ds(i * SEQ + t * TILE, TILE)
                        if kind == "a":
                            sp.wait_ge(sa_ready, FROM + i * NTILE + t + 1)
                            sp.dma_start(gate_a[:, c], sa[t % 2][:]).then_inc(a_stored[t % 2], 16)
                        if kind == "y":
                            if t == 0 and not last:
                                sp.wait_ge(lo_ready, FROM + i * 3 + 3)
                                sp.sem_inc(load_turn, 1)
                                load(2, i + 1)
                            sp.wait_ge(mr_ready, FROM + i * NTILE + t + 1)
                            sp.dma_start(merged_r[:, c], mr[t % 2][:]).then_inc(y_stored[t % 2], 16)
                all_steps(sp, body)
                for b in range(2):
                    sp.wait_ge(a_stored[b], FROM + KD * NTILE // 2 * 16)
                    sp.wait_ge(y_stored[b], FROM + KD * NTILE // 2 * 16)

            @block.scalar
            def _(act):
                def split(s, i, freed):
                    act.wait_ge(w_loaded[s], FROM + (i + 1) * 16)
                    act.wait_ge(z_ready, FROM + freed)
                    nc.scalar.activation(w_hi[s][:], w_raw[s][:], ACT.Copy, scale=WSCALE).then_inc(hi_ready, 1)

                split(0, 0, 0)
                split(1, 0, 0)

                def body(i, last):
                    for s in range(NI):
                        if s in SPLIT_AT:
                            sl, ahead = SPLIT_AT[s]
                            if not (last and ahead):
                                split(sl, i + ahead, i * NI + (FREED[sl] if ahead else 0))
                        kind, t = KINDS[s // NTILE], s % NTILE
                        if kind == "y":
                            continue
                        act.wait_ge(z_ready, FROM + i * NI + s + 1)
                        if kind == "g":
                            act.wait_ge(mr_ready, FROM + i * NTILE)
                            nc.scalar.activation(sg[t][:], pz[s % 4][:], ACT.Sigmoid,
                                                 scale=1.0 / WSCALE).then_inc(sg_ready, 1)
                        else:
                            act.wait_ge(a_stored[t % 2], FROM + (i * 2 + t // 2) * 16)
                            nc.scalar.activation(sa[t % 2][:], pz[s % 4][:], ACT.Sigmoid,
                                                 scale=1.0 / WSCALE).then_inc(sa_ready, 1)
                all_steps(act, body)

            @block.vector
            def _(dve):
                def split(s, count):
                    dve.wait_ge(hi_ready, FROM + count)
                    nc.vector.scalar_tensor_tensor(out=w_lo[s][:], in0=w_raw[s][:], scalar=WSCALE, in1=w_hi[s][:],
                                                   op0=ALU.mult, op1=ALU.subtract).then_inc(lo_ready, 1)

                split(0, 1)
                split(1, 2)

                def body(i, last):
                    for s in range(NI):
                        if s in SPLIT_AT:
                            sl, ahead = SPLIT_AT[s]
                            if not (last and ahead):
                                split(sl, i * 3 + {2: 3, 0: 4, 1: 5}[sl])
                        if KINDS[s // NTILE] == "y":
                            t = s % NTILE
                            dve.wait_ge(z_ready, FROM + i * NI + s + 1)
                            dve.wait_ge(sg_ready, FROM + i * NTILE + t + 1)
                            dve.wait_ge(y_stored[t % 2], FROM + (i * 2 + t // 2) * 16)
                            nc.vector.scalar_tensor_tensor(out=mr[t % 2][:], in0=pz[s % 4][:], scalar=1.0 / WSCALE,
                                                           in1=sg[t][:], op0=ALU.mult,
                                                           op1=ALU.mult).then_inc(mr_ready, 1)
                all_steps(dve, body)

            @block.tensor
            def _(pe):
                def body(i, last):
                    for s in range(NI):
                        kind, t = KINDS[s // NTILE], s % NTILE
                        if t == 0:
                            pe.wait_ge(lo_ready, FROM + i * 3 + s // NTILE + 1)
                            if kind == "y":
                                pe.wait_ge(og_loaded, FROM + 2 * RH * 16)
                        if kind == "g":
                            pe.wait_ge(mr_ready, FROM + i * NTILE)
                        elif kind == "a":
                            pe.wait_ge(sg_ready, FROM + i * NTILE + t + 1)
                        else:
                            pe.wait_ge(sa_ready, FROM + i * NTILE + t + 1)
                        n = 0
                        for k in range(KD):
                            if kind == "y":
                                c = slice(k * SEQ + t * TILE, k * SEQ + (t + 1) * TILE)
                                hi, lo = og_hi[:, c], og_lo[:, c]
                            else:
                                c = slice(P + t * TILE, P + (t + 1) * TILE)
                                hi, lo = ut_hi[:, k, c], ut_lo[:, k, c]
                            sl = s // NTILE
                            for w, m in ((w_hi, hi), (w_hi, lo), (w_lo, hi)):
                                mm = nc.tensor.matmul(pz[s % 4][:], w[sl][:, k, :], m,
                                                      start=n == 0, stop=n == 3 * KD - 1)
                                n += 1
                        mm.then_inc(z_ready, 1)
                all_steps(pe, body)


def merge_and_project(nc, x, w_a, w_out, oa_parts, merged_r, gate_a, out):
    with ExitStack() as ctx:
        def sb(name, shape, dt=F32):
            return ctx.enter_context(nc.sbuf_tensor("mo_" + name, shape, dt))

        sem = Semaphores(nc, ctx, "mo_")

        og_hi, og_lo = sb("og_hi", [P, AH * SEQ], F16), sb("og_lo", [P, AH * SEQ], F16)
        m_hi, m_lo = sb("m_hi", [P, KD, SEQ], F16), sb("m_lo", [P, KD, SEQ], F16)
        w_raw = [sb(f"w_raw{b}", [P, KD, P]) for b in range(2)]
        w_hi = [sb(f"w_hi{b}", [P, KD, P], F16) for b in range(2)]
        w_lo = [sb(f"w_lo{b}", [P, KD, P], F16) for b in range(2)]
        wo_hi, wo_lo = sb("wo_hi", [P, KD, D], F16), sb("wo_lo", [P, KD, D], F16)
        rp = [sb(f"rp{b}", [P, TILE]) for b in range(2)]
        ga = [sb(f"ga{b}", [P, TILE]) for b in range(2)]
        ya = [sb(f"ya{b}", [P, TILE]) for b in range(2)]
        mg = [sb(f"mg{b}", [P, TILE]) for b in range(2)]
        xw = [sb(f"xw{b}", [P, D]) for b in range(2)]
        pz = [ctx.enter_context(nc.psum_tensor(f"mo_pz{b}", [P, TILE], F32)) for b in range(4)]
        w_loaded, t_loaded, x_loaded = (sem.two(n) for n in ("w_loaded", "t_loaded", "x_loaded"))
        hi_ready, lo_ready, z_ready = sem("hi_ready"), sem("lo_ready"), sem("z_ready")
        ya_ready, mg_ready, mhi_ready, mlo_ready = sem.many("ya_ready mg_ready mhi_ready mlo_ready")
        load_turn = sem("load_turn")
        o_ready, y_ready, stored = sem("o_ready"), sem("y_ready"), sem.two("stored")

        og_loaded = [sem(f"og_loaded{h}") for h in range(AH)]
        w_ac = w_a.rearrange("(k p) n -> p k n", p=P)
        w_oc = w_out.rearrange("(k p) n -> p k n", p=P)

        sem.start()
        def feature_tiles(eng, body):
            with eng.Fori(0, KD // 2 - 1) as ii:
                for b in range(2):
                    body(ii * 2 + b, b, False)
            body(KD - 2, 0, False)
            body(KD - 1, 1, True)

        SPLIT_AT = 1

        with nc.Block() as block:
            @block.sync
            def _(sp):
                def weights(i):
                    sp.wait_ge(lo_ready, FROM + i * 2)
                    sp.sem_inc(load_turn, 1)
                    sp.dma_start(w_raw[0][:], w_ac[:, :, bass.ds(i * P, P)]).then_inc(w_loaded[0], 16)
                    sp.dma_start(w_raw[1][:], w_oc[:, :, bass.ds(i * P, P)]).then_inc(w_loaded[1], 16)

                def body(i, b, last):
                    if not last:
                        weights(i + 1)
                    for t in range(NTILE):
                        c = bass.ds(i * SEQ + t * TILE, TILE)
                        sp.wait_ge(mg_ready, FROM + i * NTILE + max(0, t - 1))
                        sp.sem_inc(load_turn, 1)
                        sp.dma_start(rp[t % 2][:], merged_r[:, c]).then_inc(t_loaded[t % 2], 16)
                        sp.dma_start(ga[t % 2][:], gate_a[:, c]).then_inc(t_loaded[t % 2], 16)

                weights(0)
                feature_tiles(sp, body)

            @block.gpsimd
            def _(pool):
                with pool.Fori(0, KD) as i:
                    for t in range(NTILE + 1):
                        if t < NTILE:
                            pool.wait_ge(ya_ready, FROM + i * NTILE + t + 1)
                            pool.wait_ge(mlo_ready, FROM + i * NTILE + max(0, t - 1))
                            nc.gpsimd.tensor_tensor(out=mg[t % 2][:], in0=ya[t % 2][:], in1=rp[t % 2][:],
                                                    op=ALU.add).then_inc(mg_ready, 1)
                        if t:
                            pool.wait_ge(mhi_ready, FROM + i * NTILE + t)
                            c = slice((t - 1) * TILE, t * TILE)
                            nc.gpsimd.tensor_tensor(out=m_lo[:, bass.ds(i, 1), c], in0=mg[(t - 1) % 2][:, None, :],
                                                    in1=m_hi[:, bass.ds(i, 1), c], op=ALU.subtract
                                                    ).then_inc(mlo_ready, 1)

            @block.scalar
            def _(act):
                for h in range(AH):
                    c = slice(h * SEQ, (h + 1) * SEQ)
                    for part, dst in enumerate((og_hi, og_lo)):
                        act.dma_start(dst[:, c], oa_parts[part, :, c]).then_inc(og_loaded[h], 16)

                def split(i, b):
                    act.wait_ge(w_loaded[0], FROM + (i + 1) * 16)
                    nc.scalar.activation(w_hi[b][:], w_raw[0][:], ACT.Copy, scale=WSCALE).then_inc(hi_ready, 1)
                    act.wait_ge(w_loaded[1], FROM + (i + 1) * 16)
                    nc.scalar.activation(wo_hi[:, :, bass.ds(i * P, P)], w_raw[1][:], ACT.Copy,
                                         scale=WSCALE).then_inc(hi_ready, 1)

                def body(i, b, last):
                    for t in range(NTILE):
                        act.wait_ge(mg_ready, FROM + i * NTILE + t + 1)
                        nc.scalar.activation(m_hi[:, bass.ds(i, 1), t * TILE:(t + 1) * TILE],
                                             mg[t % 2][:, None, :], ACT.Copy).then_inc(mhi_ready, 1)
                        if t == SPLIT_AT and not last:
                            split(i + 1, 1 - b)

                split(0, 0)
                feature_tiles(act, body)

            @block.vector
            def _(dve):
                def split(i, b):
                    dve.wait_ge(hi_ready, FROM + i * 2 + 1)
                    nc.vector.scalar_tensor_tensor(out=w_lo[b][:], in0=w_raw[0][:], scalar=WSCALE,
                                                   in1=w_hi[b][:], op0=ALU.mult,
                                                   op1=ALU.subtract).then_inc(lo_ready, 1)
                    dve.wait_ge(hi_ready, FROM + i * 2 + 2)
                    c = bass.ds(i * P, P)
                    nc.vector.scalar_tensor_tensor(out=wo_lo[:, :, c], in0=w_raw[1][:], scalar=WSCALE,
                                                   in1=wo_hi[:, :, c], op0=ALU.mult,
                                                   op1=ALU.subtract).then_inc(lo_ready, 1)

                def body(i, b, last):
                    for t in range(NTILE):
                        dve.wait_ge(z_ready, FROM + i * NTILE + t + 1)
                        dve.wait_ge(t_loaded[t % 2], FROM + (i * 2 + t // 2 + 1) * 32)
                        nc.vector.scalar_tensor_tensor(out=ya[t % 2][:], in0=pz[t][:], scalar=1.0 / WSCALE,
                                                       in1=ga[t % 2][:], op0=ALU.mult,
                                                       op1=ALU.mult).then_inc(ya_ready, 1)
                        if t == SPLIT_AT and not last:
                            split(i + 1, 1 - b)

                split(0, 0)
                feature_tiles(dve, body)

            @block.tensor
            def _(pe):
                def body(i, b, last):
                    pe.wait_ge(lo_ready, FROM + i * 2 + 1)
                    for t in range(NTILE):
                        pe.wait_ge(ya_ready, FROM + i * NTILE)
                        n = 0
                        for k in range(KD):
                            if t == 0:
                                pe.wait_ge(og_loaded[k], FROM + 32)
                            c = slice(k * SEQ + t * TILE, k * SEQ + (t + 1) * TILE)
                            for w, m in ((w_hi, og_hi), (w_hi, og_lo), (w_lo, og_hi)):
                                mm = nc.tensor.matmul(pz[t][:], w[b][:, k, :], m[:, c],
                                                      start=n == 0, stop=n == 3 * KD - 1)
                                n += 1
                        mm.then_inc(z_ready, 1)
                feature_tiles(pe, body)

        with nc.Block() as block:
            @block.sync
            def _(sp):
                with sp.Fori(0, SEQ // P // 2) as ii:
                    for b in range(2):
                        w = ii * 2 + b
                        sp.wait_ge(stored[b], FROM + ii * 16)
                        sp.dma_start(xw[b][:], x[bass.ds(w * P, P), :]).then_inc(x_loaded[b], 16)

            @block.scalar
            def _(act):
                with act.Fori(0, SEQ // P // 2) as ii:
                    for b in range(2):
                        w = ii * 2 + b
                        act.wait_ge(y_ready, FROM + w * 2 + 2)
                        act.dma_start(out[bass.ds(w * P, P), :], xw[b][:]).then_inc(stored[b], 16)
                for b in range(2):
                    act.wait_ge(stored[b], FROM + SEQ // P // 2 * 16)

            @block.vector
            def _(dve):
                with dve.Fori(0, SEQ // P // 2) as ii:
                    for b in range(2):
                        w = ii * 2 + b
                        dve.wait_ge(x_loaded[b], FROM + (ii + 1) * 16)
                        for j in range(2):
                            dve.wait_ge(o_ready, FROM + w * 2 + j + 1)
                            c = slice(j * TILE, (j + 1) * TILE)
                            nc.vector.scalar_tensor_tensor(out=xw[b][:, c], in0=pz[2 * b + j][:],
                                                           scalar=1.0 / WSCALE, in1=xw[b][:, c], op0=ALU.mult,
                                                           op1=ALU.add).then_inc(y_ready, 1)

            @block.tensor
            def _(pe):
                with pe.Fori(0, SEQ // P // 2) as ii:
                    for b in range(2):
                        w = ii * 2 + b
                        for j in range(2):
                            pe.wait_ge(y_ready, FROM + ii * 4)
                            n = 0
                            for k in range(KD):
                                c = bass.ds(w * P, P)
                                for m, wo in ((m_hi, wo_hi), (m_hi, wo_lo), (m_lo, wo_hi)):
                                    mm = nc.tensor.matmul(pz[2 * b + j][:], m[:, k, c],
                                                          wo[:, k, j * TILE:(j + 1) * TILE],
                                                          start=n == 0, stop=n == 3 * KD - 1)
                                    n += 1
                            mm.then_inc(o_ready, 1)


def hybrid_layer(nc, x, meta, norm_g, w_in, lb_logits, r_norm_g, q_norm_g, k_norm_g, w_r, w_a, w_out, out):
    w_cols = w_in[0].rearrange("(k p) n -> p k n", p=P)
    x, w_r, w_a, w_out, out = x[0], w_r[0], w_a[0], w_out[0], out[0]

    def scratch(name, shape, dt):
        return nc.dram_tensor(name, shape, dt).ap()

    or_parts = scratch("or_parts", [2, P, RH * SEQ], F16)
    merged_r = scratch("merged_r", [P, KD * SEQ], F32)
    gate_a = scratch("gate_a", [P, KD * SEQ], F32)
    aq_parts = scratch("aq_parts", [2, P, AH * SEQ], F16)
    iq_parts = scratch("iq_parts", [2, P, IH // 2 * SEQ], F16)
    ag = scratch("ag", [P, AH * SEQ], F32)
    oa_parts = scratch("oa_parts", [2, P, AH * SEQ], F16)

    with ExitStack() as ctx:
        def sb(name, shape, dt):
            return ctx.enter_context(nc.sbuf_tensor(name, shape, dt))

        ident = sb("ident", [P, P], F32)
        with ExitStack() as keys_live:
            with nc.sbuf_tensor("ut_hi", [P, KD, T], F16) as ut_hi, nc.sbuf_tensor("ut_lo", [P, KD, T], F16) as ut_lo:
                normed_input(nc, x, meta, norm_g, ut_hi, ut_lo, ident)
                recurrence(nc, w_cols, lb_logits, r_norm_g, ut_hi, ut_lo, or_parts, ident)
                merge_recurrent(nc, w_cols, w_r, ut_hi, ut_lo, or_parts, merged_r, gate_a)

                def keyed(name, shape, dt):
                    return keys_live.enter_context(nc.sbuf_tensor(name, shape, dt, side="right"))
                kt_hi, kt_lo = keyed("kt_hi", [P, KVH, T], F16), keyed("kt_lo", [P, KVH, T], F16)
                v_all = keyed("v_all", [P, NW, KVH * P], F32)
                ik_hi, ik_lo = keyed("ik_hi", [P, T], F16), keyed("ik_lo", [ID, T], F16)
                iw_all = keyed("iw_all", [P, NW, IH], F32)
                keys_values(nc, w_cols, k_norm_g, ut_hi, ut_lo, kt_hi, kt_lo, v_all, ik_hi, ik_lo, iw_all)
                queries(nc, w_cols, q_norm_g, ut_hi, ut_lo, aq_parts, iq_parts, ag)
            attention(nc, aq_parts, iq_parts, ag, kt_hi, kt_lo, v_all, ik_hi, ik_lo, iw_all, oa_parts, ident)
        merge_and_project(nc, x, w_a, w_out, oa_parts, merged_r, gate_a, out)


_INS = ["x", "meta", "norm_g", "w_in", "lb_logits", "r_norm_g", "q_norm_g", "k_norm_g", "w_r", "w_a", "w_out"]


def kernel(**inputs):
    import numpy as np
    from concourse import bacc
    from concourse.bass_utils import run_bass_kernel_spmd

    nc = bacc.Bacc("TRN2", target_bir_lowering=False, num_devices=1)
    arrays, args = {}, []
    for name in _INS:
        a = np.ascontiguousarray(inputs[name])
        arrays[f"in_{name}"] = a
        args.append(nc.dram_tensor(f"in_{name}", a.shape, mybir.dt.from_np(a.dtype), kind="ExternalInput").ap())
    out = nc.dram_tensor("out0", (1, SEQ, D), F32, kind="ExternalOutput").ap()
    hybrid_layer(nc, *args, out)
    return run_bass_kernel_spmd(nc, [arrays], core_ids=[0]).results[0]["out0"]
```
